# Optimizing a Trainium2 kernel written in Bass

```python
import math
import jax, jax.numpy as jnp
from jax import lax
import numpy as np

D_MODEL = 1024
BATCH = 1
SEQ = 512
DEPTH = 2

H_A = 8
HD_A = 64
DILATED_PAIRS = ((128, 1), (512, 4), (2048, 16))
H_B = 8
HD_B = 64
H_C = 8
Q_LORA = 256
KV_LORA = 128
NOPE_C = 64
ROPE_C = 32
V_C = 64
ROPE_THETA = 10000.0
N_BRANCHES = 3
BRANCH_WIDTH = 512
N_BUCKETS = 32
MAX_DISTANCE = 2048
Q_BLOCK = 128
N_GROUPS = 4
EXPERTS_PER_GROUP = 4
N_EXPERTS = 16
TOP_K = 2
D_FF_EXPERT = 256
EPS = 1e-6
IN_SPLIT_SIZES = (3 * H_A * HD_A, 3 * H_B * HD_B, H_B, Q_LORA, KV_LORA, ROPE_C, N_BRANCHES * D_MODEL)
D_IN = 3 * H_A * HD_A + 3 * H_B * HD_B + H_B + Q_LORA + KV_LORA + ROPE_C + N_BRANCHES * D_MODEL

kernel_name = 'hybrid_dilated_fox_mla_hiermoe'

def rms_norm(x, g):
    xf = x.astype(jnp.float32)
    y = xf * lax.rsqrt(jnp.mean(xf * xf, axis=-1, keepdims=True) + EPS)
    return (y * g.astype(jnp.float32)).astype(x.dtype)

def t5_bucket(dist):
    max_exact = N_BUCKETS // 2
    log_ratio = np.log(np.maximum(dist, max_exact) / max_exact) / np.log(MAX_DISTANCE / max_exact)
    large = np.minimum(max_exact + (log_ratio * (N_BUCKETS - max_exact)).astype(np.int32), N_BUCKETS - 1)
    return np.where(dist < max_exact, dist, large).astype(np.int32)

def rope_tables(positions, dim):
    half = dim // 2
    inv_freq = ROPE_THETA ** (-jnp.arange(half, dtype=jnp.float32) / half)
    ang = positions.astype(jnp.float32)[..., None] * inv_freq
    return jnp.cos(ang)[:, :, None, :], jnp.sin(ang)[:, :, None, :]

def apply_rope(x, cos, sin):
    half = x.shape[-1] // 2
    x1, x2 = x[..., :half], x[..., half:]
    c, s = cos.astype(x.dtype), sin.astype(x.dtype)
    return jnp.concatenate([x1 * c - x2 * s, x1 * s + x2 * c], axis=-1)

def dilated_branch(q, k, v, rel_bias, window_sub, dil):
    b, s_len, h, hd = q.shape
    n_sub = s_len // dil
    nb = -(-n_sub // Q_BLOCK)
    pad_end = nb * Q_BLOCK - n_sub

    def to_sub(t):
        return t.reshape(b, n_sub, dil, h, hd).transpose(0, 2, 3, 1, 4)

    qs = jnp.pad(to_sub(q), ((0, 0), (0, 0), (0, 0), (0, pad_end), (0, 0))).reshape(b, dil, h, nb, Q_BLOCK, hd)

    def kv_blocks(t):
        t = jnp.pad(to_sub(t), ((0, 0), (0, 0), (0, 0), (Q_BLOCK, pad_end), (0, 0)))
        t = t.reshape(b, dil, h, nb + 1, Q_BLOCK, hd)
        return jnp.concatenate([t[:, :, :, :-1], t[:, :, :, 1:]], axis=4)

    kb, vb = kv_blocks(k), kv_blocks(v)
    qi = np.arange(Q_BLOCK)[:, None]
    km = np.arange(2 * Q_BLOCK)[None, :]
    dist = qi + Q_BLOCK - km
    band = (dist >= 0) & (dist <= window_sub)
    valid = band[None] & ((np.arange(nb)[:, None, None] > 0) | (km[None] >= Q_BLOCK))
    bias = rel_bias[t5_bucket(np.maximum(dist, 0) * dil)].astype(jnp.float32).transpose(2, 0, 1)
    scores = jnp.einsum('bchnqd,bchnkd->bchnqk', qs, kb, preferred_element_type=jnp.float32) / math.sqrt(hd)
    scores = jnp.where(valid, scores + bias[:, None], -jnp.inf)
    m = jnp.max(scores, axis=-1, keepdims=True)
    p = jnp.exp(scores - m)
    den = jnp.sum(p, axis=-1, keepdims=True)
    o = jnp.einsum('bchnqk,bchnkd->bchnqd', p.astype(v.dtype), vb, preferred_element_type=jnp.float32) / den
    lse = (m + jnp.log(den))[..., 0]
    o = o.reshape(b, dil, h, nb * Q_BLOCK, hd)[:, :, :, :n_sub].transpose(0, 3, 1, 2, 4).reshape(b, s_len, h, hd)
    lse = lse.reshape(b, dil, h, nb * Q_BLOCK)[:, :, :, :n_sub].transpose(0, 3, 1, 2).reshape(b, s_len, h)
    return o, lse

def dilated_mixture(q, k, v, rel_bias):
    outs, lses = [], []
    for window, dil in DILATED_PAIRS:
        o, lse = dilated_branch(q, k, v, rel_bias, window // dil, dil)
        outs.append(o)
        lses.append(lse)
    w = jax.nn.softmax(jnp.stack(lses, axis=0), axis=0)
    o = jnp.sum(jnp.stack(outs, axis=0) * w[..., None], axis=0)
    return o.astype(q.dtype)

def causal_block_attention(q, k, v, scale, log_decay_cum=None):
    b, h, s_len, _ = q.shape
    dv = v.shape[-1]
    nb = s_len // Q_BLOCK
    kpos = jnp.arange(s_len)

    def one_block(j):
        start = j * Q_BLOCK
        qb = lax.dynamic_slice_in_dim(q, start, Q_BLOCK, axis=2)
        s = jnp.einsum('bhqd,bhkd->bhqk', qb, k, preferred_element_type=jnp.float32) * scale
        if log_decay_cum is not None:
            cq = lax.dynamic_slice_in_dim(log_decay_cum, start, Q_BLOCK, axis=2)
            s = s + cq[..., :, None] - log_decay_cum[..., None, :]
        qpos = start + jnp.arange(Q_BLOCK)
        s = jnp.where(kpos[None, :] <= qpos[:, None], s, -jnp.inf)
        p = jax.nn.softmax(s, axis=-1)
        return jnp.einsum('bhqk,bhkd->bhqd', p.astype(v.dtype), v)

    out = lax.map(one_block, jnp.arange(nb))
    return jnp.moveaxis(out, 0, 2).reshape(b, h, s_len, dv)

def hierarchical_moe(xn, w_rg, b_rg, w_re, b_re, w_g, w_u, w_d):
    b, s_len, d = xn.shape
    t = xn.reshape(-1, d)
    g_logits = jnp.einsum('td,dg->tg', t, w_rg, preferred_element_type=jnp.float32) + b_rg.astype(jnp.float32)
    p_group = jax.nn.softmax(g_logits, axis=-1)
    pg_top, g_idx = lax.top_k(p_group, 1)
    e_logits = (jnp.einsum('td,de->te', t, w_re, preferred_element_type=jnp.float32)
                + b_re.astype(jnp.float32)).reshape(-1, N_GROUPS, EXPERTS_PER_GROUP)
    e_sel = jnp.einsum('tge,tg->te', e_logits, jax.nn.one_hot(g_idx[:, 0], N_GROUPS, dtype=jnp.float32))
    ev, e_idx = lax.top_k(e_sel, TOP_K)
    w_e = jax.nn.softmax(ev, axis=-1) * pg_top
    gid = g_idx * EXPERTS_PER_GROUP + e_idx
    gates = jnp.sum(jax.nn.one_hot(gid, N_EXPERTS, dtype=jnp.float32) * w_e[..., None], axis=1).astype(t.dtype)
    y = jnp.zeros_like(t)
    for e in range(N_EXPERTS):
        hid = jax.nn.silu(t @ w_g[e]) * (t @ w_u[e])
        y = y + gates[:, e:e + 1] * (hid @ w_d[e])
    return y.reshape(b, s_len, d)

def setup_inputs(seed: int = 0) -> dict:
    key = jax.random.key(seed)
    ks = jax.random.split(key, 26)
    f32 = jnp.float32
    L = DEPTH

    def dense(k, shape, fan_in):
        return jax.random.normal(k, shape, f32) * fan_in ** -0.5

    def gain(k, shape):
        return 1.0 + 0.05 * jax.random.normal(k, shape, f32)

    x = jax.random.normal(ks[0], (BATCH, SEQ, D_MODEL), f32)
    offset = jax.random.randint(ks[1], (BATCH, 1), 0, 4096, dtype=jnp.int32)
    positions = offset + jnp.arange(SEQ, dtype=jnp.int32)[None, :]
    return {
        'x': x,
        'positions': positions,
        'rel_bias': 0.1 * jax.random.normal(ks[2], (N_BUCKETS, H_A), f32),
        'norm_mix': gain(ks[3], (L, D_MODEL)),
        'w_in': dense(ks[4], (L, D_MODEL, D_IN), D_MODEL),
        'b_forget': 1.0 + 2.0 * jax.random.uniform(ks[5], (L, H_B), f32),
        'gq_a': gain(ks[6], (L, HD_A)),
        'gk_a': gain(ks[7], (L, HD_A)),
        'gq_b': gain(ks[8], (L, HD_B)),
        'gk_b': gain(ks[9], (L, HD_B)),
        'gq_c': gain(ks[10], (L, NOPE_C + ROPE_C)),
        'gk_c': gain(ks[11], (L, NOPE_C + ROPE_C)),
        'norm_cq': gain(ks[12], (L, Q_LORA)),
        'norm_ckv': gain(ks[13], (L, KV_LORA)),
        'w_uq': dense(ks[14], (L, Q_LORA, H_C * (NOPE_C + ROPE_C)), Q_LORA),
        'w_ukv': dense(ks[15], (L, KV_LORA, H_C * (NOPE_C + V_C)), KV_LORA),
        'w_branch': dense(ks[16], (L, N_BRANCHES, BRANCH_WIDTH, D_MODEL), BRANCH_WIDTH),
        'w_out': dense(ks[17], (L, D_MODEL, D_MODEL), D_MODEL),
        'norm_ffn': gain(ks[18], (L, D_MODEL)),
        'w_router_group': dense(ks[19], (L, D_MODEL, N_GROUPS), D_MODEL),
        'b_router_group': 0.01 * jax.random.normal(ks[20], (L, N_GROUPS), f32),
        'w_router_expert': dense(ks[21], (L, D_MODEL, N_EXPERTS), D_MODEL),
        'b_router_expert': 0.01 * jax.random.normal(ks[22], (L, N_EXPERTS), f32),
        'w_expert_gate': dense(ks[23], (L, N_EXPERTS, D_MODEL, D_FF_EXPERT), D_MODEL),
        'w_expert_up': dense(ks[24], (L, N_EXPERTS, D_MODEL, D_FF_EXPERT), D_MODEL),
        'w_expert_down': dense(ks[25], (L, N_EXPERTS, D_FF_EXPERT, D_MODEL), D_FF_EXPERT),
    }

def reference(x, positions, rel_bias, norm_mix, w_in, b_forget, gq_a, gk_a, gq_b, gk_b, gq_c, gk_c,
              norm_cq, norm_ckv, w_uq, w_ukv, w_branch, w_out, norm_ffn, w_router_group, b_router_group,
              w_router_expert, b_router_expert, w_expert_gate, w_expert_up, w_expert_down):
    b, s_len, d = x.shape
    cos, sin = rope_tables(positions, ROPE_C)
    split_points = [int(i) for i in np.cumsum(IN_SPLIT_SIZES)[:-1]]
    for l in range(DEPTH):
        xn = rms_norm(x, norm_mix[l])
        h = xn @ w_in[l]
        ha, hb, hf, hcq, hckv, hkr, hg = jnp.split(h, split_points, axis=-1)

        qa, ka, va = [t.reshape(b, s_len, H_A, HD_A) for t in jnp.split(ha, 3, axis=-1)]
        o_a = dilated_mixture(rms_norm(qa, gq_a[l]), rms_norm(ka, gk_a[l]), va, rel_bias)
        o_a = o_a.reshape(b, s_len, BRANCH_WIDTH)

        qb, kb, vb = [t.reshape(b, s_len, H_B, HD_B).transpose(0, 2, 1, 3) for t in jnp.split(hb, 3, axis=-1)]
        log_f = jax.nn.log_sigmoid(hf.astype(jnp.float32) + b_forget[l].astype(jnp.float32))
        cum = jnp.cumsum(log_f, axis=1).transpose(0, 2, 1)
        o_b = causal_block_attention(rms_norm(qb, gq_b[l]), rms_norm(kb, gk_b[l]), vb, 1.0 / math.sqrt(HD_B), cum)
        o_b = o_b.transpose(0, 2, 1, 3).reshape(b, s_len, BRANCH_WIDTH)

        qc = (rms_norm(hcq, norm_cq[l]) @ w_uq[l]).reshape(b, s_len, H_C, NOPE_C + ROPE_C)
        kvc = (rms_norm(hckv, norm_ckv[l]) @ w_ukv[l]).reshape(b, s_len, H_C, NOPE_C + V_C)
        q_nope = rms_norm(qc[..., :NOPE_C], gq_c[l][:NOPE_C])
        q_rope = apply_rope(rms_norm(qc[..., NOPE_C:], gq_c[l][NOPE_C:]), cos, sin)
        k_nope = rms_norm(kvc[..., :NOPE_C], gk_c[l][:NOPE_C])
        vc = kvc[..., NOPE_C:]
        k_rope = apply_rope(rms_norm(hkr, gk_c[l][NOPE_C:])[:, :, None, :], cos, sin)
        q_full = jnp.concatenate([q_nope, q_rope], axis=-1).transpose(0, 2, 1, 3)
        k_full = jnp.concatenate([k_nope, jnp.broadcast_to(k_rope, (b, s_len, H_C, ROPE_C))], axis=-1).transpose(0, 2, 1, 3)
        o_c = causal_block_attention(q_full, k_full, vc.transpose(0, 2, 1, 3), 1.0 / math.sqrt(NOPE_C + ROPE_C))
        o_c = o_c.transpose(0, 2, 1, 3).reshape(b, s_len, BRANCH_WIDTH)

        branches = jnp.stack([o_a, o_b, o_c], axis=2)
        proj = jnp.einsum('bsgc,gcd->bsgd', branches, w_branch[l])
        gates = jax.nn.sigmoid(hg.reshape(b, s_len, N_BRANCHES, d))
        x = x + jnp.sum(gates * proj, axis=2) @ w_out[l]

        x = x + hierarchical_moe(rms_norm(x, norm_ffn[l]), w_router_group[l], b_router_group[l],
                                 w_router_expert[l], b_router_expert[l], w_expert_gate[l],
                                 w_expert_up[l], w_expert_down[l])
    return x


_drawn_inputs = setup_inputs


def setup_inputs(seed=0):
    import zlib

    import numpy as np

    out = dict(_drawn_inputs(seed))
    spreads = {}
    factors = {'gq_a': 3.174, 'gk_c': 4.558, 'b_router_group': 2.984, 'b_router_expert': 3.836}
    for name, (base, spread) in spreads.items():
        noise = np.random.default_rng([zlib.crc32(name.encode()), seed]).standard_normal(out[name].shape)
        drawn = base * np.exp(spread * noise) if base else spread * noise
        out[name] = __import__('jax').numpy.asarray(drawn.astype(out[name].dtype))
    for name, factor in factors.items():
        out[name] = (out[name] * factor).astype(out[name].dtype)
    return out
```

```python
from contextlib import ExitStack
import math

import numpy as np
import concourse.bass as bass
from concourse import mybir

F32 = mybir.dt.float32
F32R = mybir.dt.float32r
BF16 = mybir.dt.bfloat16
I32 = mybir.dt.int32
ALU = mybir.AluOpType
ACT = mybir.ActivationFunctionType
AX_X = mybir.AxisListType.X

P = 128
D = 1024
SEQ = 512
DEPTH = 2
KD = D // P
NT = SEQ // P
H = 8
HD = 64
BW = H * HD
NOPE, ROPE = 64, 32
QH = NOPE + ROPE
HALF = ROPE // 2
Q_LORA, KV_LORA = 256, 128
N_BUCKETS, MAX_DISTANCE = 32, 2048
DILATED_PAIRS = ((128, 1), (512, 4), (2048, 16))
NG, EG, NE, FF = 4, 4, 16, 256
EPS = 1e-6
MASKED = -1.0e30
COL_SMALL = 6 * BW
N_SMALL = H + Q_LORA + KV_LORA + ROPE
COL_GATE = COL_SMALL + N_SMALL
LEAD = 2
RAW, HL = 4, 3
BIAS_LEN = SEQ + P


def shape_constants():
    i = np.arange(BIAS_LEN)
    dist = SEQ - 1 - i
    d0 = np.maximum(dist, 0)
    exact = N_BUCKETS // 2
    ratio = np.log(np.maximum(d0, exact) / exact) / np.log(MAX_DISTANCE / exact)
    large = np.minimum(exact + (ratio * (N_BUCKETS - exact)).astype(np.int32), N_BUCKETS - 1)
    bucket = np.where(d0 < exact, d0, large)
    count = sum(((dist % dil == 0) & (dist <= window)).astype(int) for window, dil in DILATED_PAIRS)
    count = np.where(dist >= 0, count, 0)
    scale = math.sqrt(HD)
    hot = np.zeros((N_BUCKETS + 1, BIAS_LEN), np.float32)
    hot[bucket, i] = np.where(count > 0, scale, 0.0)
    hot[N_BUCKETS] = np.where(count > 0, scale * np.log(np.maximum(count, 1)), MASKED)
    p, j = np.arange(P)[:, None], np.arange(SEQ)[None, :]
    tri = (j >= p).astype(np.float32)
    mask = np.where(j <= p + SEQ - P, 0.0, MASKED).astype(np.float32)
    sel = np.zeros((3 * 32, H, P), np.float32)
    for h in range(H):
        sel[[h, 32 + h, 64 + h], h] = -scale
    freq = np.broadcast_to(np.float32(10000.0) ** (-np.arange(HALF, dtype=np.float32) / HALF), (P, HALF))
    first = np.broadcast_to(np.arange(4, 0, -1, dtype=np.float32), (P, 4))
    return {"ident": np.eye(P, dtype=np.float32), "hot": hot, "tri": tri, "mask": mask,
            "sel": sel.reshape(96, H * P), "freq": np.ascontiguousarray(freq, np.float32),
            "first": np.ascontiguousarray(first)}


GROUPS = [("qk", 0, KD, BW), ("qk", 1, KD, BW), ("v", 0, KD, BW), ("small", 0, KD, N_SMALL),
          ("qk", 2, KD, BW), ("qk", 3, KD, BW), ("v", 1, KD, BW),
          ("uq", 0, 2, 4 * QH), ("uq", 1, 2, 4 * QH), ("gate", 0, KD, 512), ("ukv", 0, 1, 512),
          ("ukv", 1, 1, 512), ("branch", 0, 4, 512), ("gate", 1, KD, 512), ("branch", 1, 4, 512)]
for _b in (1, 2):
    for _c in (0, 1):
        GROUPS += [("gate", 2 * _b + _c, KD, 512), ("branch", 2 * _b + _c, 4, 512)]
GROUPS += [("out", 0, KD, 512), ("out", 1, KD, 512)]
PIECES = [(g, k) for g, grp in enumerate(GROUPS) for k in range(grp[2])]
NP_ = len(PIECES)
START = {g: min(s for s, pc in enumerate(PIECES) if pc[0] == g) for g in range(len(GROUPS))}
END = {g: START[g] + GROUPS[g][2] - 1 for g in START}
GID = {(n, i): g for g, (n, i, _, _) in enumerate(GROUPS)}
OUT0 = START[GID["out", 0]]
UNITS = [(b, qt, h) for b in range(3) for qt in range(NT) for h in range(H)]
UNIT_SLOT = {}
_s = END[GID["v", 0]] + 1
for _i, (_b, _qt, _h) in enumerate(UNITS):
    UNIT_SLOT.setdefault(_s, []).append(_i)
    if not (_b > 0 and _qt == 0 and _h % 2 == 0):
        _s += 1
LAST_UNIT_SLOT = _s - 1
POSTS = [("qk", 0), ("qk", 1), ("qk", 2), ("qk", 3), ("uq", 0), ("uq", 1), ("ukv", 0), ("ukv", 1)]
POST_AT = {GID[p]: j for j, p in enumerate(POSTS)}
POST_PE = {}
for _j, _p in enumerate(POSTS):
    _e = END[GID[_p]] + 6 + (2 if _p == ("uq", 1) and False else 0) + (1 if _p == ("ukv", 1) else 0)
    POST_PE.setdefault(_e, []).append((_j, (0, 1)))
    POST_PE.setdefault(_e + 1, []).append((_j, (2, 3)))
SMALL_END = END[GID["small", 0]]
C_TR = {SMALL_END + 9: [("cum",)], SMALL_END + 10: [("C", 0)], SMALL_END + 11: [("C", 1)],
        SMALL_END + 12: [("C", 2)]}
O_TR = {}
for _s0, _us in UNIT_SLOT.items():
    for _i in _us:
        if UNITS[_i][2] == H - 1:
            O_TR.setdefault(_s0 + 3, []).append((UNITS[_i][0], UNITS[_i][1]))


def steps_of(slot):
    us = UNIT_SLOT.get(slot, [])
    if len(us) == 2:
        return [(us[0], us[0] - 1, (0, 1)), (us[1], us[1] - 1, (2, 3))]
    if len(us) == 1:
        return [(us[0], us[0] - 1 if us[0] else None, (0, 1, 2, 3))]
    if slot == LAST_UNIT_SLOT + 1:
        return [(None, len(UNITS) - 1, (0, 1, 2, 3))]
    return [(None, None, (0, 1, 2, 3))]


def turn_order():
    order = {}
    for s in range(OUT0):
        for new, old, _ in steps_of(s):
            if old is not None:
                order[("P", old)] = len(order)
        for key in turns_of(s):
            order[key] = len(order)
    return order


def turns_of(s):
    keys = [("O", b, qt) for b, qt in O_TR.get(s, [])]
    keys += C_TR.get(s, [])
    for j, toks in POST_PE.get(s, []):
        keys += [("Q", j, t) for t in toks]
    return keys


TURN = turn_order()
SOFT = {0: 1.0 / math.sqrt(HD), 1: 1.0 / math.sqrt(HD), 2: 1.0 / math.sqrt(QH)}


def build(nc, t):
    ctx = ExitStack()
    with ctx:
        def sb(name, shape, dt=F32):
            return ctx.enter_context(nc.sbuf_tensor(name, shape, dt))

        def sem(name):
            return ctx.enter_context(nc.semaphore(name))

        bank = [ctx.enter_context(nc.psum_tensor(f"bank{i}", [P, 512], F32)) for i in range(8)]
        acc, sc_bank, turn, o_bank = bank[0:4], bank[4:6], bank[6], bank[7]

        with nc.sbuf_tensor("x_rows", [P, NT, D], F32) as x_rows:
            pass
        oT1 = sb("oT1", [P, 2, 4, SEQ], F32R)
        oT0 = sb("oT0", [P, 2, 4, SEQ], F32R)
        rows = sb("rows", [P, NT, D])
        xT = sb("xT", [P, 2, KD, SEQ], F32R)
        raw = sb("raw", [P, RAW, 512])
        wh = sb("wh", [P, HL, 512], F32R)
        wl = sb("wl", [P, HL, 512], F32R)
        q_c = sb("q_c", [P, H, SEQ])
        bias_a = q_c
        ac = sb("ac", [P, 6144])
        qT_a = ac[:, 0:2048].rearrange("p (c s) -> p c s", c=4)
        kT_a = ac[:, 2048:4096].rearrange("p (c s) -> p c s", c=4)
        v_a = ac[:, 4096:6144].rearrange("p (n c) -> p n c", n=NT)
        kT_c = ac[:, 0:4096].rearrange("p (h s) -> p h s", h=H)
        v_c = v_a
        bqkv = sb("bqkv", [P, 6144])
        qT_b = bqkv[:, 0:2048].rearrange("p (c s) -> p c s", c=4)
        kT_b = bqkv[:, 2048:4096].rearrange("p (c s) -> p c s", c=4)
        v_b = bqkv[:, 4096:6144].rearrange("p (n c) -> p n c", n=NT)
        head_odd = sb("head_odd", [P, NT, 512])
        head_rows = [rows[:, :, 512:D], head_odd]
        small = rows[:, :, 0:N_SMALL]
        squares = sb("squares", [P, 2, 512])
        gate_t = sb("gate_t", [P, NT, 512])
        prob = sb("prob", [P, 2, 512])
        probT = sb("probT", [P, 512])
        o_rows = sb("o_rows", [P, 512])
        cT_kv = sb("cT_kv", [P, 2, 1, SEQ], F32R)
        cT = [oT1[:, :, 0, :], oT1[:, :, 1, :], cT_kv[:, :, 0, :]]
        ident = sb("ident", [P, P])
        tri = gate_t[:, 0, :]
        mask = sb("mask", [P, SEQ])
        sel = sb("sel", [96, H, P], BF16)
        cum = squares[0:96, 0, :]
        cum_b = squares[0:96, 1, 0:SEQ // 2].bitcast(BF16)
        cum_p = sb("cum_p", [96, SEQ], BF16)
        lf96 = gate_t[:, 1, 0:NT * 96].rearrange("p (n c) -> p n c", n=NT)
        cosT = sb("cosT", [P, NT, HALF])
        sinT = sb("sinT", [P, NT, HALF])
        freq = sb("freq", [P, HALF])
        first = sb("first", [P, 4])
        pos_i = sb("pos_i", [P, NT], I32)
        pos_f = sb("pos_f", [P, NT])
        ssx = sb("ssx", [P, NT])
        rsx = sb("rsx", [P, NT])
        pw = sb("pw", [P, 32])
        ssq = sb("ssq", [P, NT, 8])
        rsq = sb("rsq", [P, NT, 8])
        ssc = sb("ssc", [P, 3, NT])
        rsc = sb("rsc", [P, 3, NT])
        nmax = sb("nmax", [P, 2])
        den = sb("den", [P, 2, H])
        rden = sb("rden", [P, H])
        rope_t = sb("rope_t", [P, 4, 4 * HALF])
        kr = sb("kr", [P, NT, ROPE])
        fz = sb("fz", [P, 4, NT * H])
        gcol = sb("gcol", [P, 2 * KD])
        ghead = sb("ghead", [P, 6])
        gc = sb("gc", [P, 3])
        grope = sb("grope", [P, 2, ROPE])
        bfg = sb("bfg", [P, H])
        bro = sb("bro", [P, NG + NE])
        wr = sb("wr", [P, KD, NG + NE])
        wrh = sb("wrh", [P, KD, NG + NE], F32R)
        wrl = sb("wrl", [P, KD, NG + NE], F32R)
        relb = sb("relb", [N_BUCKETS + 1, H])
        r4 = prob[:, 0, 0:128].rearrange("p (q n c) -> p q n c", q=8, n=NT)
        r1 = prob[:, 0, 128:176].rearrange("p (q n) -> p q n", q=12)
        lg = prob[:, 0, 192:192 + NT * (NG + NE)].rearrange("p (n c) -> p n c", n=NT)
        gates = prob[:, 1, 0:NT * NE].rearrange("p (n e) -> p n e", n=NT)
        hot = head_odd[0:N_BUCKETS + 1, :, :].rearrange("p b c -> p (b c)")[:, 0:BIAS_LEN]
        biasT = squares[0:H, :, :].rearrange("p a b -> p (a b)")[:, 0:BIAS_LEN]
        bias_dram = nc.dram_tensor("bias_dram", [H, P, BIAS_LEN], F32, kind="Internal")

        NAMES = ["x_in", "gains_in", "bias_in", "x_again", "hi_ready", "lo_ready", "piece_used", "acc_done",
                 "acc_read", "gate_read", "sum_ready", "scale_ready", "rows_ready", "wide_done", "wide_hi", "wide_lo",
                 "turn_done", "turn_hi", "turn_read", "scores_done", "shifted", "probs_ready", "pv_done",
                 "o_ready", "v_copied", "rows_copied", "sq_ready", "sq_summed", "post_done", "post_aux",
                 "gate_ready", "branch_ready", "merged", "cum_split", "small_copied", "fz_dve", "fz_act",
                 "csq_ready", "csum_ready", "c_ready", "kr_ready", "pool_own", "dve_own",
                 "router_done", "logits", "r_dve", "r_act", "gates_ready",
                 "h_ready", "hid_act", "hid_ready", "hidT_ready", "y_done", "y_added", "wr_split", "r_pair",
                 "x_out", "turn2_done", "x_done"]
        RAW_SEMS = [sem(f"raw_in{i}") for i in range(RAW)]
        S = {n: sem(n) for n in NAMES}
        (x_in, gains_in, bias_in, x_again, hi_ready, lo_ready, piece_used, acc_done, acc_read, gate_read, sum_ready,
         scale_ready, rows_ready, wide_done, wide_hi, wide_lo, turn_done, turn_hi, turn_read, scores_done,
         shifted, probs_ready, pv_done, o_ready, v_copied, rows_copied, sq_ready, sq_summed, post_done,
         post_aux, gate_ready, branch_ready, merged, cum_split, small_copied, fz_dve, fz_act, csq_ready,
         csum_ready, c_ready, kr_ready, pool_own, dve_own, router_done, logits, r_dve, r_act, gates_ready,
         h_ready, hid_act, hid_ready, hidT_ready, y_done, y_added, wr_split, r_pair, x_out, turn2_done,
         x_done) = (S[n] for n in NAMES)
        arrived, released, resumed = sem("arrived"), sem("released"), sem("resumed")
        const_in, bias_mm, bias_sb, bias_out, rope_ready, set_ready, rope_steps = (
            sem(n) for n in ("const_in", "bias_mm", "bias_sb", "bias_out", "rope_ready", "set_ready", "rope_steps"))
        cleared = range(RAW_SEMS[0].num, x_done.num + 1)
        assert len(cleared) == RAW + len(NAMES)
        N_CONST = 8
        sel_in = sem("sel_in")
        dve_c, pool_c = sem("dve_c"), sem("pool_c")
        LO_TURN = {}
        for key in sorted(TURN, key=TURN.get):
            if key[0] in ("C", "O"):
                LO_TURN[key] = len(LO_TURN)

        block = ctx.enter_context(nc.Block())

        def raw_landed(eng, i):
            eng.wait_ge(RAW_SEMS[i % RAW], 16 * (i // RAW + 1))

        def layer_end(eng, layer):
            eng.sem_inc(arrived, 1)
            eng.wait_ge(released, layer + 1)
            eng.sem_inc(resumed, 1)

        def at(ap, layer):
            v = ap[bass.ds(layer, 1)]
            names = "abcd"[:len(ap.shape) - 1]
            return v.rearrange(f"o {' '.join(names)} -> (o {names[0]}) {' '.join(names[1:])}")

        E0 = NP_
        PPE = KD + 4

        N_GAINS = 2 + 8 + 4 + 2 + 3 + 2 + 1

        def skew(dram, h):
            ap = dram[h:h + 1, 0, P - 1:P - 1 + SEQ]
            return bass.AP(tensor=ap.tensor, offset=ap.offset, ap=[[BIAS_LEN - 1, P], [1, SEQ]])

        def expert_loads(sp, layer, wg, wu, wd):
            for e in range(NE):
                for j in range(PPE):
                    i = E0 + e * PPE + j
                    sp.wait_ge(lo_ready, i - RAW + 1)
                    s = RAW_SEMS[i % RAW]
                    idx = bass.ds(layer * NE + e, 1)
                    if j < KD:
                        sp.dma_start(raw[:, i % RAW, 0:FF], at(wg, layer * NE + e)[j * P:(j + 1) * P, :]).then_inc(s, 16)
                        sp.dma_start(raw[:, i % RAW, FF:], at(wu, layer * NE + e)[j * P:(j + 1) * P, :]).then_inc(s, 16)
                    else:
                        c, k = (j - KD) // 2, (j - KD) % 2
                        src = at(wd, layer * NE + e)[k * P:(k + 1) * P, c * 512:(c + 1) * 512]
                        sp.dma_start(raw[:, i % RAW, 0:256], src[:, 0:256]).then_inc(s, 16)
                        sp.dma_start(raw[:, i % RAW, 256:], src[:, 256:]).then_inc(s, 16)

        def expert_landed(eng, i):
            own = (NP_ - 1 - i % RAW) // RAW + 1
            later = (i // RAW + 1) - own
            eng.wait_ge(RAW_SEMS[i % RAW], 16 * (own + 2 * later))

        def sums_read(eng, g, n):
            gate = GROUPS[g][0] == "gate"
            before = sum((GROUPS[q][0] == "gate") == gate for q in range(g))
            eng.wait_ge(gate_read if gate else acc_read, 4 * before + n + 1)

        def multiplied(eng, i):
            if i >= E0:
                e, j = divmod(i - E0, PPE)
                if j == KD - 1:
                    return eng.wait_ge(h_ready, 4 * (e + 1))
                if j > KD and (j - KD) % 2:
                    return eng.wait_ge(y_done, 8 * e + 4 * ((j - KD) // 2 + 1))
                inner = NP_ - len(GROUPS) + (PPE - 3) * e + sum(q not in (KD - 1, KD + 1, KD + 3) for q in range(j + 1))
                return eng.wait_ge(piece_used, inner)
            g = PIECES[i][0]
            if i == END[g]:
                return eng.wait_ge(acc_done, 4 * (g + 1))
            return eng.wait_ge(piece_used, sum(q != END[PIECES[q][0]] for q in range(i + 1)))

        def split_hi(i, width):
            (raw_landed if i < E0 else expert_landed)(nc.scalar, i)
            if i >= HL:
                multiplied(nc.scalar, i - HL)
            nc.scalar.activation(wh[:, i % HL, 0:width], raw[:, i % RAW, 0:width], ACT.Copy).then_inc(hi_ready, 1)

        def split_lo(i, width):
            nc.vector.wait_ge(hi_ready, i + 1)
            (raw_landed if i < E0 else expert_landed)(nc.vector, i)
            nc.vector.tensor_tensor(wl[:, i % HL, 0:width], raw[:, i % RAW, 0:width],
                                    wh[:, i % HL, 0:width].bitcast(F32), ALU.subtract).then_inc(lo_ready, 1)

        def width_of(i):
            return GROUPS[PIECES[i][0]][3] if i < E0 else 512

        def passes(out, lhs, rhs, start, stop):
            nc.tensor.matmul(out, lhs[0], rhs[0], start=start, stop=False)
            nc.tensor.matmul(out, lhs[0], rhs[1], start=False, stop=False)
            return nc.tensor.matmul(out, lhs[1], rhs[0], start=False, stop=stop)

        def experts_pe(pe):
            for e in range(NE):
                for j in range(PPE):
                    i = E0 + e * PPE + j
                    pe.wait_ge(lo_ready, i + 1)
                    for n in range(NT):
                        ts = slice(n * P, (n + 1) * P)
                        if j < KD:
                            if j == 0 and e:
                                pe.wait_ge(y_added, 8 * e)
                            mm = passes(acc[n][:], (xT[:, 0, j, ts], xT[:, 1, j, ts]),
                                        (wh[:, i % HL, :], wl[:, i % HL, :]), j == 0, j == KD - 1)
                            if j == KD - 1:
                                mm.then_inc(h_ready, 1)
                        else:
                            c, k = (j - KD) // 2, (j - KD) % 2
                            if j == KD:
                                pe.wait_ge(hid_ready, 4 * e + n + 1)
                                if 4 * e + n:
                                    pe.wait_ge(hidT_ready, 4 * e + n)
                                for f in range(2):
                                    tr = pe.transpose(turn[:, f * P:(f + 1) * P],
                                                      gate_t[:, n, f * P:(f + 1) * P], ident[:])
                                tr.then_inc(turn2_done, 1)
                    if j >= KD:
                        c, k = (j - KD) // 2, (j - KD) % 2
                        pe.wait_ge(hidT_ready, 4 * e + 4)
                        for n in range(NT):
                            ts = slice(n * P, (n + 1) * P)
                            if k == 0 and c == 1:
                                pe.wait_ge(y_added, 8 * e + n + 1)
                            mm = passes(acc[n][:], (oT0[:, 0, k, ts], oT0[:, 1, k, ts]),
                                        (wh[:, i % HL, :], wl[:, i % HL, :]), k == 0, k == 1)
                            if k == 1:
                                mm.then_inc(y_done, 1)
                    if j not in (KD - 1, KD + 1, KD + 3):
                        mm.then_inc(piece_used, 1)

        def experts_act(act):
            for i in range(E0, E0 + 2):
                split_hi(i, 512)
            for e in range(NE):
                for j in range(PPE):
                    i = E0 + e * PPE + j
                    if j == KD:
                        for n in range(NT):
                            act.wait_ge(turn2_done, 4 * e + n + 1)
                            act.activation(oT0[:, 0, 0:2, n * P:(n + 1) * P],
                                           turn[:, 0:2 * P].rearrange("p (c s) -> p c s", c=2), ACT.Copy)\
                                .then_inc(hid_act, 1)
                    if i + 2 < E0 + NE * PPE:
                        split_hi(i + 2, 512)
                    if j == KD - 1:
                        for n in range(NT):
                            act.wait_ge(h_ready, 4 * e + n + 1)
                            act.activation(gate_t[:, n, FF:], acc[n][:, 0:FF], ACT.Tanh, scale=0.5)\
                                .then_inc(gate_ready, 1)

        def route(dve):
            count = [0]

            def step(ins):
                ins.then_inc(r_dve, 1)
                count[0] += 1
                dve.wait_ge(r_dve, count[0])

            def b4(a):
                return a.unsqueeze(2).broadcast_to([P, NT, 4])

            fst = first[:].unsqueeze(1).broadcast_to([P, NT, 4])
            tt, tr, ts = nc.vector.tensor_tensor, nc.vector.tensor_reduce, nc.vector.tensor_scalar
            dve.wait_ge(router_done, 1)
            step(tt(lg, sc_bank[0][:, 0:NT * 32].rearrange("p (n c) -> p n c", n=NT)[:, :, 0:NG + NE],
                    bro[:].unsqueeze(1).broadcast_to([P, NT, NG + NE]), ALU.add))
            gl = lg[:, :, 0:NG]
            step(tr(r1[:, 0, :], gl, AX_X, ALU.max))
            step(tt(r4[:, 0], gl, b4(r1[:, 0, :]), ALU.subtract))

            def first_best(dst, values, best, tmp, tmp1):
                step(tt(tmp, values, b4(best), ALU.is_ge))
                step(tt(tmp, tmp, fst, ALU.mult))
                step(tr(tmp1, tmp, AX_X, ALU.max))
                step(tt(dst, tmp, b4(tmp1), ALU.is_equal))

            g1, e1, e2, esel = r4[:, 2], r4[:, 3], r4[:, 4], r4[:, 5]
            first_best(g1, gl, r1[:, 0, :], r4[:, 6], r1[:, 1, :])
            el = lg[:, :, NG:].rearrange("p n (g e) -> p n g e", g=NG)
            gsel = gates.rearrange("p n (g e) -> p n g e", g=NG)
            for n in range(NT):
                ins = tt(gsel[:, n], el[:, n], g1[:, n].unsqueeze(2).broadcast_to([P, NG, EG]), ALU.mult)
            step(ins)
            for n in range(NT):
                ins = tr(esel[:, n], gsel[:, n].rearrange("p g e -> p e g"), AX_X, ALU.add)
            step(ins)
            step(tr(r1[:, 2, :], esel, AX_X, ALU.max))
            first_best(e1, esel, r1[:, 2, :], r4[:, 6], r1[:, 1, :])
            step(nc.vector.scalar_tensor_tensor(out=r4[:, 7], in0=e1, scalar=MASKED, in1=esel, op0=ALU.mult,
                                                op1=ALU.add))
            step(tr(r1[:, 3, :], r4[:, 7], AX_X, ALU.max))
            first_best(e2, r4[:, 7], r1[:, 3, :], r4[:, 6], r1[:, 1, :])
            step(tt(r1[:, 4, :], r1[:, 3, :], r1[:, 2, :], ALU.subtract))
            dve.sem_inc(r_pair, 1)
            dve.wait_ge(r_act, 1)
            step(tr(r1[:, 6, :], r4[:, 1], AX_X, ALU.add))
            dve.wait_ge(r_act, 2)
            step(ts(r1[:, 7, :], r1[:, 5, :], 1.0, None, ALU.add))
            step(tt(r1[:, 8, :], r1[:, 7, :], r1[:, 6, :], ALU.mult))
            step(nc.vector.reciprocal(r1[:, 9, :], r1[:, 8, :]))
            step(ts(r1[:, 9, :], r1[:, 9, :], 0.5, None, ALU.mult))
            step(tt(r1[:, 10, :], r1[:, 9, :], r1[:, 5, :], ALU.mult))
            step(tt(e1, e1, b4(r1[:, 9, :]), ALU.mult))
            step(tt(e2, e2, b4(r1[:, 10, :]), ALU.mult))
            step(tt(e1, e1, e2, ALU.add))
            for n in range(NT):
                ins = tt(gsel[:, n], e1[:, n].unsqueeze(1).broadcast_to([P, NG, EG]),
                         g1[:, n].unsqueeze(2).broadcast_to([P, NG, EG]), ALU.mult)
            step(ins)


        def experts_dve(dve):
            for i in range(E0, E0 + 2):
                split_lo(i, 512)
            for e in range(NE):
                for j in range(PPE):
                    i = E0 + e * PPE + j
                    if j == KD:
                        for n in range(NT):
                            dve.wait_ge(hid_act, 4 * e + n + 1)
                            nc.vector.tensor_tensor(oT0[:, 1, 0:2, n * P:(n + 1) * P],
                                                    turn[:, 0:2 * P].rearrange("p (c s) -> p c s", c=2),
                                                    oT0[:, 0, 0:2, n * P:(n + 1) * P].bitcast(F32), ALU.subtract)\
                                .then_inc(hidT_ready, 1)
                    if i + 2 < E0 + NE * PPE:
                        split_lo(i + 2, 512)
                    if j == KD - 1:
                        for n in range(NT):
                            dve.wait_ge(gate_ready, 4 * e + n + 1)
                            nc.vector.scalar_tensor_tensor(out=gate_t[:, n, FF:], in0=gate_t[:, n, FF:], scalar=1.0,
                                                           in1=acc[n][:, 0:FF], op0=ALU.add, op1=ALU.mult)\
                                .then_inc(merged, 1)
                            dve.wait_ge(merged, 16 + 4 * e + n + 1)
                            nc.vector.scalar_tensor_tensor(out=gate_t[:, n, 0:FF], in0=gate_t[:, n, FF:],
                                                           scalar=gates[:, n, e:e + 1], in1=acc[n][:, FF:],
                                                           op0=ALU.mult, op1=ALU.mult).then_inc(hid_ready, 1)
                    if j in (KD + 1, KD + 3):
                        c = (j - KD) // 2
                        cs = slice(512 * c, 512 * (c + 1))
                        for n in range(NT):
                            dve.wait_ge(y_done, 8 * e + 4 * c + n + 1)
                            ins = nc.vector.tensor_tensor(x_rows[:, n, cs], x_rows[:, n, cs], acc[n][:], ALU.add)
                            ins.then_inc(y_added, 1)
            dve.wait_ge(y_added, 8 * NE)
            for n in range(NT):
                dve.sem_inc(x_done, 1)

        @block.sync
        def _(sp):
            sp.dma_start(t["out"], t["x"]).then_inc(const_in, 16)
            sp.dma_start(ident[:], t["ident"]).then_inc(const_in, 16)
            sp.dma_start(hot, t["hot"]).then_inc(const_in, 16)
            sp.dma_start(mask[:], t["mask"]).then_inc(const_in, 16)
            sp.dma_start(freq[:], t["freq"]).then_inc(const_in, 16)
            sp.dma_start(first[:], t["first"]).then_inc(const_in, 16)
            with nc.allow_non_contiguous_dma(reason="512 positions, once"):
                sp.dma_start(pos_i[:], t["positions"].rearrange("b (n p) -> p (b n)", p=P)).then_inc(const_in, 16)
            sp.wait_ge(set_ready, 2)
            sp.dma_start(relb[0:N_BUCKETS, :], t["rel_bias"]).then_inc(const_in, 16)
            sp.wait_ge(bias_sb, 2)
            sp.dma_start(bias_dram[:], biasT.unsqueeze(1).broadcast_to([H, P, BIAS_LEN]))\
                .then_inc(bias_out, 16)
            sp.wait_ge(const_in, 16 * N_CONST)
            sp.wait_ge(bias_out, 16)
            with sp.Fori(0, DEPTH) as layer:
                w_in = at(t["w_in"], layer)
                sp.dma_start(tri, t["tri"]).then_inc(gains_in, 16)
                for n in range(NT):
                    sp.dma_start(x_rows[:, n, :], t["out"].rearrange("b (n p) d -> (b n) p d", p=P)[n])\
                        .then_inc(x_in, 16)

                def load_piece(i):
                    if i >= RAW:
                        sp.wait_ge(lo_ready, i - RAW + 1)
                    g, k = PIECES[i]
                    name, idx, _, width = GROUPS[g]
                    dst = raw[:, i % RAW, 0:width]
                    if name in ("qk", "v", "small", "gate"):
                        col = {"qk": [0, BW, 3 * BW, 4 * BW], "v": [2 * BW, 5 * BW], "small": [COL_SMALL],
                               "gate": [COL_GATE + 512 * c for c in range(6)]}[name][idx]
                        src = w_in[k * P:(k + 1) * P, col:col + width]
                    elif name == "uq":
                        src = at(t["w_uq"], layer)[k * P:(k + 1) * P, idx * width:(idx + 1) * width]
                    elif name == "ukv":
                        src = at(t["w_ukv"], layer)[:, idx * 512:(idx + 1) * 512]
                    elif name == "branch":
                        b, c = idx // 2, idx % 2
                        src = at(t["w_branch"].rearrange("l g c d -> l (g c) d"), layer)[
                            b * BW + k * P:b * BW + (k + 1) * P, c * 512:(c + 1) * 512]
                    else:
                        src = at(t["w_out"], layer)[k * P:(k + 1) * P, idx * 512:(idx + 1) * 512]
                    sp.dma_start(dst, src).then_inc(RAW_SEMS[i % RAW], 16)

                for i in range(RAW):
                    load_piece(i)
                with nc.allow_non_contiguous_dma(reason="gains as columns"):
                    n_g = 0

                    def gain(dst, src):
                        sp.dma_start(dst, src).then_inc(gains_in, 16)

                    gain(gcol[:, 0:KD], at(t["norm_mix"].rearrange("l (k p) -> l p k", p=P), layer))
                    gain(gcol[:, KD:2 * KD], at(t["norm_ffn"].rearrange("l (k p) -> l p k", p=P), layer))
                    for c, name in enumerate(("gq_a", "gk_a", "gq_b", "gk_b")):
                        for half in range(2):
                            gain(ghead[half * HD:(half + 1) * HD, c:c + 1],
                                 at(t[name].rearrange("l (p o) -> l p o", o=1), layer))
                    for c, name in enumerate(("gq_c", "gk_c")):
                        full = t[name].rearrange("l (p o) -> l p o", o=1)
                        gain(ghead[0:NOPE, 4 + c:5 + c], at(full, layer)[0:NOPE])
                        gain(grope[:, c, :], t[name][bass.ds(layer, 1), NOPE:QH].broadcast_to([P, ROPE]))
                    gain(gc[:, 0:2], at(t["norm_cq"].rearrange("l (k p) -> l p k", p=P), layer))
                    gain(gc[:, 2:3], at(t["norm_ckv"].rearrange("l (k p) -> l p k", p=P), layer))
                    gain(bfg[:], t["b_forget"][bass.ds(layer, 1), :].broadcast_to([P, H]))
                    gain(bro[:, 0:NG], t["b_router_group"][bass.ds(layer, 1), :].broadcast_to([P, NG]))
                    gain(bro[:, NG:], t["b_router_expert"][bass.ds(layer, 1), :].broadcast_to([P, NE]))
                    gain(wr[:, :, 0:NG], at(t["w_router_group"].rearrange("l (k p) g -> l p k g", p=P), layer))
                    gain(wr[:, :, NG:], at(t["w_router_expert"].rearrange("l (k p) g -> l p k g", p=P), layer))
                for h in range(H):
                    sp.dma_start(bias_a[:, h, :], skew(bias_dram, h)).then_inc(bias_in, 16)
                for i in range(RAW, NP_):
                    if i == END[GID["branch", 3]] + RAW:
                        multiplied(sp, END[GID["branch", 3]])
                        for n in range(NT):
                            sp.dma_start(x_rows[:, n, :],
                                         t["out"].rearrange("b (n p) d -> (b n) p d", p=P)[n]).then_inc(x_again, 16)
                    load_piece(i)
                wg = t["w_expert_gate"].rearrange("l e d f -> (l e) d f")
                wu = t["w_expert_up"].rearrange("l e d f -> (l e) d f")
                wd = t["w_expert_down"].rearrange("l e f d -> (l e) f d")
                expert_loads(sp, layer, wg, wu, wd)
                sp.wait_ge(x_done, NT * 1)
                for n in range(NT):
                    sp.dma_start(t["out"].rearrange("b (n p) d -> (b n) p d", p=P)[n], x_rows[:, n, :])\
                        .then_inc(x_out, 16)
                sp.wait_ge(x_out, 16 * NT)
                layer_end(sp, layer)

        @block.tensor
        def _(pe):
            pe.wait_ge(const_in, 16 * N_CONST)
            pe.wait_ge(sel_in, 16)
            pe.wait_ge(set_ready, 2)
            for c in range(2):
                half = BIAS_LEN // 2
                pe.matmul(acc[c][0:H, 0:half], relb[:], hot[:, c * half:(c + 1) * half],
                          start=True, stop=True).then_inc(bias_mm, 1)

            def wide_turn(w):
                for kt in range(KD):
                    n = KD * w + kt
                    if kt == 0:
                        pe.wait_ge(rows_ready, NT * (w + 1))
                        if w:
                            sums_read(pe, GID["out", 0] - 1 if w == 1 else GID["out", 1], NT - 1)
                    if kt >= 4:
                        pe.wait_ge(wide_lo, n - 3)
                    for n_t in range(NT):
                        mm = pe.transpose(acc[kt % 4][:, n_t * P:(n_t + 1) * P],
                                          rows[:, n_t, kt * P:(kt + 1) * P], ident[:])
                    mm.then_inc(wide_done, 1)

            def piece(s, toks):
                g, k = PIECES[s]
                name, idx, nk, width = GROUPS[g]
                if toks[0] == 0:
                    pe.wait_ge(lo_ready, s + 1)
                if k == 0 and toks[0] == 0:
                    if name == "uq":
                        pe.wait_ge(turn_read, TURN["C", 1] + 1)
                    if name == "ukv":
                        pe.wait_ge(turn_read, TURN["C", 2] + 1)
                    if name == "branch":
                        pe.wait_ge(turn_read, TURN["O", idx // 2, NT - 1] + 1)
                    if g == 0:
                        pe.wait_ge(wide_lo, KD)
                    if name == "out" and idx == 0:
                        pe.wait_ge(wide_lo, 2 * KD)
                for n in toks:
                    if k == 0 and g > 0:
                        sums_read(pe, g - 1, n)
                    ts = slice(n * P, (n + 1) * P)
                    if name == "uq":
                        lhs = cT[k][:, 0, ts], cT[k][:, 1, ts]
                    elif name == "ukv":
                        lhs = cT[2][:, 0, ts], cT[2][:, 1, ts]
                    elif name == "branch":
                        o = (oT0, oT1, oT0)[idx // 2]
                        lhs = o[:, 0, k, ts], o[:, 1, k, ts]
                    else:
                        lhs = xT[:, 0, k, ts], xT[:, 1, k, ts]
                    mm = passes(acc[n][:, 0:width], lhs, (wh[:, s % HL, 0:width], wl[:, s % HL, 0:width]),
                                k == 0, k == nk - 1)
                    if k == nk - 1:
                        mm.then_inc(acc_done, 1)
                if toks[-1] == NT - 1 and k < nk - 1:
                    mm.then_inc(piece_used, 1)

            def scores(i):
                b, qt, h = UNITS[i]
                w = P * (qt + 1)
                out = sc_bank[i % 2][:, 0:w]
                if i >= 2:
                    pe.wait_ge(shifted, i - 1)
                qs = slice(qt * P, (qt + 1) * P)
                if b < 2:
                    q, k = (qT_a, kT_a) if b == 0 else (qT_b, kT_b)
                    r = slice((h % 2) * HD, (h % 2 + 1) * HD)
                    if (qt, h) == (0, 0):
                        pe.wait_ge(turn_read, TURN["Q", 2 * b + 1, NT - 1] + 1)
                        if b == 1:
                            pe.wait_ge(cum_split, 1)
                    if b == 1:
                        pe.matmul(out, sel[:, h, :], cum_p[:, 0:w], start=True, stop=False)
                    pe.matmul(out, q[r, h // 2, qs], k[r, h // 2, 0:w], start=(b == 0), stop=True)\
                        .then_inc(scores_done, 1)
                else:
                    if (qt, h) == (0, 0):
                        pe.wait_ge(turn_read, TURN["Q", 7, NT - 1] + 1)
                    pe.matmul(out, q_c[0:QH, h, qs], kT_c[0:QH, h, 0:w], start=True, stop=True)\
                        .then_inc(scores_done, 1)

            def turn_probs(i):
                b, qt, h = UNITS[i]
                n = TURN["P", i]
                pe.wait_ge(probs_ready, i + 1)
                if n:
                    pe.wait_ge(turn_read, n)
                for kt in range(qt + 1):
                    mm = pe.transpose(turn[:, kt * P:(kt + 1) * P], prob[:, i % 2, kt * P:(kt + 1) * P], ident[:])
                mm.then_inc(turn_done, 1)

            def weighted(i):
                b, qt, h = UNITS[i]
                v = (v_a, v_b, v_c)[b]
                if (qt, h) == (0, 0):
                    pe.wait_ge(v_copied, (4, 8, 16)[b])
                if h == 0 and i:
                    pe.wait_ge(o_ready, i // H)
                pe.wait_ge(turn_read, TURN["P", i] + 1)
                for kt in range(qt + 1):
                    mm = pe.matmul(o_bank[:, h * HD:(h + 1) * HD], probT[:, kt * P:(kt + 1) * P],
                                   v[:, kt, h * HD:(h + 1) * HD], start=(kt == 0), stop=(kt == qt))
                mm.then_inc(pv_done, 1)

            def other_turn(key):
                n = TURN[key]
                if n:
                    pe.wait_ge(turn_read, n)
                if key[0] == "cum":
                    pe.wait_ge(fz_dve, 6)
                    for n_t in range(NT):
                        mm = pe.matmul(turn[0:96, n_t * P:SEQ], lf96[:, n_t, :], tri[:, 0:SEQ - n_t * P],
                                       start=(n_t == 0), stop=(n_t == NT - 1))
                elif key[0] == "C":
                    c0 = H + key[1] * P
                    pe.wait_ge(c_ready, 1)
                    for n_t in range(NT):
                        mm = pe.transpose(turn[:, n_t * P:(n_t + 1) * P], small[:, n_t, c0:c0 + P], ident[:])
                elif key[0] == "O":
                    pe.wait_ge(o_ready, NT * key[1] + key[2] + 1)
                    for c in range(4):
                        mm = pe.transpose(turn[:, c * P:(c + 1) * P], o_rows[:, c * P:(c + 1) * P], ident[:])
                else:
                    _, j, n_t = key
                    pe.wait_ge(post_done, j + 1)
                    for c in range(4):
                        if j < 4:
                            mm = pe.transpose(turn[:, c * P:(c + 1) * P],
                                              head_rows[j % 2][:, n_t, c * P:(c + 1) * P], ident[:])
                        else:
                            mm = pe.transpose(turn[0:QH, c * P:(c + 1) * P],
                                              head_rows[j % 2][:, n_t, c * QH:(c + 1) * QH], ident[:])
                mm.then_inc(turn_done, 1)

            with pe.Fori(0, DEPTH) as layer:
                wide_turn(0)
                for s in range(NP_):
                    if s == OUT0:
                        wide_turn(1)
                    for n_s, (new, old, toks) in enumerate(steps_of(s)):
                        if new is not None:
                            scores(new)
                        if old is not None:
                            turn_probs(old)
                        if toks[-1] == NT - 1:
                            for key in turns_of(s):
                                other_turn(key)
                        piece(s, toks)
                        if old is not None:
                            weighted(old)
                wide_turn(2)
                pe.wait_ge(wide_lo, 3 * KD)
                pe.wait_ge(wr_split, 2)
                for n in range(NT):
                    for k in range(KD):
                        ts = slice(n * P, (n + 1) * P)
                        mm = passes(sc_bank[0][:, n * 32:n * 32 + NG + NE], (xT[:, 0, k, ts], xT[:, 1, k, ts]),
                                    (wrh[:, k, :], wrl[:, k, :]), k == 0, k == KD - 1)
                mm.then_inc(router_done, 1)
                experts_pe(pe)
                layer_end(pe, layer)

        @block.scalar
        def _(act):
            act.wait_ge(bias_mm, 2)
            half = BIAS_LEN // 2
            for c in range(2):
                act.activation(biasT[:, c * half:(c + 1) * half], acc[c][0:H, 0:half], ACT.Copy).then_inc(bias_sb, 1)
            act.wait_ge(rope_ready, 1)
            act.activation(sinT[:], rope_t[:, 0, 0:NT * HALF].rearrange("p (n f) -> p n f", n=NT), ACT.Sin)\
                .then_inc(rope_steps, 1)
            act.activation(cosT[:], rope_t[:, 1, 0:NT * HALF].rearrange("p (n f) -> p n f", n=NT), ACT.Sin)\
                .then_inc(rope_steps, 1)

            def square_rows(w):
                for n in range(NT):
                    if n == 0 and w == 0:
                        act.wait_ge(x_in, 16 * NT)
                    if w == 1:
                        sums_read(act, GID["out", 1], n)
                        act.wait_ge(wide_done, 2 * KD)
                    act.activation(rows[:, n, :], x_rows[:, n, :], ACT.Square, accum_out=ssx[:, n:n + 1])\
                        .then_inc(sum_ready, 1)

            def wide_hi_of(w):
                for kt in range(KD):
                    act.wait_ge(wide_done, KD * w + kt + 1)
                    if w == 0 and kt == 0:
                        act.wait_ge(gains_in, 16 * N_GAINS)
                    if kt == 0 and w:
                        multiplied(act, (OUT0 if w == 1 else NP_) - 1)
                    scale = 0.5 if w == 1 else gcol[:, (w // 2) * KD + kt:(w // 2) * KD + kt + 1]
                    act.activation(xT[:, 0, kt, :], acc[kt % 4][:], ACT.Copy, scale=scale).then_inc(wide_hi, 1)

            def expo(i):
                b, qt, h = UNITS[i]
                w = P * (qt + 1)
                act.wait_ge(shifted, i + 1)
                if h == 0 and i >= 2 * H:
                    act.wait_ge(o_ready, i // H - 1)
                act.activation(prob[:, i % 2, 0:w], prob[:, i % 2, 0:w], ACT.Exp, scale=-1.0,
                               bias=nmax[:, i % 2:i % 2 + 1],
                               accum_out=den[:, (i // H) % 2, h:h + 1]).then_inc(probs_ready, 1)

            def turned(key):
                n = TURN[key]
                act.wait_ge(turn_done, n + 1)
                if key[0] == "P":
                    w = P * (UNITS[key[1]][1] + 1)
                    if key[1]:
                        act.wait_ge(pv_done, key[1])
                    act.activation(probT[:, 0:w], turn[:, 0:w], ACT.Copy).then_inc(turn_read, 1)
                elif key[0] == "cum":
                    act.activation(cum[:], turn[0:96, :], ACT.Copy).then_inc(turn_read, 1)
                elif key[0] == "C":
                    act.wait_ge(rows_ready, NT)
                    act.activation(cT[key[1]][:, 0, :], turn[:], ACT.Copy, scale=gc[:, key[1]:key[1] + 1])\
                        .then_inc(turn_hi, 1)
                elif key[0] == "O":
                    _, b, qt = key
                    o = (oT0, oT1, oT0)[b]
                    if b == 2 and qt == 0:
                        multiplied(act, END[GID["branch", 1]])
                    if b == 1 and qt == 0:
                        multiplied(act, END[GID["uq", 1]])
                    act.activation(o[:, 0, :, qt * P:(qt + 1) * P],
                                   turn[:].rearrange("p (c s) -> p c s", c=4), ACT.Copy).then_inc(turn_hi, 1)
                else:
                    _, j, n_t = key
                    ts = slice(n_t * P, (n_t + 1) * P)
                    if j < 4:
                        dst = (qT_a, kT_a, qT_b, kT_b)[j][:, :, ts]
                        act.activation(dst, turn[:].rearrange("p (c s) -> p c s", c=4), ACT.Copy,
                                       scale=ghead[:, j:j + 1]).then_inc(turn_read, 1)
                    else:
                        a_done = 4 * H * 1
                        if n_t == 0:
                            act.wait_ge(pv_done, a_done)
                        full = q_c if j < 6 else kT_c
                        dst = full[0:QH, 4 * (j % 2):4 * (j % 2) + 4, ts]
                        act.activation(dst, turn[0:QH, :].rearrange("p (c s) -> p c s", c=4), ACT.Copy,
                                       scale=ghead[0:QH, 4 + (j - 4) // 2:5 + (j - 4) // 2]).then_inc(turn_read, 1)

            def squares_of(j):
                width = (512, 4 * QH, 512)[(j - 2) // 2 if j >= 4 else 0]
                for n in range(NT):
                    m = 4 * j + n
                    act.wait_ge(rows_copied, m + 1)
                    if m >= 2:
                        act.wait_ge(sq_summed, m - 1)
                    if m == 8:
                        act.wait_ge(cum_split, 1)
                    act.activation(squares[:, m % 2, 0:width], head_rows[j % 2][:, n, 0:width], ACT.Square)\
                        .then_inc(sq_ready, 1)
                if j >= 6:
                    if j == 6:
                        act.wait_ge(pv_done, 4 * H)
                    for n in range(NT):
                        act.activation(v_c[:, n, 256 * (j - 6):256 * (j - 5)].rearrange("p (h c) -> p h c", h=4),
                                       head_rows[j % 2][:, n, :].rearrange("p (h c) -> p h c", h=4)[:, :, NOPE:],
                                       ACT.Copy).then_inc(v_copied, 1)

            with act.Fori(0, DEPTH) as layer:
                square_rows(0)
                wide_hi_of(0)
                for i in range(LEAD):
                    split_hi(i, width_of(i))
                for s in range(NP_):
                    if s == OUT0:
                        wide_hi_of(1)
                    for new, old, toks in steps_of(s):
                        if old is not None:
                            turned(("P", old))
                        if new is not None:
                            expo(new)
                    for key in turns_of(s):
                        turned(key)
                    if s + LEAD < NP_:
                        split_hi(s + LEAD, width_of(s + LEAD))
                    if s:
                        g = PIECES[s - 1][0]
                        if END[g] == s - 1 and GROUPS[g][0] == "gate":
                            for n in range(NT):
                                act.wait_ge(acc_done, 4 * g + n + 1)
                                if GROUPS[g][1]:
                                    act.wait_ge(branch_ready, 4 * (GROUPS[g][1] - 1) + n + 1)
                                act.activation(gate_t[:, n, :], acc[n][:], ACT.Tanh, scale=0.5).then_inc(gate_read, 1)
                    for g, j in POST_AT.items():
                        if s == END[g] + 2:
                            squares_of(j)
                    if s == SMALL_END + 2:
                        act.wait_ge(small_copied, NT)
                        act.wait_ge(sq_summed, 8)
                        for c, (c0, c1) in enumerate(((H, H + Q_LORA), (H + Q_LORA, H + Q_LORA + KV_LORA),
                                                      (H + Q_LORA + KV_LORA, N_SMALL))):
                            for n in range(NT):
                                m = NT * c + n
                                if m >= 4:
                                    act.wait_ge(csq_ready, m - 3)
                                act.activation(squares[:, (m % 4) // 2, 256 * (m % 2):256 * (m % 2) + c1 - c0], small[:, n, c0:c1], ACT.Square,
                                               accum_out=ssc[:, c, n:n + 1]).then_inc(csq_ready, 1)
                        act.wait_ge(fz_dve, 2)
                        act.activation(fz[:, 2, :], fz[:, 1, :], ACT.Exp, scale=-1.0).then_inc(fz_act, 1)
                        act.wait_ge(fz_act, 1)
                        act.activation(fz[:, 3, :], fz[:, 2, :], ACT.Ln, bias=1.0).then_inc(fz_act, 1)
                square_rows(1)
                wide_hi_of(2)
                act.wait_ge(gains_in, 16 * N_GAINS)
                act.activation(wrh[:], wr[:], ACT.Copy).then_inc(wr_split, 1)
                act.wait_ge(r_dve, 3)
                act.activation(r4[:, 1], r4[:, 0], ACT.Exp).then_inc(r_act, 1)
                act.wait_ge(r_pair, 1)
                act.activation(r1[:, 5, :], r1[:, 4, :], ACT.Exp).then_inc(r_act, 1)
                experts_act(act)
                layer_end(act, layer)


        @block.vector
        def _(dve):
            nc.vector.memset(relb[:], 1.0).then_inc(set_ready, 1)
            nc.vector.memset(ghead[:], 1.0).then_inc(set_ready, 1)
            dve.wait_ge(const_in, 16 * N_CONST)
            nc.vector.tensor_copy(pos_f[:], pos_i[:]).then_inc(dve_c, 1)
            ang, turns, r = (rope_t[:, c, 0:NT * HALF] for c in (0, 1, 2))
            v3 = lambda a: a.rearrange("p (n f) -> p n f", n=NT)
            dve.wait_ge(dve_c, 1)
            nc.vector.tensor_tensor(v3(ang), pos_f[:].unsqueeze(2).broadcast_to([P, NT, HALF]),
                                    freq[:].unsqueeze(1).broadcast_to([P, NT, HALF]), ALU.mult).then_inc(dve_c, 1)
            dve.wait_ge(dve_c, 2)
            ROUND = 1.5 * 2.0 ** 23
            nc.vector.tensor_scalar(turns, ang, 1.0 / (2 * math.pi), ROUND, ALU.mult, ALU.add).then_inc(dve_c, 1)
            dve.wait_ge(dve_c, 3)
            nc.vector.tensor_scalar(turns, turns, ROUND, None, ALU.subtract).then_inc(dve_c, 1)
            dve.wait_ge(dve_c, 4)
            parts = (6.28125, 0.0019350051879882812, 2 * math.pi - 6.28125 - 0.0019350051879882812)
            c = 4
            src = ang
            for part in parts:
                nc.vector.scalar_tensor_tensor(out=r, in0=turns, scalar=-part, in1=src, op0=ALU.mult,
                                               op1=ALU.add).then_inc(dve_c, 1)
                c += 1
                dve.wait_ge(dve_c, c)
                src = r
            LIM = 3.1415925
            nc.vector.tensor_scalar(ang, r, LIM, -LIM, ALU.min, ALU.max).then_inc(dve_c, 1)
            dve.wait_ge(dve_c, c + 1)
            nc.vector.scalar_tensor_tensor(out=r, in0=ang, scalar=-1.0, in1=ang, op0=ALU.mult, op1=ALU.min)\
                .then_inc(dve_c, 1)
            dve.wait_ge(dve_c, c + 2)
            nc.vector.tensor_scalar(turns, r, math.pi / 2, None, ALU.add).then_inc(rope_ready, 1)

            def scaled_rows(w):
                for n in range(NT):
                    if n == 0:
                        dve.wait_ge(scale_ready, 1 + w)
                    nc.vector.tensor_scalar(rows[:, n, :], x_rows[:, n, :], rsx[:, n:n + 1], None, ALU.mult)\
                        .then_inc(rows_ready, 1)

            def wide_lo_of(w):
                for kt in range(KD):
                    dve.wait_ge(wide_hi, KD * w + kt + 1)
                    hi = xT[:, 0, kt, :].bitcast(F32)
                    scale = 0.5 if w == 1 else gcol[:, (w // 2) * KD + kt:(w // 2) * KD + kt + 1]
                    nc.vector.scalar_tensor_tensor(out=xT[:, 1, kt, :], in0=acc[kt % 4][:], scalar=scale, in1=hi,
                                                   op0=ALU.mult, op1=ALU.subtract).then_inc(wide_lo, 1)

            def shift(i):
                b, qt, h = UNITS[i]
                w = P * (qt + 1)
                dve.wait_ge(scores_done, i + 1)
                if i == 0:
                    dve.wait_ge(bias_in, 16 * H)
                if i >= 2:
                    dve.wait_ge(turn_done, TURN["P", i - 2] + 1)
                add = bias_a[:, h, SEQ - w:] if b == 0 else mask[:, SEQ - w:]
                nc.vector.tensor_tensor_reduce(prob[:, i % 2, 0:w], sc_bank[i % 2][:, 0:w], add, -SOFT[b], 3.0e38,
                                               ALU.add, ALU.min, nmax[:, i % 2:i % 2 + 1]).then_inc(shifted, 1)

            def normalise(i):
                q = i // H
                dve.wait_ge(probs_ready, i + 1)
                if q:
                    b, qt, _ = UNITS[i - H]
                    dve.wait_ge(turn_done, TURN["O", b, qt] + 1)
                nc.vector.reciprocal(rden[:], den[:, q % 2, :]).then_inc(dve_own, 1)
                dve.wait_ge(pv_done, i + 1)
                dve.wait_ge(dve_own, q + 1)
                nc.vector.tensor_tensor(o_rows[:].rearrange("p (h c) -> p h c", h=H),
                                        o_bank[:].rearrange("p (h c) -> p h c", h=H),
                                        rden[:].unsqueeze(2).broadcast_to([P, H, HD]), ALU.mult).then_inc(o_ready, 1)

            def turned_lo(key):
                dve.wait_ge(turn_hi, LO_TURN[key] + 1)
                if key[0] == "C":
                    k = key[1]
                    nc.vector.scalar_tensor_tensor(out=cT[k][:, 1, :], in0=turn[:], scalar=gc[:, k:k + 1],
                                                   in1=cT[k][:, 0, :].bitcast(F32), op0=ALU.mult,
                                                   op1=ALU.subtract).then_inc(turn_read, 1)
                else:
                    _, b, qt = key
                    o = (oT0, oT1, oT0)[b]
                    qs = slice(qt * P, (qt + 1) * P)
                    nc.vector.tensor_tensor(o[:, 1, :, qs], turn[:].rearrange("p (c s) -> p c s", c=4),
                                            o[:, 0, :, qs].bitcast(F32), ALU.subtract).then_inc(turn_read, 1)

            def read_group(g, n):
                name, idx, _, width = GROUPS[g]
                dve.wait_ge(acc_done, 4 * g + n + 1)
                src = acc[n][:, 0:width]
                if g in POST_AT:
                    j = POST_AT[g]
                    if j >= 2 and n == 0:
                        dve.wait_ge(turn_done, TURN["Q", j - 2, NT - 1] + 1)
                    if j >= 2 and n == 0 and j - 2 >= 6:
                        dve.wait_ge(v_copied, 16)
                    if j == 0 and n == 0:
                        dve.wait_ge(wide_done, KD)
                    nc.vector.tensor_copy(head_rows[j % 2][:, n, 0:width], src).then_inc(acc_read, 1)
                elif name == "v":
                    v = (v_a, v_b)[idx]
                    nc.vector.tensor_copy(v[:, n, :], src).then_inc(acc_read, 1)
                elif name == "small":
                    nc.vector.tensor_copy(small[:, n, :], src).then_inc(acc_read, 1)
                elif name == "branch":
                    b, c = idx // 2, idx % 2
                    cs = slice(512 * c, 512 * (c + 1))
                    if n == 0 and b == 0 and c == 0:
                        dve.wait_ge(turn_done, TURN["C", 2] + 1)
                        dve.wait_ge(post_done, 3)
                    if n == 0 and b == 0 and c == 1:
                        dve.wait_ge(turn_done, TURN["Q", 6, NT - 1] + 1)
                    if b == 0:
                        nc.vector.scalar_tensor_tensor(out=rows[:, n, cs], in0=gate_t[:, n, :], scalar=1.0, in1=src,
                                                       op0=ALU.add, op1=ALU.mult).then_inc(acc_read, 1)
                    else:
                        m = 4 * (idx - 2) + n
                        nc.vector.scalar_tensor_tensor(out=gate_t[:, n, :], in0=gate_t[:, n, :], scalar=1.0,
                                                       in1=src, op0=ALU.add, op1=ALU.mult).then_inc(acc_read, 1)
                        sums_read(dve, g, n)
                        nc.vector.tensor_tensor(rows[:, n, cs], rows[:, n, cs], gate_t[:, n, :], ALU.add)\
                            .then_inc(merged, 1)
                else:
                    cs = slice(512 * idx, 512 * (idx + 1))
                    if n == 0 and idx == 0:
                        dve.wait_ge(x_again, 16 * NT)
                    nc.vector.tensor_tensor(x_rows[:, n, cs], x_rows[:, n, cs], src, ALU.add).then_inc(acc_read, 1)

            def after_read(g, n):
                name, idx, _, _ = GROUPS[g]
                if name not in ("qk", "uq", "ukv", "v", "small", "branch"):
                    return
                if name == "branch" and idx >= 2:
                    dve.wait_ge(merged, 4 * (idx - 2) + n + 1)
                sums_read(dve, g, n)
                s_ = {"v": v_copied, "small": small_copied, "branch": branch_ready}.get(name, rows_copied)
                dve.sem_inc(s_, 1)

            def sums_of(j):
                name = POSTS[j][0]
                for n in range(NT):
                    m = 4 * j + n
                    dve.wait_ge(sq_ready, m + 1)
                    if n == 0 and j:
                        dve.wait_ge(post_done, j)
                    sq = squares[:, m % 2, :]
                    if name == "qk":
                        nc.vector.tensor_reduce(ssq[:, n, :], sq.rearrange("p (h c) -> p h c", h=H), AX_X, ALU.add)\
                            .then_inc(sq_summed, 1)
                    elif name == "uq":
                        v = sq[:, 0:4 * QH].rearrange("p (h c) -> p h c", h=4)
                        nc.vector.tensor_reduce(ssq[:, n, 0:4], v[:, :, 0:NOPE], AX_X, ALU.add)
                        nc.vector.tensor_reduce(ssq[:, n, 4:8], v[:, :, NOPE:], AX_X, ALU.add).then_inc(sq_summed, 1)
                    else:
                        v = sq.rearrange("p (h c) -> p h c", h=4)
                        nc.vector.tensor_reduce(ssq[:, n, 0:4], v[:, :, 0:NOPE], AX_X, ALU.add).then_inc(sq_summed, 1)

            with dve.Fori(0, DEPTH) as layer:
                scaled_rows(0)
                wide_lo_of(0)
                for i in range(LEAD):
                    split_lo(i, width_of(i))
                for s in range(NP_):
                    if s == OUT0:
                        for n in range(NT):
                            read_group(PIECES[s - 1][0], n)
                        dve.wait_ge(merged, 16)
                        for n in range(NT):
                            dve.sem_inc(rows_ready, 1)
                        wide_lo_of(1)
                    g = PIECES[s - 1][0] if s else None
                    ended = s and s != OUT0 and END[g] == s - 1 and GROUPS[g][0] != "gate"
                    steps = steps_of(s)
                    for n_s, (new, old, toks) in enumerate(steps):
                        half = toks[:len(toks) // 2] if len(toks) == 4 else toks[:1]
                        rest = toks[len(half):]
                        if ended:
                            for n in half:
                                read_group(g, n)
                        if new is not None:
                            shift(new)
                        if ended:
                            for n in rest:
                                read_group(g, n)
                            for n in toks:
                                after_read(g, n)
                        if len(steps) == 2 and old is not None and UNITS[old][2] == H - 1:
                            normalise(old)
                    for _, old, _ in (steps_of(s - 1) if s else []):
                        if len(steps_of(s - 1)) == 1 and old is not None and UNITS[old][2] == H - 1:
                            normalise(old)
                    for key in turns_of(s):
                        if key in LO_TURN:
                            turned_lo(key)
                    if s + LEAD < NP_:
                        split_lo(s + LEAD, width_of(s + LEAD))
                    for gg, j in POST_AT.items():
                        if s == END[gg] + 2:
                            sums_of(j)
                    if s == SMALL_END + 2:
                        z, a, ln = fz[:, 0, :], fz[:, 1, :], fz[:, 3, :]
                        hf = lambda q: q.rearrange("p (n h) -> p n h", n=NT)
                        nc.vector.tensor_tensor(hf(z), small[:, :, 0:H],
                                                bfg[:].unsqueeze(1).broadcast_to([P, NT, H]), ALU.add)\
                            .then_inc(fz_dve, 1)
                        dve.wait_ge(fz_dve, 1)
                        nc.vector.scalar_tensor_tensor(out=a, in0=z, scalar=-1.0, in1=z, op0=ALU.mult,
                                                       op1=ALU.max).then_inc(fz_dve, 1)
                        dve.wait_ge(fz_act, 2)
                        nc.vector.scalar_tensor_tensor(out=a, in0=z, scalar=0.0, in1=ln, op0=ALU.min,
                                                       op1=ALU.subtract).then_inc(fz_dve, 1)
                        dve.wait_ge(fz_dve, 3)
                        nc.vector.memset(lf96, 0.0).then_inc(csum_ready, 1)
                        dve.wait_ge(csum_ready, 1)
                        for c in range(3):
                            nc.vector.tensor_copy(lf96[:, :, 32 * c:32 * c + H], hf(a)).then_inc(fz_dve, 1)
                    if s == SMALL_END + 9:
                        dve.wait_ge(turn_read, TURN["cum",] + 1)
                        chain = (lambda ins, c=[0]: (ins.then_inc(post_aux, 1), c.__setitem__(0, c[0] + 1),
                                                     dve.wait_ge(post_aux, c[0])))
                        chain(nc.vector.tensor_copy(cum_b[:], cum[:]))
                        nc.vector.tensor_copy(cum_p[0:32, :], cum_b[0:32, :])
                        chain(nc.vector.tensor_tensor(cum[:], cum[:], cum_b[:], ALU.subtract))
                        chain(nc.vector.tensor_copy(cum_b[:], cum[:]))
                        nc.vector.tensor_copy(cum_p[32:64, :], cum_b[32:64, :])
                        chain(nc.vector.tensor_tensor(cum[:], cum[:], cum_b[:], ALU.subtract))
                        nc.vector.tensor_copy(cum_p[64:96, :], cum[64:96, :]).then_inc(cum_split, 1)
                g = len(GROUPS) - 1
                for n in range(NT):
                    read_group(g, n)
                scaled_rows(1)
                wide_lo_of(2)
                dve.wait_ge(wr_split, 1)
                nc.vector.tensor_tensor(wrl[:], wr[:], wrh[:].bitcast(F32), ALU.subtract).then_inc(wr_split, 1)
                route(dve)
                experts_dve(dve)
                layer_end(dve, layer)

        @block.gpsimd
        def _(pool):
            nc.gpsimd.memset(pw[:], -0.5).then_inc(pool_c, 1)
            pool.dma_start(sel[:].rearrange("p h q -> p (h q)"), t["sel"]).then_inc(sel_in, 16)
            pool.wait_ge(pool_c, 1)
            pool.wait_ge(rope_steps, 2)
            with pool.Fori(0, DEPTH) as layer:
                own = [0]

                def step(ins):
                    ins.then_inc(pool_own, 1)
                    own[0] += 1
                    pool.wait_ge(pool_own, own[0])

                def rsqrt(dst, src, n, divisor):
                    step(nc.gpsimd.tensor_scalar(src, src, 1.0 / divisor, EPS, ALU.mult, ALU.add))
                    return nc.gpsimd.tensor_tensor(dst, src, pw[:, 0:n], ALU.pow)

                def heads_normed(j):
                    name, idx = POSTS[j]
                    pool.wait_ge(sq_summed, 4 * j + 4)
                    buf = head_rows[j % 2]
                    if name == "qk":
                        step(rsqrt(rsq[:].rearrange("p n h -> p (n h)"), ssq[:].rearrange("p n h -> p (n h)"), 32, HD))
                        for n in range(NT):
                            v = buf[:, n, :].rearrange("p (h c) -> p h c", h=H)
                            ins = nc.gpsimd.tensor_tensor(v, v, rsq[:, n, :].unsqueeze(2).broadcast_to([P, H, HD]),
                                                          ALU.mult)
                        ins.then_inc(post_done, 1)
                        return
                    pw4 = pw[:, 0:16].rearrange("p (n h) -> p n h", n=NT)
                    step(nc.gpsimd.tensor_scalar(ssq[:, :, 0:4], ssq[:, :, 0:4], 1.0 / NOPE, EPS, ALU.mult, ALU.add))
                    step(nc.gpsimd.tensor_tensor(rsq[:, :, 0:4], ssq[:, :, 0:4], pw4, ALU.pow))
                    if name == "uq":
                        step(nc.gpsimd.tensor_scalar(ssq[:, :, 4:8], ssq[:, :, 4:8], 1.0 / ROPE, EPS, ALU.mult, ALU.add))
                        step(nc.gpsimd.tensor_tensor(rsq[:, :, 4:8], ssq[:, :, 4:8], pw4, ALU.pow))
                        for n in range(NT):
                            v = buf[:, n, 0:4 * QH].rearrange("p (h c) -> p h c", h=4)
                            nc.gpsimd.tensor_tensor(v[:, :, 0:NOPE], v[:, :, 0:NOPE],
                                                    rsq[:, n, 0:4].unsqueeze(2).broadcast_to([P, 4, NOPE]), ALU.mult)
                            step(nc.gpsimd.tensor_tensor(v[:, :, NOPE:], v[:, :, NOPE:],
                                                         rsq[:, n, 4:8].unsqueeze(2).broadcast_to([P, 4, ROPE]),
                                                         ALU.mult))
                            step(nc.gpsimd.tensor_tensor(v[:, :, NOPE:], v[:, :, NOPE:],
                                                         grope[:, 0, :].unsqueeze(1).broadcast_to([P, 4, ROPE]),
                                                         ALU.mult))
                            rotate(v[:, :, NOPE:NOPE + HALF], v[:, :, NOPE + HALF:], n, 4)
                        pool.sem_inc(post_done, 1)
                        return
                    if j == 6:
                        pool.wait_ge(v_copied, 12)
                    else:
                        pool.wait_ge(v_copied, 16)
                    for n in range(NT):
                        src = buf[:, n, :].rearrange("p (h c) -> p h c", h=4)
                        tmp = rope_t[:, 0:4, :].rearrange("p a b -> p (a b)")[:, 0:4 * NOPE]\
                            .rearrange("p (h c) -> p h c", h=4)
                        step(nc.gpsimd.tensor_tensor(tmp, src[:, :, 0:NOPE],
                                                     rsq[:, n, 0:4].unsqueeze(2).broadcast_to([P, 4, NOPE]), ALU.mult))
                        dst = buf[:, n, 0:4 * QH].rearrange("p (h c) -> p h c", h=4)
                        nc.gpsimd.tensor_copy(dst[:, :, 0:NOPE], tmp)
                        step(nc.gpsimd.tensor_copy(dst[:, :, NOPE:], kr[:, n, :].unsqueeze(1).broadcast_to([P, 4, ROPE])))
                    pool.sem_inc(post_done, 1)

                def rotate(x1, x2, n, heads):
                    shape = [P, heads, HALF]
                    c = cosT[:, n, :].unsqueeze(1).broadcast_to(shape)
                    s_ = sinT[:, n, :].unsqueeze(1).broadcast_to(shape)
                    m = [rope_t[:, q, 0:heads * HALF].rearrange("p (h f) -> p h f", h=heads) for q in range(4)]
                    tt = nc.gpsimd.tensor_tensor
                    tt(m[0], x1, c, ALU.mult)
                    tt(m[1], x2, s_, ALU.mult)
                    tt(m[2], x1, s_, ALU.mult)
                    step(tt(m[3], x2, c, ALU.mult))
                    tt(x1, m[0], m[1], ALU.subtract)
                    step(tt(x2, m[2], m[3], ALU.add))

                def row_scale(w):
                    pool.wait_ge(sum_ready, NT * (w + 1))
                    step(nc.gpsimd.tensor_scalar(ssx[:], ssx[:], 1.0 / D, EPS, ALU.mult, ALU.add))
                    nc.gpsimd.tensor_tensor(rsx[:], ssx[:], pw[:, 0:NT], ALU.pow).then_inc(scale_ready, 1)

                row_scale(0)
                heads_normed(0)
                heads_normed(1)
                pool.wait_ge(csq_ready, 3 * NT)
                for c, width in enumerate((Q_LORA, KV_LORA, ROPE)):
                    step(rsqrt(rsc[:, c, :], ssc[:, c, :], NT, width))
                for n in range(NT):
                    nc.gpsimd.tensor_scalar(small[:, n, H:H + Q_LORA], small[:, n, H:H + Q_LORA],
                                            rsc[:, 0, n:n + 1], None, ALU.mult)
                    ins = nc.gpsimd.tensor_scalar(small[:, n, H + Q_LORA:H + Q_LORA + KV_LORA],
                                                  small[:, n, H + Q_LORA:H + Q_LORA + KV_LORA],
                                                  rsc[:, 1, n:n + 1], None, ALU.mult)
                ins.then_inc(c_ready, 1)
                for n in range(NT):
                    step(nc.gpsimd.tensor_scalar(kr[:, n, :], small[:, n, N_SMALL - ROPE:], rsc[:, 2, n:n + 1],
                                                 None, ALU.mult))
                    step(nc.gpsimd.tensor_tensor(kr[:, n, :], kr[:, n, :], grope[:, 1, :], ALU.mult))
                    rotate(kr[:, n, 0:HALF].unsqueeze(1), kr[:, n, HALF:].unsqueeze(1), n, 1)
                for j in range(2, 8):
                    heads_normed(j)
                row_scale(1)
                pool.wait_ge(arrived, 4 * layer + 4)
                pool.sem_inc(resumed, 1)
                pool.sem_clear(cleared)
                pool.sem_inc(released, 1)



_INS = ["x", "positions", "rel_bias", "norm_mix", "w_in", "b_forget", "gq_a", "gk_a", "gq_b", "gk_b", "gq_c", "gk_c",
        "norm_cq", "norm_ckv", "w_uq", "w_ukv", "w_branch", "w_out", "norm_ffn", "w_router_group", "b_router_group",
        "w_router_expert", "b_router_expert", "w_expert_gate", "w_expert_up", "w_expert_down"]


def kernel(**inputs):
    import numpy as _np
    import concourse.bacc as _bacc
    from concourse import mybir as _mybir
    from concourse.bass_utils import run_bass_kernel_spmd as _run

    nc = _bacc.Bacc("TRN2", target_bir_lowering=False, num_devices=1)
    arrays, t = {}, {}
    given = {name: _np.ascontiguousarray(inputs[name]) for name in _INS}
    given.update(shape_constants())
    for name, a in given.items():
        arrays[f"in_{name}_dram"] = a
        t[name] = nc.dram_tensor(f"in_{name}_dram", a.shape, _mybir.dt.from_np(a.dtype), kind="ExternalInput").ap()
    t["out"] = nc.dram_tensor("out_0_dram", (1, SEQ, D), _mybir.dt.float32, kind="ExternalOutput").ap()
    build(nc, t)
    r = _run(nc, [arrays], core_ids=[0])
    return r.results[0]["out_0_dram"]
```

```python
from contextlib import ExitStack
import math

import numpy as np
import concourse.bass as bass
from concourse import mybir

F32 = mybir.dt.float32
F32R = mybir.dt.float32r
BF16 = mybir.dt.bfloat16
I32 = mybir.dt.int32
ALU = mybir.AluOpType
ACT = mybir.ActivationFunctionType
AX_X = mybir.AxisListType.X

P = 128
D = 1024
SEQ = 512
DEPTH = 2
KD = D // P
NT = SEQ // P
H = 8
HD = 64
BW = H * HD
NOPE, ROPE = 64, 32
QH = NOPE + ROPE
HALF = ROPE // 2
Q_LORA, KV_LORA = 256, 128
N_BUCKETS, MAX_DISTANCE = 32, 2048
DILATED_PAIRS = ((128, 1), (512, 4), (2048, 16))
NG, EG, NE, FF = 4, 4, 16, 256
EPS = 1e-6
MASKED = -1.0e30
COL_SMALL = 6 * BW
N_SMALL = H + Q_LORA + KV_LORA + ROPE
COL_GATE = COL_SMALL + N_SMALL
LEAD = 2
NCH = 23
RAW, HL = 4, 3
BIAS_LEN = SEQ + P


def shape_constants():
    i = np.arange(BIAS_LEN)
    dist = SEQ - 1 - i
    d0 = np.maximum(dist, 0)
    exact = N_BUCKETS // 2
    ratio = np.log(np.maximum(d0, exact) / exact) / np.log(MAX_DISTANCE / exact)
    large = np.minimum(exact + (ratio * (N_BUCKETS - exact)).astype(np.int32), N_BUCKETS - 1)
    bucket = np.where(d0 < exact, d0, large)
    count = sum(((dist % dil == 0) & (dist <= window)).astype(int) for window, dil in DILATED_PAIRS)
    count = np.where(dist >= 0, count, 0)
    scale = math.sqrt(HD)
    hot = np.zeros((N_BUCKETS + 1, BIAS_LEN), np.float32)
    hot[bucket, i] = np.where(count > 0, scale, 0.0)
    hot[N_BUCKETS] = np.where(count > 0, scale * np.log(np.maximum(count, 1)), MASKED)
    p, j = np.arange(P)[:, None], np.arange(SEQ)[None, :]
    tri = (j >= p).astype(np.float32)
    mask = np.where(j <= p + SEQ - P, 0.0, MASKED).astype(np.float32)
    sel = np.zeros((3 * 32, H, P), np.float32)
    for h in range(H):
        sel[[h, 32 + h, 64 + h], h] = -scale
    freq = np.broadcast_to(np.float32(10000.0) ** (-np.arange(HALF, dtype=np.float32) / HALF), (P, HALF))
    first = np.broadcast_to(np.arange(4, 0, -1, dtype=np.float32), (P, 4))
    return {"ident": np.eye(P, dtype=np.float32), "hot": hot, "tri": tri, "mask": mask,
            "sel": sel.reshape(96, H * P), "freq": np.ascontiguousarray(freq, np.float32),
            "first": np.ascontiguousarray(first),
            "erow": np.ascontiguousarray(np.broadcast_to(np.arange(NE, dtype=np.float32), (P, NE))),
            "tok_id": np.arange(SEQ, dtype=np.int32).reshape(NT, P).T.copy()}


GROUPS = [("qk", 0, KD, BW), ("qk", 1, KD, BW), ("v", 0, KD, BW), ("small", 0, KD, N_SMALL),
          ("qk", 2, KD, BW), ("qk", 3, KD, BW), ("v", 1, KD, BW),
          ("uq", 0, 2, 4 * QH), ("uq", 1, 2, 4 * QH), ("gate", 0, KD, 512), ("ukv", 0, 1, 512),
          ("ukv", 1, 1, 512), ("branch", 0, 4, 512), ("gate", 1, KD, 512), ("branch", 1, 4, 512)]
for _b in (1, 2):
    for _c in (0, 1):
        GROUPS += [("gate", 2 * _b + _c, KD, 512), ("branch", 2 * _b + _c, 4, 512)]
GROUPS += [("out", 0, KD, 512), ("out", 1, KD, 512)]
PIECES = [(g, k) for g, grp in enumerate(GROUPS) for k in range(grp[2])]
NP_ = len(PIECES)
START = {g: min(s for s, pc in enumerate(PIECES) if pc[0] == g) for g in range(len(GROUPS))}
END = {g: START[g] + GROUPS[g][2] - 1 for g in START}
GID = {(n, i): g for g, (n, i, _, _) in enumerate(GROUPS)}
OUT0 = START[GID["out", 0]]
UNITS = [(b, qt, h) for b in range(3) for qt in range(NT) for h in range(H)]
UNIT_SLOT = {}
_s = END[GID["v", 0]] + 1
for _i, (_b, _qt, _h) in enumerate(UNITS):
    UNIT_SLOT.setdefault(_s, []).append(_i)
    if not (_b > 0 and _qt == 0 and _h % 2 == 0):
        _s += 1
LAST_UNIT_SLOT = _s - 1
POSTS = [("qk", 0), ("qk", 1), ("qk", 2), ("qk", 3), ("uq", 0), ("uq", 1), ("ukv", 0), ("ukv", 1)]
POST_AT = {GID[p]: j for j, p in enumerate(POSTS)}
POST_PE = {}
for _j, _p in enumerate(POSTS):
    _e = END[GID[_p]] + 6 + (2 if _p == ("uq", 1) and False else 0) + (1 if _p == ("ukv", 1) else 0)
    POST_PE.setdefault(_e, []).append((_j, (0, 1)))
    POST_PE.setdefault(_e + 1, []).append((_j, (2, 3)))
SMALL_END = END[GID["small", 0]]
C_TR = {SMALL_END + 9: [("cum",)], SMALL_END + 10: [("C", 0)], SMALL_END + 11: [("C", 1)],
        SMALL_END + 12: [("C", 2)]}
O_TR = {}
for _s0, _us in UNIT_SLOT.items():
    for _i in _us:
        if UNITS[_i][2] == H - 1:
            O_TR.setdefault(_s0 + 3, []).append((UNITS[_i][0], UNITS[_i][1]))


def steps_of(slot):
    us = UNIT_SLOT.get(slot, [])
    if len(us) == 2:
        return [(us[0], us[0] - 1, (0, 1)), (us[1], us[1] - 1, (2, 3))]
    if len(us) == 1:
        return [(us[0], us[0] - 1 if us[0] else None, (0, 1, 2, 3))]
    if slot == LAST_UNIT_SLOT + 1:
        return [(None, len(UNITS) - 1, (0, 1, 2, 3))]
    return [(None, None, (0, 1, 2, 3))]


def turn_order():
    order = {}
    for s in range(OUT0):
        for new, old, _ in steps_of(s):
            if old is not None:
                order[("P", old)] = len(order)
        for key in turns_of(s):
            order[key] = len(order)
    return order


def turns_of(s):
    keys = [("O", b, qt) for b, qt in O_TR.get(s, [])]
    keys += C_TR.get(s, [])
    for j, toks in POST_PE.get(s, []):
        keys += [("Q", j, t) for t in toks]
    return keys


TURN = turn_order()
SOFT = {0: 1.0 / math.sqrt(HD), 1: 1.0 / math.sqrt(HD), 2: 1.0 / math.sqrt(QH)}


def build(nc, t):
    ctx = ExitStack()
    with ctx:
        def sb(name, shape, dt=F32):
            return ctx.enter_context(nc.sbuf_tensor(name, shape, dt))

        def sem(name):
            return ctx.enter_context(nc.semaphore(name))

        bank = [ctx.enter_context(nc.psum_tensor(f"bank{i}", [P, 512], F32)) for i in range(8)]
        acc, sc_bank, turn, o_bank = bank[0:4], bank[4:6], bank[6], bank[7]

        with nc.sbuf_tensor("x_rows", [P, NT, D], F32) as x_rows:
            pass
        oT1 = sb("oT1", [P, 2, 4, SEQ], F32R)
        oT0 = sb("oT0", [P, 2, 4, SEQ], F32R)
        rows = sb("rows", [P, NT, D])
        xT = sb("xT", [P, 2, KD, SEQ], F32R)
        raw = sb("raw", [P, RAW, 512])
        wh = sb("wh", [P, HL, 512], F32R)
        wl = sb("wl", [P, HL, 512], F32R)
        q_c = sb("q_c", [P, H, SEQ])
        bias_a = q_c
        ac = sb("ac", [P, 6144])
        qT_a = ac[:, 0:2048].rearrange("p (c s) -> p c s", c=4)
        kT_a = ac[:, 2048:4096].rearrange("p (c s) -> p c s", c=4)
        v_a = ac[:, 4096:6144].rearrange("p (n c) -> p n c", n=NT)
        kT_c = ac[:, 0:4096].rearrange("p (h s) -> p h s", h=H)
        v_c = v_a
        bqkv = sb("bqkv", [P, 6144])
        qT_b = bqkv[:, 0:2048].rearrange("p (c s) -> p c s", c=4)
        kT_b = bqkv[:, 2048:4096].rearrange("p (c s) -> p c s", c=4)
        v_b = bqkv[:, 4096:6144].rearrange("p (n c) -> p n c", n=NT)
        head_odd = sb("head_odd", [P, NT, 512])
        head_rows = [rows[:, :, 512:D], head_odd]
        small = rows[:, :, 0:N_SMALL]
        squares = sb("squares", [P, 2, 512])
        gate_t = sb("gate_t", [P, NT, 512])
        prob = sb("prob", [P, 2, 512])
        probT = sb("probT", [P, 512])
        o_rows = sb("o_rows", [P, 512])
        cT_kv = sb("cT_kv", [P, 2, 1, SEQ], F32R)
        cT = [oT1[:, :, 0, :], oT1[:, :, 1, :], cT_kv[:, :, 0, :]]
        ident = sb("ident", [P, P])
        tri = gate_t[:, 0, :]
        mask = sb("mask", [P, SEQ])
        sel = sb("sel", [96, H, P], BF16)
        cum = squares[0:96, 0, :]
        cum_b = squares[0:96, 1, 0:SEQ // 2].bitcast(BF16)
        cum_p = sb("cum_p", [96, SEQ], BF16)
        lf96 = gate_t[:, 1, 0:NT * 96].rearrange("p (n c) -> p n c", n=NT)
        cosT = sb("cosT", [P, NT, HALF])
        sinT = sb("sinT", [P, NT, HALF])
        freq = sb("freq", [P, HALF])
        first = sb("first", [P, 4])
        pos_i = sb("pos_i", [P, NT], I32)
        pos_f = sb("pos_f", [P, NT])
        ssx = sb("ssx", [P, NT])
        rsx = sb("rsx", [P, NT])
        pw = sb("pw", [P, 32])
        ssq = sb("ssq", [P, NT, 8])
        rsq = sb("rsq", [P, NT, 8])
        ssc = sb("ssc", [P, 3, NT])
        rsc = sb("rsc", [P, 3, NT])
        nmax = sb("nmax", [P, 2])
        den = sb("den", [P, 2, H])
        rden = sb("rden", [P, H])
        rope_t = sb("rope_t", [P, 4, 4 * HALF])
        kr = sb("kr", [P, NT, ROPE])
        fz = sb("fz", [P, 4, NT * H])
        gcol = sb("gcol", [P, KD])
        ghead = sb("ghead", [P, 6])
        gc = sb("gc", [P, 3])
        grope = sb("grope", [P, 2, ROPE])
        bfg = sb("bfg", [P, H])
        bro = sb("bro", [P, NG + NE])
        wr = sb("wr", [P, KD, NG + NE])
        wrh = sb("wrh", [P, KD, NG + NE], F32R)
        wrl = sb("wrl", [P, KD, NG + NE], F32R)
        relb = sb("relb", [N_BUCKETS + 1, H])
        r4 = prob[:, 0, 0:128].rearrange("p (q n c) -> p q n c", q=8, n=NT)
        r1 = prob[:, 0, 128:176].rearrange("p (q n) -> p q n", q=12)
        lg = prob[:, 0, 192:192 + NT * (NG + NE)].rearrange("p (n c) -> p n c", n=NT)
        grow = ac[:, 0:D]
        tri2 = ac[:, 1024:1280]
        work = ac[:, 1280:1536].rearrange("p (q n e) -> p q n e", q=4, n=NT)
        mk = ac[:, 1536:1728].rearrange("p (q n e) -> p q n e", q=3, n=NT)
        few = ac[:, 1728:1848].rearrange("p (q e) -> p q e", q=5)
        xg = ac[:, 2048:4096].rearrange("p (b d) -> p b d", b=2)
        ysb = ac[:, 4096:6144].rearrange("p (b d) -> p b d", b=2)
        pair_raw = bqkv.rearrange("p (j k c) -> p j k c", j=6, k=2)
        pair_w = xT.rearrange("p a k s -> p (a k s)")[:, 0:6144].rearrange("p (r h k c) -> p r h k c", r=3, h=2, k=2)
        xgT_all = oT0.rearrange("p a k s -> p (a k s)").rearrange("p (b h k s) -> p b h k s", b=2, h=2, k=KD)
        xgT = [xgT_all[:, 0], xgT_all[:, 1]]
        hidT = cT_kv.rearrange("p a o s -> p (a o s)")[:, 0:512].rearrange("p (h k s) -> p h k s", h=2, k=2)
        th, hid = squares[:, 0, 0:FF], squares[:, 1, 0:FF]
        erow = sb("erow", [P, NE])
        tok_id = sb("tok_id", [P, NT], I32)
        addr_i = sb("addr_i", [P, 2 * NT], I32)
        tab_i = sb("tab_i", [P, NCH], I32)
        idx_ov = sb("idx_ov", [P, 1], I32)
        zero_i = sb("zero_i", [P, NCH], I32)
        ctl = sb("ctl", [1, 8], I32)
        h_bank, y_bank, hid_bank, xg_bank, count_bank = bank[0:2], bank[2:4], bank[4], bank[5:7], bank[7]
        tok_tab = nc.dram_tensor("tok_tab", [P * NCH, 1], I32, kind="Internal")
        xn_dram = nc.dram_tensor("xn_dram", [SEQ, D], F32, kind="Internal").ap()
        yslots = nc.dram_tensor("yslots", [P, NCH, D], F32, kind="Internal").ap()
        hot = head_odd[0:N_BUCKETS + 1, :, :].rearrange("p b c -> p (b c)")[:, 0:BIAS_LEN]
        biasT = squares[0:H, :, :].rearrange("p a b -> p (a b)")[:, 0:BIAS_LEN]
        bias_dram = nc.dram_tensor("bias_dram", [H, P, BIAS_LEN], F32, kind="Internal")

        OV = ["w", "x", "idx", "hi", "lo", "used", "turned", "xhi", "xT", "th", "silu", "hid", "hturned", "hhi",
              "hT", "y0", "y1", "out"]
        NAMES = ["x_in", "gains_in", "bias_in", "x_again", "hi_ready", "lo_ready", "piece_used", "acc_done",
                 "acc_read", "gate_read", "sum_ready", "scale_ready", "rows_ready", "wide_done", "wide_hi", "wide_lo",
                 "turn_done", "turn_hi", "turn_read", "scores_done", "shifted", "probs_ready", "pv_done",
                 "o_ready", "v_copied", "rows_copied", "sq_ready", "sq_summed", "post_done", "post_aux",
                 "gate_ready", "branch_ready", "merged", "cum_split", "small_copied", "fz_dve", "fz_act",
                 "csq_ready", "csum_ready", "c_ready", "kr_ready", "pool_own", "dve_own",
                 "router_done", "r_dve", "r_act", "r_mask", "r_counted", "r_addr", "r_ctl", "wr_split", "r_pair",
                 "experts_const", "xn_out", "tab_zeroed", "tab_out", "tab_in",
                 "pair_hi_ready", "pair_lo_ready", "pair_used", "h_done", "y_done", "xg_turned", "xgT_hi", "xgT_lo",
                 "th_ready", "silu_half", "hid_ready", "hid_turned", "hidT_hi", "hidT_lo", "waits_passed",
                 "x_first", "x_out", "x_done"]
        RAW_SEMS = [sem(f"raw_in{i}") for i in range(RAW)]
        pair_in = [sem(f"pair_in{j}") for j in range(6)]
        xg_in = [sem(f"xg_in{b}") for b in range(2)]
        y_out = [sem(f"y_out{b}") for b in range(2)]
        y_read = [sem(f"y_read{b}") for b in range(2)]
        back_in = [sem(f"back_in{n}") for n in range(NT)]
        ov = {n: sem(f"over_{n}") for n in OV}
        S = {n: sem(n) for n in NAMES}
        (x_in, gains_in, bias_in, x_again, hi_ready, lo_ready, piece_used, acc_done, acc_read, gate_read, sum_ready,
         scale_ready, rows_ready, wide_done, wide_hi, wide_lo, turn_done, turn_hi, turn_read, scores_done,
         shifted, probs_ready, pv_done, o_ready, v_copied, rows_copied, sq_ready, sq_summed, post_done,
         post_aux, gate_ready, branch_ready, merged, cum_split, small_copied, fz_dve, fz_act, csq_ready,
         csum_ready, c_ready, kr_ready, pool_own, dve_own, router_done, r_dve, r_act, r_mask, r_counted, r_addr,
         r_ctl, wr_split, r_pair, experts_const, xn_out, tab_zeroed, tab_out, tab_in, pair_hi_ready,
         pair_lo_ready, pair_used, h_done, y_done, xg_turned, xgT_hi, xgT_lo, th_ready, silu_half, hid_ready,
         hid_turned, hidT_hi, hidT_lo, waits_passed, x_first, x_out, x_done) = (S[n] for n in NAMES)
        arrived, released, resumed = sem("arrived"), sem("released"), sem("resumed")
        const_in, bias_mm, bias_sb, bias_out, rope_ready, set_ready, rope_steps = (
            sem(n) for n in ("const_in", "bias_mm", "bias_sb", "bias_out", "rope_ready", "set_ready", "rope_steps"))
        cleared = range(RAW_SEMS[0].num, x_done.num + 1)
        assert len(cleared) == RAW + 16 + len(OV) + len(NAMES)
        N_CONST = 10
        sel_in, table_zero, slots_set = sem("sel_in"), sem("table_zero"), sem("slots_set")
        dve_c, pool_c = sem("dve_c"), sem("pool_c")
        LO_TURN = {}
        for key in sorted(TURN, key=TURN.get):
            if key[0] in ("C", "O"):
                LO_TURN[key] = len(LO_TURN)

        block = ctx.enter_context(nc.Block())

        def raw_landed(eng, i):
            eng.wait_ge(RAW_SEMS[i % RAW], 16 * (i // RAW + 1))

        def layer_end(eng, layer):
            eng.sem_inc(arrived, 1)
            eng.wait_ge(released, layer + 1)
            eng.sem_inc(resumed, 1)

        def at(ap, layer):
            v = ap[bass.ds(layer, 1)]
            names = "abcd"[:len(ap.shape) - 1]
            return v.rearrange(f"o {' '.join(names)} -> (o {names[0]}) {' '.join(names[1:])}")

        N_GAINS = 1 + 8 + 4 + 2 + 3 + 2 + 1

        def skew(dram, h):
            ap = dram[h:h + 1, 0, P - 1:P - 1 + SEQ]
            return bass.AP(tensor=ap.tensor, offset=ap.offset, ap=[[BIAS_LEN - 1, P], [1, SEQ]])

        def sums_read(eng, g, n):
            gate = GROUPS[g][0] == "gate"
            before = sum((GROUPS[q][0] == "gate") == gate for q in range(g))
            eng.wait_ge(gate_read if gate else acc_read, 4 * before + n + 1)

        def multiplied(eng, i):
            g = PIECES[i][0]
            if i == END[g]:
                return eng.wait_ge(acc_done, 4 * (g + 1))
            return eng.wait_ge(piece_used, sum(q != END[PIECES[q][0]] for q in range(i + 1)))

        def split_hi(i, width):
            raw_landed(nc.scalar, i)
            if i >= HL:
                multiplied(nc.scalar, i - HL)
            nc.scalar.activation(wh[:, i % HL, 0:width], raw[:, i % RAW, 0:width], ACT.Copy).then_inc(hi_ready, 1)

        def split_lo(i, width):
            nc.vector.wait_ge(hi_ready, i + 1)
            raw_landed(nc.vector, i)
            nc.vector.tensor_tensor(wl[:, i % HL, 0:width], raw[:, i % RAW, 0:width],
                                    wh[:, i % HL, 0:width].bitcast(F32), ALU.subtract).then_inc(lo_ready, 1)

        def width_of(i):
            return GROUPS[PIECES[i][0]][3]

        def passes(out, lhs, rhs, start, stop):
            nc.tensor.matmul(out, lhs[0], rhs[0], start=start, stop=False)
            nc.tensor.matmul(out, lhs[0], rhs[1], start=False, stop=False)
            return nc.tensor.matmul(out, lhs[1], rhs[0], start=False, stop=stop)

        def is_const(e, value):
            return isinstance(e, int) and e == value

        def pos_wait(eng, s_, value):
            if not isinstance(value, int) or value > 0:
                eng.wait_ge(s_, value)

        def expert_steps(eng, step):
            step(0, 0, 0)
            step(1, 1, 0)
            with eng.Fori(0, (NE - 4) // 2) as i:
                step(2 * i + 2, 0, i + 1)
                step(2 * i + 3, 1, i + 1)
            step(NE - 2, 0, NE // 2 - 1)
            step(NE - 1, 1, NE // 2 - 1)

        def pair_no(e, j):
            return j if is_const(e, -1) else 4 + 6 * e + j

        def pair_role(e, j):
            return 4 + j if is_const(e, NE - 1) else j

        def pair_ring(e, j):
            return (j if is_const(e, -1) else 1 + j) % 3

        def pair_landed(eng, e, j):
            role = pair_role(e, j)
            eng.wait_ge(pair_in[role], 32 * (e + 2) if role < 4 else 16 * (e + 1))

        def pair_multiplied(eng, e, j):
            if j == 3:
                eng.wait_ge(h_done, e + 2)
            elif j > 3:
                eng.wait_ge(y_done, 2 * e + j - 3)
            else:
                eng.wait_ge(pair_used, 3 * (e + 1) + j + 1)

        def pair_hi(e, j):
            pair_landed(nc.scalar, e, j)
            if j >= 3:
                pair_multiplied(nc.scalar, e, j - 3)
            elif is_const(e, 0):
                pair_multiplied(nc.scalar, -1, j + 1)
            elif not is_const(e, -1):
                pair_multiplied(nc.scalar, e - 1, j + 3)
            nc.scalar.activation(pair_w[:, pair_ring(e, j), 0], pair_raw[:, pair_role(e, j)], ACT.Copy)\
                .then_inc(pair_hi_ready, 1)

        def pair_lo(e, j):
            nc.vector.wait_ge(pair_hi_ready, pair_no(e, j) + 1)
            pair_landed(nc.vector, e, j)
            nc.vector.tensor_tensor(pair_w[:, pair_ring(e, j), 1], pair_raw[:, pair_role(e, j)],
                                    pair_w[:, pair_ring(e, j), 0].bitcast(F32), ALU.subtract)\
                .then_inc(pair_lo_ready, 1)

        def load_gate_up(sp, expert, j, s_):
            for half, w in ((0, "w_expert_gate"), (1, "w_expert_up")):
                src = at(t[w].rearrange("l e (k p) f -> (l e) p k f", p=P), expert)
                sp.dma_start(pair_raw[:, j, :, half * FF:(half + 1) * FF], src[:, 2 * j:2 * j + 2, :]).then_inc(s_, 16)

        def load_down(sp, expert, c, s_):
            src = at(t["w_expert_down"].rearrange("l e (k p) d -> (l e) p k d", p=P), expert)
            sp.dma_start(pair_raw[:, 4 + c], src[:, :, 512 * c:512 * (c + 1)]).then_inc(s_, 16)

        def gate_up(out, x_, r_, j):
            for k in range(2):
                kt = 2 * j + k
                mm = passes(out, (x_[:, 0, kt], x_[:, 1, kt]), (pair_w[:, r_, 0, k], pair_w[:, r_, 1, k]),
                            kt == 0, kt == KD - 1)
            return mm

        def down(out, r_):
            for k in range(2):
                mm = passes(out, (hidT[:, 0, k], hidT[:, 1, k]), (pair_w[:, r_, 0, k], pair_w[:, r_, 1, k]),
                            k == 0, k == 1)
            return mm

        def turn_chunk_rows(src, inc):
            for b in range(2):
                for k in range(4):
                    mm = nc.tensor.transpose(xg_bank[b][:, k * P:(k + 1) * P],
                                             src[:, (4 * b + k) * P:(4 * b + k + 1) * P], ident[:])
                mm.then_inc(inc, 1)

        def turn_hidden(inc):
            for k in range(2):
                mm = nc.tensor.transpose(hid_bank[:, k * P:(k + 1) * P], hid[:, k * P:(k + 1) * P], ident[:])
            mm.then_inc(inc, 1)

        def chunk_T(x_, half, b):
            return x_[:, half, 4 * b:4 * b + 4].rearrange("p k s -> p (k s)")

        def hidden_T(half):
            return hidT[:, half].rearrange("p k s -> p (k s)")

        def overflow(eng, body):
            eng.wait_ge(r_ctl, 1)
            n_over = eng.value_load(ctl[0:1, 7:8], min_val=0, max_val=NCH - NE)
            with eng.If(n_over > 0):
                for par in range(2):
                    eng.wait_ge(y_out[par], 16 * NE // 2)
                with eng.Fori(0, n_over) as c:
                    body(c)
                    eng.wait_ge(ov["out"], 16 * (c + 1))
                    eng.sem_inc(waits_passed, 1)

        def overflow_sp(sp, layer):
            def body(c):
                expert = sp.value_load(ctl[0:1, bass.ds(c, 1)], min_val=0, max_val=NE - 1)
                for j in range(4):
                    load_gate_up(sp, layer * NE + expert, j, ov["w"])
                for q in range(2):
                    load_down(sp, layer * NE + expert, q, ov["w"])
            overflow(sp, body)

        def overflow_pe(pe):
            def body(c):
                pe.wait_ge(ov["x"], 16 * (c + 1))
                turn_chunk_rows(xg[:, 0, :], ov["turned"])
                pe.wait_ge(ov["xT"], 2 * c + 2)
                for j in range(4):
                    pe.wait_ge(ov["lo"], 6 * c + j + 1)
                    gate_up(h_bank[0][:], xgT[0], j % 3, j).then_inc(ov["used"], 1)
                pe.wait_ge(ov["hid"], c + 1)
                turn_hidden(ov["hturned"])
                pe.wait_ge(ov["hT"], c + 1)
                for q in range(2):
                    pe.wait_ge(ov["lo"], 6 * c + 5 + q)
                    down(y_bank[q][:], (4 + q) % 3).then_inc(ov["used"], 1)
            overflow(pe, body)

        def overflow_act(act):
            def body(c):
                def hi(j):
                    act.wait_ge(ov["w"], 160 * (c + 1))
                    if j >= 3:
                        act.wait_ge(ov["used"], 6 * c + j - 2)
                    nc.scalar.activation(pair_w[:, j % 3, 0], pair_raw[:, j], ACT.Copy).then_inc(ov["hi"], 1)
                for j in range(3):
                    hi(j)
                for b in range(2):
                    act.wait_ge(ov["turned"], 2 * c + b + 1)
                    nc.scalar.activation(chunk_T(xgT[0], 0, b), xg_bank[b][:], ACT.Copy).then_inc(ov["xhi"], 1)
                for j in range(3, 6):
                    hi(j)
                act.wait_ge(ov["used"], 6 * c + 4)
                nc.scalar.activation(th, h_bank[0][:, 0:FF], ACT.Tanh, scale=0.5).then_inc(ov["th"], 1)
                act.wait_ge(ov["hturned"], c + 1)
                nc.scalar.activation(hidden_T(0), hid_bank[:, 0:2 * P], ACT.Copy).then_inc(ov["hhi"], 1)
                act.wait_ge(ov["used"], 6 * c + 5)
                nc.scalar.activation(ysb[:, 0, 0:512], y_bank[0][:], ACT.Copy).then_inc(ov["y0"], 1)
                act.wait_ge(ov["y0"], c + 1)
                act.wait_ge(ov["y1"], c + 1)
                act.wait_ge(slots_set, 16)
                act.dma_start(yslots[:, bass.ds(NE + c, 1), :].rearrange("p o d -> p (o d)"), ysb[:, 0, :])\
                    .then_inc(ov["out"], 16)
            overflow(act, body)

        def overflow_dve(dve):
            def body(c):
                nc.vector.tensor_copy(idx_ov[:], tab_i[:, bass.ds(NE + c, 1)]).then_inc(ov["idx"], 1)

                def lo(j):
                    dve.wait_ge(ov["hi"], 6 * c + j + 1)
                    nc.vector.tensor_tensor(pair_w[:, j % 3, 1], pair_raw[:, j], pair_w[:, j % 3, 0].bitcast(F32),
                                            ALU.subtract).then_inc(ov["lo"], 1)
                for j in range(3):
                    lo(j)
                for b in range(2):
                    dve.wait_ge(ov["xhi"], 2 * c + b + 1)
                    nc.vector.tensor_tensor(chunk_T(xgT[0], 1, b), xg_bank[b][:], chunk_T(xgT[0], 0, b).bitcast(F32),
                                            ALU.subtract).then_inc(ov["xT"], 1)
                for j in range(3, 6):
                    lo(j)
                dve.wait_ge(ov["th"], c + 1)
                nc.vector.scalar_tensor_tensor(out=th, in0=th, scalar=1.0, in1=h_bank[0][:, 0:FF], op0=ALU.add,
                                               op1=ALU.mult).then_inc(ov["silu"], 1)
                dve.wait_ge(ov["silu"], c + 1)
                nc.vector.tensor_tensor(hid, th, h_bank[0][:, FF:], ALU.mult).then_inc(ov["hid"], 1)
                dve.wait_ge(ov["hhi"], c + 1)
                nc.vector.tensor_tensor(hidden_T(1), hid_bank[:, 0:2 * P], hidden_T(0).bitcast(F32), ALU.subtract)\
                    .then_inc(ov["hT"], 1)
                dve.wait_ge(ov["used"], 6 * c + 6)
                nc.vector.tensor_copy(ysb[:, 0, 512:], y_bank[1][:]).then_inc(ov["y1"], 1)
            overflow(dve, body)

        def overflow_pool(pool):
            def body(c):
                pool.wait_ge(ov["idx"], c + 1)
                pool.sem_inc(waits_passed, 1)
                gather(xg[:, 0, :], xn_dram, idx_ov[:, 0:1], ov["x"])
            overflow(pool, body)

        def gather(dst, dram, index, inc):
            nc.gpsimd.indirect_dma_start(out=dst, out_offset=None, in_=dram,
                                         in_offset=bass.IndirectOffsetOnAxis(ap=index, axis=0)).then_inc(inc, 16)

        def experts_sp(sp, layer):
            def passed(value):
                sp.wait_ge(pair_lo_ready, value)
                sp.sem_inc(waits_passed, 1)

            def step(e, par, half):
                if not is_const(e, NE - 1):
                    for j in range(4):
                        passed(j + 1 if is_const(e, 0) else pair_no(e - 1, j) + 1)
                        load_gate_up(sp, layer * NE + (e + 1), j, pair_in[j])
                if not is_const(e, 0):
                    for c in range(2):
                        passed(pair_no(e - 1, 4 + c) + 1)
                        load_down(sp, layer * NE + e, c, pair_in[4 + c])

            expert_steps(sp, step)
            overflow_sp(sp, layer)

        def experts_pe(pe):
            pe.wait_ge(r_mask, 1)
            for n in range(NT):
                for m in range(n + 1):
                    nc.tensor.matmul(count_bank[:, n * NE:(n + 1) * NE], tri2[:, 0:P] if m == n else tri2[:, P:],
                                     mk[:, 2, m, :], start=(m == 0), stop=(m == n))
            for m in range(NT):
                mm = nc.tensor.matmul(count_bank[:, NT * NE:(NT + 1) * NE], tri2[:, P:], mk[:, 2, m, :],
                                      start=(m == 0), stop=(m == NT - 1))
            mm.then_inc(r_counted, 1)

            def turn_chunk(e, par, half):
                pe.wait_ge(xg_in[par], 16 * (half + 1))
                pos_wait(pe, xgT_lo, 2 * e)
                turn_chunk_rows(xg[:, par, :], xg_turned)

            turn_chunk(0, 0, 0)
            turn_chunk(1, 1, 0)
            for j in range(4):
                pe.wait_ge(pair_lo_ready, j + 1)
                gate_up(h_bank[0][:], xgT[0], pair_ring(-1, j), j).then_inc(h_done if j == 3 else pair_used, 1)

            def step(e, par, half):
                for j in range(4):
                    if not is_const(e, NE - 1):
                        if j == 0:
                            pos_wait(pe, hid_ready, e)
                            pe.wait_ge(xgT_lo, 2 * (e + 2))
                        pe.wait_ge(pair_lo_ready, pair_no(e, j) + 1)
                        gate_up(h_bank[1 - par][:], xgT[1 - par], pair_ring(e, j), j)\
                            .then_inc(h_done if j == 3 else pair_used, 1)
                    if j == 1:
                        pe.wait_ge(hid_ready, e + 1)
                        pos_wait(pe, hidT_lo, e)
                        turn_hidden(hid_turned)
                if not (isinstance(e, int) and e >= NE - 2):
                    turn_chunk(e + 2, par, half + 1)
                pe.wait_ge(hidT_lo, e + 1)
                for c in range(2):
                    j = c if is_const(e, NE - 1) else 4 + c
                    pos_wait(pe, y_read[c], e)
                    pe.wait_ge(pair_lo_ready, pair_no(e, j) + 1)
                    down(y_bank[c][:], pair_ring(e, j)).then_inc(y_done, 1)

            expert_steps(pe, step)
            overflow_pe(pe)

        def experts_act(act):
            def rows_hi(e, par):
                for b in range(2):
                    act.wait_ge(xg_turned, 2 * e + b + 1)
                    nc.scalar.activation(chunk_T(xgT[par], 0, b), xg_bank[b][:], ACT.Copy).then_inc(xgT_hi, 1)

            def gate_tanh(e, par):
                act.wait_ge(h_done, e + 1)
                pos_wait(act, hid_ready, e)
                nc.scalar.activation(th, h_bank[par][:, 0:FF], ACT.Tanh, scale=0.5).then_inc(th_ready, 1)

            pair_hi(-1, 2)
            rows_hi(0, 0)
            rows_hi(1, 1)
            pair_hi(-1, 3)
            pair_hi(0, 0)
            pair_hi(0, 1)
            gate_tanh(0, 0)
            pair_hi(0, 2)

            def step(e, par, half):
                end = is_const(e, NE - 1)
                if not end:
                    pair_hi(e, 3)
                act.wait_ge(hid_turned, e + 1)
                nc.scalar.activation(hidden_T(0), hid_bank[:, 0:2 * P], ACT.Copy).then_inc(hidT_hi, 1)
                if not end:
                    pair_hi(e, 4)
                    pair_hi(e, 5)
                    gate_tanh(e + 1, 1 - par)
                    if not is_const(e, NE - 2):
                        rows_hi(e + 2, par)
                    pair_hi(e + 1, 0)
                act.wait_ge(y_done, 2 * e + 1)
                pos_wait(act, y_out[par], 16 * half)
                nc.scalar.activation(ysb[:, par, 0:512], y_bank[0][:], ACT.Copy).then_inc(y_read[0], 1)
                if not end:
                    pair_hi(e + 1, 1)
                    if not is_const(e, NE - 2):
                        pair_hi(e + 1, 2)
                act.wait_ge(y_read[0], e + 1)
                act.wait_ge(y_read[1], e + 1)
                dst = yslots[:, e:e + 1, :] if isinstance(e, int) else yslots[:, bass.ds(e, 1), :]
                act.dma_start(dst.rearrange("p o d -> p (o d)"), ysb[:, par, :]).then_inc(y_out[par], 16)

            expert_steps(act, step)
            overflow_act(act)

        def experts_dve(dve):
            def rows_lo(e, par):
                for b in range(2):
                    dve.wait_ge(xgT_hi, 2 * e + b + 1)
                    nc.vector.tensor_tensor(chunk_T(xgT[par], 1, b), xg_bank[b][:],
                                            chunk_T(xgT[par], 0, b).bitcast(F32), ALU.subtract).then_inc(xgT_lo, 1)

            def silu(e, par):
                dve.wait_ge(th_ready, e + 1)
                nc.vector.scalar_tensor_tensor(out=th, in0=th, scalar=1.0, in1=h_bank[par][:, 0:FF], op0=ALU.add,
                                               op1=ALU.mult).then_inc(silu_half, 1)
                dve.wait_ge(silu_half, e + 1)
                pos_wait(dve, hid_turned, e)
                nc.vector.tensor_tensor(hid, th, h_bank[par][:, FF:], ALU.mult).then_inc(hid_ready, 1)

            for j in range(3):
                pair_lo(-1, j)
            rows_lo(0, 0)
            rows_lo(1, 1)
            pair_lo(-1, 3)
            pair_lo(0, 0)
            pair_lo(0, 1)
            silu(0, 0)
            pair_lo(0, 2)

            def step(e, par, half):
                end = is_const(e, NE - 1)
                if not end:
                    pair_lo(e, 3)
                dve.wait_ge(hidT_hi, e + 1)
                nc.vector.tensor_tensor(hidden_T(1), hid_bank[:, 0:2 * P], hidden_T(0).bitcast(F32), ALU.subtract)\
                    .then_inc(hidT_lo, 1)
                if not end:
                    pair_lo(e, 4)
                    pair_lo(e, 5)
                    silu(e + 1, 1 - par)
                    if not is_const(e, NE - 2):
                        rows_lo(e + 2, par)
                    pair_lo(e + 1, 0)
                    pair_lo(e + 1, 1)
                dve.wait_ge(y_done, 2 * e + 2)
                pos_wait(dve, y_out[par], 16 * half)
                nc.vector.tensor_copy(ysb[:, par, 512:], y_bank[1][:]).then_inc(y_read[1], 1)
                if not end and not is_const(e, NE - 2):
                    pair_lo(e + 1, 2)

            expert_steps(dve, step)
            overflow_dve(dve)
            for k in range(2):
                for n in range(NT):
                    if k == 0:
                        dve.wait_ge(back_in[n], 32)
                    else:
                        dve.wait_ge(x_first, n + 1)
                    nc.vector.scalar_tensor_tensor(out=x_rows[:, n, :], in0=back(n, k), scalar=r1[:, 9 + k, n:n + 1],
                                                   in1=x_rows[:, n, :], op0=ALU.mult, op1=ALU.add)\
                        .then_inc((x_first, x_done)[k], 1)

        def back(n, k):
            return rows[:, n, :] if k else q_c.rearrange("p h s -> p (h s)")[:, n * D:(n + 1) * D]

        def experts_pool(pool):
            pool.wait_ge(tab_zeroed, 16)
            pool.wait_ge(r_addr, 1)
            for k in range(2):
                for n in range(NT):
                    nc.gpsimd.indirect_dma_start(
                        out=tok_tab[:], in_=tok_id[:, n:n + 1], in_offset=None,
                        out_offset=bass.IndirectOffsetOnAxis(ap=addr_i[:, k * NT + n:k * NT + n + 1], axis=0)
                    ).then_inc(tab_out, 16)
            pool.wait_ge(tab_out, 16 * 2 * NT)
            pool.dma_start(tab_i[:], tok_tab.rearrange("(p c) o -> p (c o)", c=NCH)).then_inc(tab_in, 16)
            pool.wait_ge(tab_in, 16)
            pool.wait_ge(xn_out, 16 * NT)
            for e in range(NE):
                if e >= 2:
                    pool.wait_ge(xg_turned, 2 * (e - 1))
                gather(xg[:, e % 2, :], xn_dram, tab_i[:, e:e + 1], xg_in[e % 2])
            overflow_pool(pool)
            for par in range(2):
                pool.wait_ge(y_out[par], 16 * NE // 2)
            pool.wait_ge(slots_set, 16)
            for n in range(NT):
                for k in range(2):
                    gather(back(n, k), yslots.rearrange("p c d -> (p c) d"),
                           addr_i[:, k * NT + n:k * NT + n + 1], back_in[n])

        def route(dve):
            count = [0]

            def step(ins):
                ins.then_inc(r_dve, 1)
                count[0] += 1
                dve.wait_ge(r_dve, count[0])

            def b4(a):
                return a.unsqueeze(2).broadcast_to([P, NT, 4])

            def be(a):
                return a.unsqueeze(1).broadcast_to([P, NT, NE])

            fst = first[:].unsqueeze(1).broadcast_to([P, NT, 4])
            tt, tr, ts = nc.vector.tensor_tensor, nc.vector.tensor_reduce, nc.vector.tensor_scalar
            stt = nc.vector.scalar_tensor_tensor
            dve.wait_ge(router_done, 1)
            step(tt(lg, sc_bank[0][:, 0:NT * 32].rearrange("p (n c) -> p n c", n=NT)[:, :, 0:NG + NE],
                    bro[:].unsqueeze(1).broadcast_to([P, NT, NG + NE]), ALU.add))
            gl = lg[:, :, 0:NG]
            step(tr(r1[:, 0, :], gl, AX_X, ALU.max))
            step(tt(r4[:, 0], gl, b4(r1[:, 0, :]), ALU.subtract))

            def first_best(dst, values, best, tmp, tmp1):
                step(tt(tmp, values, b4(best), ALU.is_ge))
                step(tt(tmp, tmp, fst, ALU.mult))
                step(tr(tmp1, tmp, AX_X, ALU.max))
                step(tt(dst, tmp, b4(tmp1), ALU.is_equal))

            g1, e1, e2, esel = r4[:, 2], r4[:, 3], r4[:, 4], r4[:, 5]
            first_best(g1, gl, r1[:, 0, :], r4[:, 6], r1[:, 1, :])
            el = lg[:, :, NG:].rearrange("p n (g e) -> p n g e", g=NG)
            gsel = work[:, 0].rearrange("p n (g e) -> p n g e", g=NG)
            for n in range(NT):
                ins = tt(gsel[:, n], el[:, n], g1[:, n].unsqueeze(2).broadcast_to([P, NG, EG]), ALU.mult)
            step(ins)
            for n in range(NT):
                ins = tr(esel[:, n], gsel[:, n].rearrange("p g e -> p e g"), AX_X, ALU.add)
            step(ins)
            step(tr(r1[:, 2, :], esel, AX_X, ALU.max))
            first_best(e1, esel, r1[:, 2, :], r4[:, 6], r1[:, 1, :])
            step(stt(out=r4[:, 7], in0=e1, scalar=MASKED, in1=esel, op0=ALU.mult, op1=ALU.add))
            step(tr(r1[:, 3, :], r4[:, 7], AX_X, ALU.max))
            first_best(e2, r4[:, 7], r1[:, 3, :], r4[:, 6], r1[:, 1, :])
            for k, ek in ((0, e1), (1, e2)):
                for n in range(NT):
                    ins = tt(mk[:, k, n].rearrange("p (g e) -> p g e", g=NG),
                             ek[:, n].unsqueeze(1).broadcast_to([P, NG, EG]),
                             g1[:, n].unsqueeze(2).broadcast_to([P, NG, EG]), ALU.mult)
            step(ins)
            step(tt(mk[:, 2], mk[:, 0], mk[:, 1], ALU.add))
            dve.sem_inc(r_mask, 1)
            step(tt(r1[:, 4, :], r1[:, 3, :], r1[:, 2, :], ALU.subtract))
            dve.sem_inc(r_pair, 1)
            dve.wait_ge(r_counted, 1)
            rank, over, q_, place = work[:, 1], work[:, 2], work[:, 3], work[:, 0]
            cnt, ovc, extra = few[:, 0, 8:], few[:, 1, 8:], few[:, 2, 8:]
            step(ts(rank, count_bank[:, 0:NT * NE].rearrange("p (n e) -> p n e", n=NT), -1.0, None, ALU.add))
            step(nc.vector.tensor_copy(cnt, count_bank[:, NT * NE:(NT + 1) * NE]))
            step(nc.vector.memset(few[:, 3:5, :], 0.0))
            step(ts(ovc, cnt, float(P), None, ALU.is_gt))
            step(stt(out=ovc, in0=cnt, scalar=2.0 * P, in1=ovc, op0=ALU.is_gt, op1=ALU.add))
            step(stt(out=ovc, in0=cnt, scalar=3.0 * P, in1=ovc, op0=ALU.is_gt, op1=ALU.add))
            step(nc.vector.tensor_copy(few[:, 3, 8:], ovc))
            for b, sh in enumerate((1, 2, 4, 8)):
                s_, d_ = few[:, 3 + b % 2], few[:, 4 - b % 2]
                step(tt(d_[:, 8:], s_[:, 8:], s_[:, 8 - sh:8 + NE - sh], ALU.add))
            incl = few[:, 3, 8:]
            step(tt(extra, incl, ovc, ALU.subtract))
            step(stt(out=extra, in0=extra, scalar=float(NE - 1), in1=erow[:], op0=ALU.add, op1=ALU.subtract))
            step(ts(over, rank, float(P), None, ALU.is_ge))
            step(stt(out=q_, in0=rank, scalar=2.0 * P, in1=over, op0=ALU.is_ge, op1=ALU.add))
            step(stt(out=q_, in0=rank, scalar=3.0 * P, in1=q_, op0=ALU.is_ge, op1=ALU.add))
            step(tt(place, over, be(extra), ALU.mult))
            step(tt(place, place, be(erow[:]), ALU.add))
            step(stt(out=place, in0=rank, scalar=float(NCH), in1=place, op0=ALU.mult, op1=ALU.add))
            step(stt(out=place, in0=q_, scalar=float(1 - P * NCH), in1=place, op0=ALU.mult, op1=ALU.add))
            for k in range(2):
                step(tt(work[:, 1], mk[:, k], place, ALU.mult))
                step(tr(r1[:, 6 + k, :], work[:, 1], AX_X, ALU.add))
            step(nc.vector.tensor_copy(addr_i[:], r1[:, 6:8, :].rearrange("p k n -> p (k n)")))
            dve.sem_inc(r_addr, 1)
            n_ov = NCH - NE
            cmp = work[0:1, 1:3].rearrange("p a n e -> p (a n e)")[:, 0:n_ov * NE].rearrange("p (c e) -> p c e", c=n_ov)
            step(tt(cmp, incl[0:1].unsqueeze(1).broadcast_to([1, n_ov, NE]),
                    erow[0:1, 0:n_ov].unsqueeze(2).broadcast_to([1, n_ov, NE]), ALU.is_le))
            step(tr(few[0:1, 2, 0:n_ov], cmp, AX_X, ALU.add))
            step(nc.vector.tensor_copy(ctl[0:1, 0:n_ov], few[0:1, 2, 0:n_ov]))
            step(nc.vector.tensor_copy(ctl[0:1, 7:8], few[0:1, 3, 8 + NE - 1:8 + NE]))
            dve.sem_inc(r_ctl, 1)
            dve.wait_ge(r_act, 2)
            step(tr(r1[:, 6, :], r4[:, 1], AX_X, ALU.add))
            step(ts(r1[:, 7, :], r1[:, 5, :], 1.0, None, ALU.add))
            step(tt(r1[:, 8, :], r1[:, 7, :], r1[:, 6, :], ALU.mult))
            step(nc.vector.reciprocal(r1[:, 9, :], r1[:, 8, :]))
            step(ts(r1[:, 9, :], r1[:, 9, :], 0.5, None, ALU.mult))
            step(tt(r1[:, 10, :], r1[:, 9, :], r1[:, 5, :], ALU.mult))

        @block.sync
        def _(sp):
            sp.dma_start(t["out"], t["x"]).then_inc(const_in, 16)
            sp.dma_start(ident[:], t["ident"]).then_inc(const_in, 16)
            sp.dma_start(hot, t["hot"]).then_inc(const_in, 16)
            sp.dma_start(mask[:], t["mask"]).then_inc(const_in, 16)
            sp.dma_start(freq[:], t["freq"]).then_inc(const_in, 16)
            sp.dma_start(first[:], t["first"]).then_inc(const_in, 16)
            sp.dma_start(erow[:], t["erow"]).then_inc(const_in, 16)
            sp.dma_start(tok_id[:], t["tok_id"]).then_inc(const_in, 16)
            with nc.allow_non_contiguous_dma(reason="512 positions, once"):
                sp.dma_start(pos_i[:], t["positions"].rearrange("b (n p) -> p (b n)", p=P)).then_inc(const_in, 16)
            sp.wait_ge(set_ready, 2)
            sp.dma_start(relb[0:N_BUCKETS, :], t["rel_bias"]).then_inc(const_in, 16)
            sp.wait_ge(bias_sb, 2)
            sp.dma_start(bias_dram[:], biasT.unsqueeze(1).broadcast_to([H, P, BIAS_LEN]))\
                .then_inc(bias_out, 16)
            sp.wait_ge(const_in, 16 * N_CONST)
            sp.wait_ge(bias_out, 16)
            with sp.Fori(0, DEPTH) as layer:
                w_in = at(t["w_in"], layer)
                sp.dma_start(tri, t["tri"]).then_inc(gains_in, 16)
                for n in range(NT):
                    sp.dma_start(x_rows[:, n, :], t["out"].rearrange("b (n p) d -> (b n) p d", p=P)[n])\
                        .then_inc(x_in, 16)

                def load_piece(i):
                    if i >= RAW:
                        sp.wait_ge(lo_ready, i - RAW + 1)
                    g, k = PIECES[i]
                    name, idx, _, width = GROUPS[g]
                    dst = raw[:, i % RAW, 0:width]
                    if name in ("qk", "v", "small", "gate"):
                        col = {"qk": [0, BW, 3 * BW, 4 * BW], "v": [2 * BW, 5 * BW], "small": [COL_SMALL],
                               "gate": [COL_GATE + 512 * c for c in range(6)]}[name][idx]
                        src = w_in[k * P:(k + 1) * P, col:col + width]
                    elif name == "uq":
                        src = at(t["w_uq"], layer)[k * P:(k + 1) * P, idx * width:(idx + 1) * width]
                    elif name == "ukv":
                        src = at(t["w_ukv"], layer)[:, idx * 512:(idx + 1) * 512]
                    elif name == "branch":
                        b, c = idx // 2, idx % 2
                        src = at(t["w_branch"].rearrange("l g c d -> l (g c) d"), layer)[
                            b * BW + k * P:b * BW + (k + 1) * P, c * 512:(c + 1) * 512]
                    else:
                        src = at(t["w_out"], layer)[k * P:(k + 1) * P, idx * 512:(idx + 1) * 512]
                    sp.dma_start(dst, src).then_inc(RAW_SEMS[i % RAW], 16)

                for i in range(RAW):
                    load_piece(i)
                with nc.allow_non_contiguous_dma(reason="gains as columns"):
                    n_g = 0

                    def gain(dst, src):
                        sp.dma_start(dst, src).then_inc(gains_in, 16)

                    gain(gcol[:, 0:KD], at(t["norm_mix"].rearrange("l (k p) -> l p k", p=P), layer))
                    for c, name in enumerate(("gq_a", "gk_a", "gq_b", "gk_b")):
                        for half in range(2):
                            gain(ghead[half * HD:(half + 1) * HD, c:c + 1],
                                 at(t[name].rearrange("l (p o) -> l p o", o=1), layer))
                    for c, name in enumerate(("gq_c", "gk_c")):
                        full = t[name].rearrange("l (p o) -> l p o", o=1)
                        gain(ghead[0:NOPE, 4 + c:5 + c], at(full, layer)[0:NOPE])
                        gain(grope[:, c, :], t[name][bass.ds(layer, 1), NOPE:QH].broadcast_to([P, ROPE]))
                    gain(gc[:, 0:2], at(t["norm_cq"].rearrange("l (k p) -> l p k", p=P), layer))
                    gain(gc[:, 2:3], at(t["norm_ckv"].rearrange("l (k p) -> l p k", p=P), layer))
                    gain(bfg[:], t["b_forget"][bass.ds(layer, 1), :].broadcast_to([P, H]))
                    gain(bro[:, 0:NG], t["b_router_group"][bass.ds(layer, 1), :].broadcast_to([P, NG]))
                    gain(bro[:, NG:], t["b_router_expert"][bass.ds(layer, 1), :].broadcast_to([P, NE]))
                    gain(wr[:, :, 0:NG], at(t["w_router_group"].rearrange("l (k p) g -> l p k g", p=P), layer))
                    gain(wr[:, :, NG:], at(t["w_router_expert"].rearrange("l (k p) g -> l p k g", p=P), layer))
                for h in range(H):
                    sp.dma_start(bias_a[:, h, :], skew(bias_dram, h)).then_inc(bias_in, 16)
                for i in range(RAW, NP_):
                    if i == END[GID["branch", 3]] + RAW:
                        multiplied(sp, END[GID["branch", 3]])
                        for n in range(NT):
                            sp.dma_start(x_rows[:, n, :],
                                         t["out"].rearrange("b (n p) d -> (b n) p d", p=P)[n]).then_inc(x_again, 16)
                    load_piece(i)
                    if i == OUT0:
                        sp.wait_ge(pv_done, len(UNITS))
                        sp.dma_start(grow, t["norm_ffn"][bass.ds(layer, 1), :].broadcast_to([P, D]))\
                            .then_inc(experts_const, 16)
                        sp.dma_start(tri2, t["tri"][:, 0:2 * P]).then_inc(experts_const, 16)
                        sp.wait_ge(table_zero, 1)
                        sp.dma_start(tok_tab.rearrange("(p c) o -> p (c o)", c=NCH), zero_i[:]).then_inc(tab_zeroed, 16)
                for j in range(4):
                    load_gate_up(sp, layer * NE, j, pair_in[j])
                for c in range(2):
                    load_down(sp, layer * NE, c, pair_in[4 + c])
                for n in range(NT):
                    sp.wait_ge(rows_ready, NT * 2 + n + 1)
                    sp.dma_start(xn_dram.rearrange("(n p) d -> n p d", p=P)[n], rows[:, n, :]).then_inc(xn_out, 16)
                experts_sp(sp, layer)
                for n in range(NT):
                    sp.wait_ge(x_done, n + 1)
                    sp.dma_start(t["out"].rearrange("b (n p) d -> (b n) p d", p=P)[n], x_rows[:, n, :])\
                        .then_inc(x_out, 16)
                sp.wait_ge(x_out, 16 * NT)
                layer_end(sp, layer)

        @block.tensor
        def _(pe):
            pe.wait_ge(const_in, 16 * N_CONST)
            pe.wait_ge(sel_in, 16)
            pe.wait_ge(set_ready, 2)
            for c in range(2):
                half = BIAS_LEN // 2
                pe.matmul(acc[c][0:H, 0:half], relb[:], hot[:, c * half:(c + 1) * half],
                          start=True, stop=True).then_inc(bias_mm, 1)

            def wide_turn(w):
                for kt in range(KD):
                    n = KD * w + kt
                    if kt == 0:
                        pe.wait_ge(rows_ready, NT * (w + 1))
                        if w:
                            sums_read(pe, GID["out", 0] - 1 if w == 1 else GID["out", 1], NT - 1)
                    if kt >= 4:
                        pe.wait_ge(wide_lo, n - 3)
                    for n_t in range(NT):
                        mm = pe.transpose(acc[kt % 4][:, n_t * P:(n_t + 1) * P],
                                          rows[:, n_t, kt * P:(kt + 1) * P], ident[:])
                    mm.then_inc(wide_done, 1)

            def piece(s, toks):
                g, k = PIECES[s]
                name, idx, nk, width = GROUPS[g]
                if toks[0] == 0:
                    pe.wait_ge(lo_ready, s + 1)
                if k == 0 and toks[0] == 0:
                    if name == "uq":
                        pe.wait_ge(turn_read, TURN["C", 1] + 1)
                    if name == "ukv":
                        pe.wait_ge(turn_read, TURN["C", 2] + 1)
                    if name == "branch":
                        pe.wait_ge(turn_read, TURN["O", idx // 2, NT - 1] + 1)
                    if g == 0:
                        pe.wait_ge(wide_lo, KD)
                    if name == "out" and idx == 0:
                        pe.wait_ge(wide_lo, 2 * KD)
                for n in toks:
                    if k == 0 and g > 0:
                        sums_read(pe, g - 1, n)
                    ts = slice(n * P, (n + 1) * P)
                    if name == "uq":
                        lhs = cT[k][:, 0, ts], cT[k][:, 1, ts]
                    elif name == "ukv":
                        lhs = cT[2][:, 0, ts], cT[2][:, 1, ts]
                    elif name == "branch":
                        o = (oT0, oT1, oT0)[idx // 2]
                        lhs = o[:, 0, k, ts], o[:, 1, k, ts]
                    else:
                        lhs = xT[:, 0, k, ts], xT[:, 1, k, ts]
                    mm = passes(acc[n][:, 0:width], lhs, (wh[:, s % HL, 0:width], wl[:, s % HL, 0:width]),
                                k == 0, k == nk - 1)
                    if k == nk - 1:
                        mm.then_inc(acc_done, 1)
                if toks[-1] == NT - 1 and k < nk - 1:
                    mm.then_inc(piece_used, 1)

            def scores(i):
                b, qt, h = UNITS[i]
                w = P * (qt + 1)
                out = sc_bank[i % 2][:, 0:w]
                if i >= 2:
                    pe.wait_ge(shifted, i - 1)
                qs = slice(qt * P, (qt + 1) * P)
                if b < 2:
                    q, k = (qT_a, kT_a) if b == 0 else (qT_b, kT_b)
                    r = slice((h % 2) * HD, (h % 2 + 1) * HD)
                    if (qt, h) == (0, 0):
                        pe.wait_ge(turn_read, TURN["Q", 2 * b + 1, NT - 1] + 1)
                        if b == 1:
                            pe.wait_ge(cum_split, 1)
                    if b == 1:
                        pe.matmul(out, sel[:, h, :], cum_p[:, 0:w], start=True, stop=False)
                    pe.matmul(out, q[r, h // 2, qs], k[r, h // 2, 0:w], start=(b == 0), stop=True)\
                        .then_inc(scores_done, 1)
                else:
                    if (qt, h) == (0, 0):
                        pe.wait_ge(turn_read, TURN["Q", 7, NT - 1] + 1)
                    pe.matmul(out, q_c[0:QH, h, qs], kT_c[0:QH, h, 0:w], start=True, stop=True)\
                        .then_inc(scores_done, 1)

            def turn_probs(i):
                b, qt, h = UNITS[i]
                n = TURN["P", i]
                pe.wait_ge(probs_ready, i + 1)
                if n:
                    pe.wait_ge(turn_read, n)
                for kt in range(qt + 1):
                    mm = pe.transpose(turn[:, kt * P:(kt + 1) * P], prob[:, i % 2, kt * P:(kt + 1) * P], ident[:])
                mm.then_inc(turn_done, 1)

            def weighted(i):
                b, qt, h = UNITS[i]
                v = (v_a, v_b, v_c)[b]
                if (qt, h) == (0, 0):
                    pe.wait_ge(v_copied, (4, 8, 16)[b])
                if h == 0 and i:
                    pe.wait_ge(o_ready, i // H)
                pe.wait_ge(turn_read, TURN["P", i] + 1)
                for kt in range(qt + 1):
                    mm = pe.matmul(o_bank[:, h * HD:(h + 1) * HD], probT[:, kt * P:(kt + 1) * P],
                                   v[:, kt, h * HD:(h + 1) * HD], start=(kt == 0), stop=(kt == qt))
                mm.then_inc(pv_done, 1)

            def other_turn(key):
                n = TURN[key]
                if n:
                    pe.wait_ge(turn_read, n)
                if key[0] == "cum":
                    pe.wait_ge(fz_dve, 6)
                    for n_t in range(NT):
                        mm = pe.matmul(turn[0:96, n_t * P:SEQ], lf96[:, n_t, :], tri[:, 0:SEQ - n_t * P],
                                       start=(n_t == 0), stop=(n_t == NT - 1))
                elif key[0] == "C":
                    c0 = H + key[1] * P
                    pe.wait_ge(c_ready, 1)
                    for n_t in range(NT):
                        mm = pe.transpose(turn[:, n_t * P:(n_t + 1) * P], small[:, n_t, c0:c0 + P], ident[:])
                elif key[0] == "O":
                    pe.wait_ge(o_ready, NT * key[1] + key[2] + 1)
                    for c in range(4):
                        mm = pe.transpose(turn[:, c * P:(c + 1) * P], o_rows[:, c * P:(c + 1) * P], ident[:])
                else:
                    _, j, n_t = key
                    pe.wait_ge(post_done, j + 1)
                    for c in range(4):
                        if j < 4:
                            mm = pe.transpose(turn[:, c * P:(c + 1) * P],
                                              head_rows[j % 2][:, n_t, c * P:(c + 1) * P], ident[:])
                        else:
                            mm = pe.transpose(turn[0:QH, c * P:(c + 1) * P],
                                              head_rows[j % 2][:, n_t, c * QH:(c + 1) * QH], ident[:])
                mm.then_inc(turn_done, 1)

            with pe.Fori(0, DEPTH) as layer:
                wide_turn(0)
                for s in range(NP_):
                    if s == OUT0:
                        wide_turn(1)
                    for n_s, (new, old, toks) in enumerate(steps_of(s)):
                        if new is not None:
                            scores(new)
                        if old is not None:
                            turn_probs(old)
                        if toks[-1] == NT - 1:
                            for key in turns_of(s):
                                other_turn(key)
                        piece(s, toks)
                        if old is not None:
                            weighted(old)
                wide_turn(2)
                pe.wait_ge(wide_lo, 3 * KD)
                pe.wait_ge(wr_split, 2)
                for n in range(NT):
                    for k in range(KD):
                        ts = slice(n * P, (n + 1) * P)
                        mm = passes(sc_bank[0][:, n * 32:n * 32 + NG + NE], (xT[:, 0, k, ts], xT[:, 1, k, ts]),
                                    (wrh[:, k, :], wrl[:, k, :]), k == 0, k == KD - 1)
                mm.then_inc(router_done, 1)
                experts_pe(pe)
                layer_end(pe, layer)

        @block.scalar
        def _(act):
            act.wait_ge(bias_mm, 2)
            half = BIAS_LEN // 2
            for c in range(2):
                act.activation(biasT[:, c * half:(c + 1) * half], acc[c][0:H, 0:half], ACT.Copy).then_inc(bias_sb, 1)
            act.wait_ge(const_in, 16 * N_CONST)
            act.dma_start(yslots[:, NE:, :].rearrange("p c (k q) -> p (c k) q", q=P),
                          ident[:].unsqueeze(1).broadcast_to([P, (NCH - NE) * D // P, P])).then_inc(slots_set, 16)
            act.wait_ge(rope_ready, 1)
            act.activation(sinT[:], rope_t[:, 0, 0:NT * HALF].rearrange("p (n f) -> p n f", n=NT), ACT.Sin)\
                .then_inc(rope_steps, 1)
            act.activation(cosT[:], rope_t[:, 1, 0:NT * HALF].rearrange("p (n f) -> p n f", n=NT), ACT.Sin)\
                .then_inc(rope_steps, 1)

            def square_rows(w):
                for n in range(NT):
                    if n == 0 and w == 0:
                        act.wait_ge(x_in, 16 * NT)
                    if w == 1:
                        sums_read(act, GID["out", 1], n)
                        act.wait_ge(wide_done, 2 * KD)
                    act.activation(rows[:, n, :], x_rows[:, n, :], ACT.Square, accum_out=ssx[:, n:n + 1])\
                        .then_inc(sum_ready, 1)

            def wide_hi_of(w):
                for kt in range(KD):
                    act.wait_ge(wide_done, KD * w + kt + 1)
                    if w == 0 and kt == 0:
                        act.wait_ge(gains_in, 16 * N_GAINS)
                    if kt == 0 and w:
                        multiplied(act, (OUT0 if w == 1 else NP_) - 1)
                    scale = (gcol[:, kt:kt + 1], 0.5, 1.0)[w]
                    act.activation(xT[:, 0, kt, :], acc[kt % 4][:], ACT.Copy, scale=scale).then_inc(wide_hi, 1)

            def expo(i):
                b, qt, h = UNITS[i]
                w = P * (qt + 1)
                act.wait_ge(shifted, i + 1)
                if h == 0 and i >= 2 * H:
                    act.wait_ge(o_ready, i // H - 1)
                act.activation(prob[:, i % 2, 0:w], prob[:, i % 2, 0:w], ACT.Exp, scale=-1.0,
                               bias=nmax[:, i % 2:i % 2 + 1],
                               accum_out=den[:, (i // H) % 2, h:h + 1]).then_inc(probs_ready, 1)

            def turned(key):
                n = TURN[key]
                act.wait_ge(turn_done, n + 1)
                if key[0] == "P":
                    w = P * (UNITS[key[1]][1] + 1)
                    if key[1]:
                        act.wait_ge(pv_done, key[1])
                    act.activation(probT[:, 0:w], turn[:, 0:w], ACT.Copy).then_inc(turn_read, 1)
                elif key[0] == "cum":
                    act.activation(cum[:], turn[0:96, :], ACT.Copy).then_inc(turn_read, 1)
                elif key[0] == "C":
                    act.wait_ge(rows_ready, NT)
                    act.activation(cT[key[1]][:, 0, :], turn[:], ACT.Copy, scale=gc[:, key[1]:key[1] + 1])\
                        .then_inc(turn_hi, 1)
                elif key[0] == "O":
                    _, b, qt = key
                    o = (oT0, oT1, oT0)[b]
                    if b == 2 and qt == 0:
                        multiplied(act, END[GID["branch", 1]])
                    if b == 1 and qt == 0:
                        multiplied(act, END[GID["uq", 1]])
                    act.activation(o[:, 0, :, qt * P:(qt + 1) * P],
                                   turn[:].rearrange("p (c s) -> p c s", c=4), ACT.Copy).then_inc(turn_hi, 1)
                else:
                    _, j, n_t = key
                    ts = slice(n_t * P, (n_t + 1) * P)
                    if j < 4:
                        dst = (qT_a, kT_a, qT_b, kT_b)[j][:, :, ts]
                        act.activation(dst, turn[:].rearrange("p (c s) -> p c s", c=4), ACT.Copy,
                                       scale=ghead[:, j:j + 1]).then_inc(turn_read, 1)
                    else:
                        a_done = 4 * H * 1
                        if n_t == 0:
                            act.wait_ge(pv_done, a_done)
                        full = q_c if j < 6 else kT_c
                        dst = full[0:QH, 4 * (j % 2):4 * (j % 2) + 4, ts]
                        act.activation(dst, turn[0:QH, :].rearrange("p (c s) -> p c s", c=4), ACT.Copy,
                                       scale=ghead[0:QH, 4 + (j - 4) // 2:5 + (j - 4) // 2]).then_inc(turn_read, 1)

            def squares_of(j):
                width = (512, 4 * QH, 512)[(j - 2) // 2 if j >= 4 else 0]
                for n in range(NT):
                    m = 4 * j + n
                    act.wait_ge(rows_copied, m + 1)
                    if m >= 2:
                        act.wait_ge(sq_summed, m - 1)
                    if m == 8:
                        act.wait_ge(cum_split, 1)
                    act.activation(squares[:, m % 2, 0:width], head_rows[j % 2][:, n, 0:width], ACT.Square)\
                        .then_inc(sq_ready, 1)
                if j >= 6:
                    if j == 6:
                        act.wait_ge(pv_done, 4 * H)
                    for n in range(NT):
                        act.activation(v_c[:, n, 256 * (j - 6):256 * (j - 5)].rearrange("p (h c) -> p h c", h=4),
                                       head_rows[j % 2][:, n, :].rearrange("p (h c) -> p h c", h=4)[:, :, NOPE:],
                                       ACT.Copy).then_inc(v_copied, 1)

            with act.Fori(0, DEPTH) as layer:
                square_rows(0)
                wide_hi_of(0)
                for i in range(LEAD):
                    split_hi(i, width_of(i))
                for s in range(NP_):
                    if s == OUT0:
                        wide_hi_of(1)
                    for new, old, toks in steps_of(s):
                        if old is not None:
                            turned(("P", old))
                        if new is not None:
                            expo(new)
                    for key in turns_of(s):
                        turned(key)
                    if s + LEAD < NP_:
                        split_hi(s + LEAD, width_of(s + LEAD))
                    if s:
                        g = PIECES[s - 1][0]
                        if END[g] == s - 1 and GROUPS[g][0] == "gate":
                            for n in range(NT):
                                act.wait_ge(acc_done, 4 * g + n + 1)
                                if GROUPS[g][1]:
                                    act.wait_ge(branch_ready, 4 * (GROUPS[g][1] - 1) + n + 1)
                                act.activation(gate_t[:, n, :], acc[n][:], ACT.Tanh, scale=0.5).then_inc(gate_read, 1)
                    for g, j in POST_AT.items():
                        if s == END[g] + 2:
                            squares_of(j)
                    if s == SMALL_END + 2:
                        act.wait_ge(small_copied, NT)
                        act.wait_ge(sq_summed, 8)
                        for c, (c0, c1) in enumerate(((H, H + Q_LORA), (H + Q_LORA, H + Q_LORA + KV_LORA),
                                                      (H + Q_LORA + KV_LORA, N_SMALL))):
                            for n in range(NT):
                                m = NT * c + n
                                if m >= 4:
                                    act.wait_ge(csq_ready, m - 3)
                                act.activation(squares[:, (m % 4) // 2, 256 * (m % 2):256 * (m % 2) + c1 - c0], small[:, n, c0:c1], ACT.Square,
                                               accum_out=ssc[:, c, n:n + 1]).then_inc(csq_ready, 1)
                        act.wait_ge(fz_dve, 2)
                        act.activation(fz[:, 2, :], fz[:, 1, :], ACT.Exp, scale=-1.0).then_inc(fz_act, 1)
                        act.wait_ge(fz_act, 1)
                        act.activation(fz[:, 3, :], fz[:, 2, :], ACT.Ln, bias=1.0).then_inc(fz_act, 1)
                square_rows(1)
                wide_hi_of(2)
                act.wait_ge(gains_in, 16 * N_GAINS)
                act.activation(wrh[:], wr[:], ACT.Copy).then_inc(wr_split, 1)
                act.wait_ge(r_dve, 3)
                act.activation(r4[:, 1], r4[:, 0], ACT.Exp).then_inc(r_act, 1)
                act.wait_ge(router_done, 1)
                pair_hi(-1, 0)
                act.wait_ge(r_pair, 1)
                act.activation(r1[:, 5, :], r1[:, 4, :], ACT.Exp).then_inc(r_act, 1)
                pair_hi(-1, 1)
                experts_act(act)
                layer_end(act, layer)


        @block.vector
        def _(dve):
            nc.vector.memset(relb[:], 1.0).then_inc(set_ready, 1)
            nc.vector.memset(ghead[:], 1.0).then_inc(set_ready, 1)
            dve.wait_ge(const_in, 16 * N_CONST)
            nc.vector.tensor_copy(pos_f[:], pos_i[:]).then_inc(dve_c, 1)
            ang, turns, r = (rope_t[:, c, 0:NT * HALF] for c in (0, 1, 2))
            v3 = lambda a: a.rearrange("p (n f) -> p n f", n=NT)
            dve.wait_ge(dve_c, 1)
            nc.vector.tensor_tensor(v3(ang), pos_f[:].unsqueeze(2).broadcast_to([P, NT, HALF]),
                                    freq[:].unsqueeze(1).broadcast_to([P, NT, HALF]), ALU.mult).then_inc(dve_c, 1)
            dve.wait_ge(dve_c, 2)
            ROUND = 1.5 * 2.0 ** 23
            nc.vector.tensor_scalar(turns, ang, 1.0 / (2 * math.pi), ROUND, ALU.mult, ALU.add).then_inc(dve_c, 1)
            dve.wait_ge(dve_c, 3)
            nc.vector.tensor_scalar(turns, turns, ROUND, None, ALU.subtract).then_inc(dve_c, 1)
            dve.wait_ge(dve_c, 4)
            parts = (6.28125, 0.0019350051879882812, 2 * math.pi - 6.28125 - 0.0019350051879882812)
            c = 4
            src = ang
            for part in parts:
                nc.vector.scalar_tensor_tensor(out=r, in0=turns, scalar=-part, in1=src, op0=ALU.mult,
                                               op1=ALU.add).then_inc(dve_c, 1)
                c += 1
                dve.wait_ge(dve_c, c)
                src = r
            LIM = 3.1415925
            nc.vector.tensor_scalar(ang, r, LIM, -LIM, ALU.min, ALU.max).then_inc(dve_c, 1)
            dve.wait_ge(dve_c, c + 1)
            nc.vector.scalar_tensor_tensor(out=r, in0=ang, scalar=-1.0, in1=ang, op0=ALU.mult, op1=ALU.min)\
                .then_inc(dve_c, 1)
            dve.wait_ge(dve_c, c + 2)
            nc.vector.tensor_scalar(turns, r, math.pi / 2, None, ALU.add).then_inc(rope_ready, 1)

            def scaled_rows(w):
                for n in range(NT):
                    if n == 0:
                        dve.wait_ge(scale_ready, 1 + w)
                        if w:
                            dve.wait_ge(experts_const, 32)
                    if w == 0:
                        nc.vector.tensor_scalar(rows[:, n, :], x_rows[:, n, :], rsx[:, n:n + 1], None, ALU.mult)\
                            .then_inc(rows_ready, 1)
                    else:
                        nc.vector.scalar_tensor_tensor(out=rows[:, n, :], in0=x_rows[:, n, :], scalar=rsx[:, n:n + 1],
                                                       in1=grow, op0=ALU.mult, op1=ALU.mult).then_inc(rows_ready, 1)

            def wide_lo_of(w):
                for kt in range(KD):
                    dve.wait_ge(wide_hi, KD * w + kt + 1)
                    hi = xT[:, 0, kt, :].bitcast(F32)
                    scale = (gcol[:, kt:kt + 1], 0.5, 1.0)[w]
                    nc.vector.scalar_tensor_tensor(out=xT[:, 1, kt, :], in0=acc[kt % 4][:], scalar=scale, in1=hi,
                                                   op0=ALU.mult, op1=ALU.subtract).then_inc(wide_lo, 1)

            def shift(i):
                b, qt, h = UNITS[i]
                w = P * (qt + 1)
                dve.wait_ge(scores_done, i + 1)
                if i == 0:
                    dve.wait_ge(bias_in, 16 * H)
                if i >= 2:
                    dve.wait_ge(turn_done, TURN["P", i - 2] + 1)
                add = bias_a[:, h, SEQ - w:] if b == 0 else mask[:, SEQ - w:]
                nc.vector.tensor_tensor_reduce(prob[:, i % 2, 0:w], sc_bank[i % 2][:, 0:w], add, -SOFT[b], 3.0e38,
                                               ALU.add, ALU.min, nmax[:, i % 2:i % 2 + 1]).then_inc(shifted, 1)

            def normalise(i):
                q = i // H
                dve.wait_ge(probs_ready, i + 1)
                if q:
                    b, qt, _ = UNITS[i - H]
                    dve.wait_ge(turn_done, TURN["O", b, qt] + 1)
                nc.vector.reciprocal(rden[:], den[:, q % 2, :]).then_inc(dve_own, 1)
                dve.wait_ge(pv_done, i + 1)
                dve.wait_ge(dve_own, q + 1)
                nc.vector.tensor_tensor(o_rows[:].rearrange("p (h c) -> p h c", h=H),
                                        o_bank[:].rearrange("p (h c) -> p h c", h=H),
                                        rden[:].unsqueeze(2).broadcast_to([P, H, HD]), ALU.mult).then_inc(o_ready, 1)

            def turned_lo(key):
                dve.wait_ge(turn_hi, LO_TURN[key] + 1)
                if key[0] == "C":
                    k = key[1]
                    nc.vector.scalar_tensor_tensor(out=cT[k][:, 1, :], in0=turn[:], scalar=gc[:, k:k + 1],
                                                   in1=cT[k][:, 0, :].bitcast(F32), op0=ALU.mult,
                                                   op1=ALU.subtract).then_inc(turn_read, 1)
                else:
                    _, b, qt = key
                    o = (oT0, oT1, oT0)[b]
                    qs = slice(qt * P, (qt + 1) * P)
                    nc.vector.tensor_tensor(o[:, 1, :, qs], turn[:].rearrange("p (c s) -> p c s", c=4),
                                            o[:, 0, :, qs].bitcast(F32), ALU.subtract).then_inc(turn_read, 1)

            def read_group(g, n):
                name, idx, _, width = GROUPS[g]
                dve.wait_ge(acc_done, 4 * g + n + 1)
                src = acc[n][:, 0:width]
                if g in POST_AT:
                    j = POST_AT[g]
                    if j >= 2 and n == 0:
                        dve.wait_ge(turn_done, TURN["Q", j - 2, NT - 1] + 1)
                    if j >= 2 and n == 0 and j - 2 >= 6:
                        dve.wait_ge(v_copied, 16)
                    if j == 0 and n == 0:
                        dve.wait_ge(wide_done, KD)
                    nc.vector.tensor_copy(head_rows[j % 2][:, n, 0:width], src).then_inc(acc_read, 1)
                elif name == "v":
                    v = (v_a, v_b)[idx]
                    nc.vector.tensor_copy(v[:, n, :], src).then_inc(acc_read, 1)
                elif name == "small":
                    nc.vector.tensor_copy(small[:, n, :], src).then_inc(acc_read, 1)
                elif name == "branch":
                    b, c = idx // 2, idx % 2
                    cs = slice(512 * c, 512 * (c + 1))
                    if n == 0 and b == 0 and c == 0:
                        dve.wait_ge(turn_done, TURN["C", 2] + 1)
                        dve.wait_ge(post_done, 3)
                    if n == 0 and b == 0 and c == 1:
                        dve.wait_ge(turn_done, TURN["Q", 6, NT - 1] + 1)
                    if b == 0:
                        nc.vector.scalar_tensor_tensor(out=rows[:, n, cs], in0=gate_t[:, n, :], scalar=1.0, in1=src,
                                                       op0=ALU.add, op1=ALU.mult).then_inc(acc_read, 1)
                    else:
                        m = 4 * (idx - 2) + n
                        nc.vector.scalar_tensor_tensor(out=gate_t[:, n, :], in0=gate_t[:, n, :], scalar=1.0,
                                                       in1=src, op0=ALU.add, op1=ALU.mult).then_inc(acc_read, 1)
                        sums_read(dve, g, n)
                        nc.vector.tensor_tensor(rows[:, n, cs], rows[:, n, cs], gate_t[:, n, :], ALU.add)\
                            .then_inc(merged, 1)
                else:
                    cs = slice(512 * idx, 512 * (idx + 1))
                    if n == 0 and idx == 0:
                        dve.wait_ge(x_again, 16 * NT)
                    nc.vector.tensor_tensor(x_rows[:, n, cs], x_rows[:, n, cs], src, ALU.add).then_inc(acc_read, 1)

            def after_read(g, n):
                name, idx, _, _ = GROUPS[g]
                if name not in ("qk", "uq", "ukv", "v", "small", "branch"):
                    return
                if name == "branch" and idx >= 2:
                    dve.wait_ge(merged, 4 * (idx - 2) + n + 1)
                sums_read(dve, g, n)
                s_ = {"v": v_copied, "small": small_copied, "branch": branch_ready}.get(name, rows_copied)
                dve.sem_inc(s_, 1)

            def sums_of(j):
                name = POSTS[j][0]
                for n in range(NT):
                    m = 4 * j + n
                    dve.wait_ge(sq_ready, m + 1)
                    if n == 0 and j:
                        dve.wait_ge(post_done, j)
                    sq = squares[:, m % 2, :]
                    if name == "qk":
                        nc.vector.tensor_reduce(ssq[:, n, :], sq.rearrange("p (h c) -> p h c", h=H), AX_X, ALU.add)\
                            .then_inc(sq_summed, 1)
                    elif name == "uq":
                        v = sq[:, 0:4 * QH].rearrange("p (h c) -> p h c", h=4)
                        nc.vector.tensor_reduce(ssq[:, n, 0:4], v[:, :, 0:NOPE], AX_X, ALU.add)
                        nc.vector.tensor_reduce(ssq[:, n, 4:8], v[:, :, NOPE:], AX_X, ALU.add).then_inc(sq_summed, 1)
                    else:
                        v = sq.rearrange("p (h c) -> p h c", h=4)
                        nc.vector.tensor_reduce(ssq[:, n, 0:4], v[:, :, 0:NOPE], AX_X, ALU.add).then_inc(sq_summed, 1)

            with dve.Fori(0, DEPTH) as layer:
                scaled_rows(0)
                wide_lo_of(0)
                for i in range(LEAD):
                    split_lo(i, width_of(i))
                for s in range(NP_):
                    if s == OUT0:
                        for n in range(NT):
                            read_group(PIECES[s - 1][0], n)
                        dve.wait_ge(merged, 16)
                        for n in range(NT):
                            dve.sem_inc(rows_ready, 1)
                        wide_lo_of(1)
                    g = PIECES[s - 1][0] if s else None
                    ended = s and s != OUT0 and END[g] == s - 1 and GROUPS[g][0] != "gate"
                    steps = steps_of(s)
                    for n_s, (new, old, toks) in enumerate(steps):
                        half = toks[:len(toks) // 2] if len(toks) == 4 else toks[:1]
                        rest = toks[len(half):]
                        if ended:
                            for n in half:
                                read_group(g, n)
                        if new is not None:
                            shift(new)
                        if ended:
                            for n in rest:
                                read_group(g, n)
                            for n in toks:
                                after_read(g, n)
                        if len(steps) == 2 and old is not None and UNITS[old][2] == H - 1:
                            normalise(old)
                    for _, old, _ in (steps_of(s - 1) if s else []):
                        if len(steps_of(s - 1)) == 1 and old is not None and UNITS[old][2] == H - 1:
                            normalise(old)
                    for key in turns_of(s):
                        if key in LO_TURN:
                            turned_lo(key)
                    if s + LEAD < NP_:
                        split_lo(s + LEAD, width_of(s + LEAD))
                    for gg, j in POST_AT.items():
                        if s == END[gg] + 2:
                            sums_of(j)
                    if s == SMALL_END + 2:
                        z, a, ln = fz[:, 0, :], fz[:, 1, :], fz[:, 3, :]
                        hf = lambda q: q.rearrange("p (n h) -> p n h", n=NT)
                        nc.vector.tensor_tensor(hf(z), small[:, :, 0:H],
                                                bfg[:].unsqueeze(1).broadcast_to([P, NT, H]), ALU.add)\
                            .then_inc(fz_dve, 1)
                        dve.wait_ge(fz_dve, 1)
                        nc.vector.scalar_tensor_tensor(out=a, in0=z, scalar=-1.0, in1=z, op0=ALU.mult,
                                                       op1=ALU.max).then_inc(fz_dve, 1)
                        dve.wait_ge(fz_act, 2)
                        nc.vector.scalar_tensor_tensor(out=a, in0=z, scalar=0.0, in1=ln, op0=ALU.min,
                                                       op1=ALU.subtract).then_inc(fz_dve, 1)
                        dve.wait_ge(fz_dve, 3)
                        nc.vector.memset(lf96, 0.0).then_inc(csum_ready, 1)
                        dve.wait_ge(csum_ready, 1)
                        for c in range(3):
                            nc.vector.tensor_copy(lf96[:, :, 32 * c:32 * c + H], hf(a)).then_inc(fz_dve, 1)
                    if s == SMALL_END + 9:
                        dve.wait_ge(turn_read, TURN["cum",] + 1)
                        chain = (lambda ins, c=[0]: (ins.then_inc(post_aux, 1), c.__setitem__(0, c[0] + 1),
                                                     dve.wait_ge(post_aux, c[0])))
                        chain(nc.vector.tensor_copy(cum_b[:], cum[:]))
                        nc.vector.tensor_copy(cum_p[0:32, :], cum_b[0:32, :])
                        chain(nc.vector.tensor_tensor(cum[:], cum[:], cum_b[:], ALU.subtract))
                        chain(nc.vector.tensor_copy(cum_b[:], cum[:]))
                        nc.vector.tensor_copy(cum_p[32:64, :], cum_b[32:64, :])
                        chain(nc.vector.tensor_tensor(cum[:], cum[:], cum_b[:], ALU.subtract))
                        nc.vector.tensor_copy(cum_p[64:96, :], cum[64:96, :]).then_inc(cum_split, 1)
                g = len(GROUPS) - 1
                for n in range(NT):
                    read_group(g, n)
                scaled_rows(1)
                wide_lo_of(2)
                dve.wait_ge(wr_split, 1)
                nc.vector.tensor_tensor(wrl[:], wr[:], wrh[:].bitcast(F32), ALU.subtract).then_inc(wr_split, 1)
                route(dve)
                experts_dve(dve)
                layer_end(dve, layer)

        @block.gpsimd
        def _(pool):
            nc.gpsimd.memset(pw[:], -0.5).then_inc(pool_c, 1)
            nc.gpsimd.memset(zero_i[:], 0).then_inc(table_zero, 1)
            pool.dma_start(sel[:].rearrange("p h q -> p (h q)"), t["sel"]).then_inc(sel_in, 16)
            pool.wait_ge(pool_c, 1)
            pool.wait_ge(rope_steps, 2)
            with pool.Fori(0, DEPTH) as layer:
                own = [0]

                def step(ins):
                    ins.then_inc(pool_own, 1)
                    own[0] += 1
                    pool.wait_ge(pool_own, own[0])

                def rsqrt(dst, src, n, divisor):
                    step(nc.gpsimd.tensor_scalar(src, src, 1.0 / divisor, EPS, ALU.mult, ALU.add))
                    return nc.gpsimd.tensor_tensor(dst, src, pw[:, 0:n], ALU.pow)

                def heads_normed(j):
                    name, idx = POSTS[j]
                    pool.wait_ge(sq_summed, 4 * j + 4)
                    buf = head_rows[j % 2]
                    if name == "qk":
                        step(rsqrt(rsq[:].rearrange("p n h -> p (n h)"), ssq[:].rearrange("p n h -> p (n h)"), 32, HD))
                        for n in range(NT):
                            v = buf[:, n, :].rearrange("p (h c) -> p h c", h=H)
                            ins = nc.gpsimd.tensor_tensor(v, v, rsq[:, n, :].unsqueeze(2).broadcast_to([P, H, HD]),
                                                          ALU.mult)
                        ins.then_inc(post_done, 1)
                        return
                    pw4 = pw[:, 0:16].rearrange("p (n h) -> p n h", n=NT)
                    step(nc.gpsimd.tensor_scalar(ssq[:, :, 0:4], ssq[:, :, 0:4], 1.0 / NOPE, EPS, ALU.mult, ALU.add))
                    step(nc.gpsimd.tensor_tensor(rsq[:, :, 0:4], ssq[:, :, 0:4], pw4, ALU.pow))
                    if name == "uq":
                        step(nc.gpsimd.tensor_scalar(ssq[:, :, 4:8], ssq[:, :, 4:8], 1.0 / ROPE, EPS, ALU.mult, ALU.add))
                        step(nc.gpsimd.tensor_tensor(rsq[:, :, 4:8], ssq[:, :, 4:8], pw4, ALU.pow))
                        for n in range(NT):
                            v = buf[:, n, 0:4 * QH].rearrange("p (h c) -> p h c", h=4)
                            nc.gpsimd.tensor_tensor(v[:, :, 0:NOPE], v[:, :, 0:NOPE],
                                                    rsq[:, n, 0:4].unsqueeze(2).broadcast_to([P, 4, NOPE]), ALU.mult)
                            step(nc.gpsimd.tensor_tensor(v[:, :, NOPE:], v[:, :, NOPE:],
                                                         rsq[:, n, 4:8].unsqueeze(2).broadcast_to([P, 4, ROPE]),
                                                         ALU.mult))
                            step(nc.gpsimd.tensor_tensor(v[:, :, NOPE:], v[:, :, NOPE:],
                                                         grope[:, 0, :].unsqueeze(1).broadcast_to([P, 4, ROPE]),
                                                         ALU.mult))
                            rotate(v[:, :, NOPE:NOPE + HALF], v[:, :, NOPE + HALF:], n, 4)
                        pool.sem_inc(post_done, 1)
                        return
                    if j == 6:
                        pool.wait_ge(v_copied, 12)
                    else:
                        pool.wait_ge(v_copied, 16)
                    for n in range(NT):
                        src = buf[:, n, :].rearrange("p (h c) -> p h c", h=4)
                        tmp = rope_t[:, 0:4, :].rearrange("p a b -> p (a b)")[:, 0:4 * NOPE]\
                            .rearrange("p (h c) -> p h c", h=4)
                        step(nc.gpsimd.tensor_tensor(tmp, src[:, :, 0:NOPE],
                                                     rsq[:, n, 0:4].unsqueeze(2).broadcast_to([P, 4, NOPE]), ALU.mult))
                        dst = buf[:, n, 0:4 * QH].rearrange("p (h c) -> p h c", h=4)
                        nc.gpsimd.tensor_copy(dst[:, :, 0:NOPE], tmp)
                        step(nc.gpsimd.tensor_copy(dst[:, :, NOPE:], kr[:, n, :].unsqueeze(1).broadcast_to([P, 4, ROPE])))
                    pool.sem_inc(post_done, 1)

                def rotate(x1, x2, n, heads):
                    shape = [P, heads, HALF]
                    c = cosT[:, n, :].unsqueeze(1).broadcast_to(shape)
                    s_ = sinT[:, n, :].unsqueeze(1).broadcast_to(shape)
                    m = [rope_t[:, q, 0:heads * HALF].rearrange("p (h f) -> p h f", h=heads) for q in range(4)]
                    tt = nc.gpsimd.tensor_tensor
                    tt(m[0], x1, c, ALU.mult)
                    tt(m[1], x2, s_, ALU.mult)
                    tt(m[2], x1, s_, ALU.mult)
                    step(tt(m[3], x2, c, ALU.mult))
                    tt(x1, m[0], m[1], ALU.subtract)
                    step(tt(x2, m[2], m[3], ALU.add))

                def row_scale(w):
                    pool.wait_ge(sum_ready, NT * (w + 1))
                    step(nc.gpsimd.tensor_scalar(ssx[:], ssx[:], 1.0 / D, EPS, ALU.mult, ALU.add))
                    nc.gpsimd.tensor_tensor(rsx[:], ssx[:], pw[:, 0:NT], ALU.pow).then_inc(scale_ready, 1)

                row_scale(0)
                heads_normed(0)
                heads_normed(1)
                pool.wait_ge(csq_ready, 3 * NT)
                for c, width in enumerate((Q_LORA, KV_LORA, ROPE)):
                    step(rsqrt(rsc[:, c, :], ssc[:, c, :], NT, width))
                for n in range(NT):
                    nc.gpsimd.tensor_scalar(small[:, n, H:H + Q_LORA], small[:, n, H:H + Q_LORA],
                                            rsc[:, 0, n:n + 1], None, ALU.mult)
                    ins = nc.gpsimd.tensor_scalar(small[:, n, H + Q_LORA:H + Q_LORA + KV_LORA],
                                                  small[:, n, H + Q_LORA:H + Q_LORA + KV_LORA],
                                                  rsc[:, 1, n:n + 1], None, ALU.mult)
                ins.then_inc(c_ready, 1)
                for n in range(NT):
                    step(nc.gpsimd.tensor_scalar(kr[:, n, :], small[:, n, N_SMALL - ROPE:], rsc[:, 2, n:n + 1],
                                                 None, ALU.mult))
                    step(nc.gpsimd.tensor_tensor(kr[:, n, :], kr[:, n, :], grope[:, 1, :], ALU.mult))
                    rotate(kr[:, n, 0:HALF].unsqueeze(1), kr[:, n, HALF:].unsqueeze(1), n, 1)
                for j in range(2, 8):
                    heads_normed(j)
                row_scale(1)
                experts_pool(pool)
                pool.wait_ge(arrived, 4 * layer + 4)
                pool.sem_inc(resumed, 1)
                pool.dma_reset(cleared)
                pool.sem_clear(cleared)
                pool.sem_inc(released, 1)



_INS = ["x", "positions", "rel_bias", "norm_mix", "w_in", "b_forget", "gq_a", "gk_a", "gq_b", "gk_b", "gq_c", "gk_c",
        "norm_cq", "norm_ckv", "w_uq", "w_ukv", "w_branch", "w_out", "norm_ffn", "w_router_group", "b_router_group",
        "w_router_expert", "b_router_expert", "w_expert_gate", "w_expert_up", "w_expert_down"]


def kernel(**inputs):
    import numpy as _np
    import concourse.bacc as _bacc
    from concourse import mybir as _mybir
    from concourse.bass_utils import run_bass_kernel_spmd as _run

    nc = _bacc.Bacc("TRN2", target_bir_lowering=False, num_devices=1)
    arrays, t = {}, {}
    given = {name: _np.ascontiguousarray(inputs[name]) for name in _INS}
    given.update(shape_constants())
    for name, a in given.items():
        arrays[f"in_{name}_dram"] = a
        t[name] = nc.dram_tensor(f"in_{name}_dram", a.shape, _mybir.dt.from_np(a.dtype), kind="ExternalInput").ap()
    t["out"] = nc.dram_tensor("out_0_dram", (1, SEQ, D), _mybir.dt.float32, kind="ExternalOutput").ap()
    build(nc, t)
    r = _run(nc, [arrays], core_ids=[0])
    return r.results[0]["out_0_dram"]
```

```python
from contextlib import ExitStack
import math

import numpy as np
import concourse.bass as bass
from concourse import mybir

F32 = mybir.dt.float32
F32R = mybir.dt.float32r
BF16 = mybir.dt.bfloat16
I32 = mybir.dt.int32
ALU = mybir.AluOpType
ACT = mybir.ActivationFunctionType
AX_X = mybir.AxisListType.X

P = 128
D = 1024
SEQ = 512
DEPTH = 2
KD = D // P
NT = SEQ // P
H = 8
HD = 64
BW = H * HD
NOPE, ROPE = 64, 32
QH = NOPE + ROPE
HALF = ROPE // 2
Q_LORA, KV_LORA = 256, 128
N_BUCKETS, MAX_DISTANCE = 32, 2048
DILATED_PAIRS = ((128, 1), (512, 4), (2048, 16))
NG, EG, NE, FF = 4, 4, 16, 256
EPS = 1e-6
MASKED = -1.0e30
COL_SMALL = 6 * BW
N_SMALL = H + Q_LORA + KV_LORA + ROPE
COL_GATE = COL_SMALL + N_SMALL
LEAD = 2
NCH = 23
RAW, HL = 4, 3
BIAS_LEN = SEQ + P


def shape_constants():
    i = np.arange(BIAS_LEN)
    dist = SEQ - 1 - i
    d0 = np.maximum(dist, 0)
    exact = N_BUCKETS // 2
    ratio = np.log(np.maximum(d0, exact) / exact) / np.log(MAX_DISTANCE / exact)
    large = np.minimum(exact + (ratio * (N_BUCKETS - exact)).astype(np.int32), N_BUCKETS - 1)
    bucket = np.where(d0 < exact, d0, large)
    count = sum(((dist % dil == 0) & (dist <= window)).astype(int) for window, dil in DILATED_PAIRS)
    count = np.where(dist >= 0, count, 0)
    scale = math.sqrt(HD)
    hot = np.zeros((N_BUCKETS + 1, BIAS_LEN), np.float32)
    hot[bucket, i] = np.where(count > 0, scale, 0.0)
    hot[N_BUCKETS] = np.where(count > 0, scale * np.log(np.maximum(count, 1)), MASKED)
    p, j = np.arange(P)[:, None], np.arange(SEQ)[None, :]
    tri = (j >= p).astype(np.float32)
    mask = np.where(j <= p + SEQ - P, 0.0, MASKED).astype(np.float32)
    sel = np.zeros((3 * 32, H, P), np.float32)
    for h in range(H):
        sel[[h, 32 + h, 64 + h], h] = -scale
    freq = np.broadcast_to(np.float32(10000.0) ** (-np.arange(HALF, dtype=np.float32) / HALF), (P, HALF))
    first = np.broadcast_to(np.arange(4, 0, -1, dtype=np.float32), (P, 4))
    return {"ident": np.eye(P, dtype=np.float32), "hot": hot, "tri": tri, "mask": mask,
            "sel": sel.reshape(96, H * P), "freq": np.ascontiguousarray(freq, np.float32),
            "first": np.ascontiguousarray(first),
            "erow": np.ascontiguousarray(np.broadcast_to(np.arange(NE, dtype=np.float32), (P, NE))),
            "tok_id": np.tile(np.arange(SEQ, dtype=np.float32).reshape(NT, P).T, (1, 2)),
            "iota": np.ascontiguousarray(np.broadcast_to(np.arange(P, dtype=np.float32), (P, P)))}


GROUPS = [("qk", 0, KD, BW), ("qk", 1, KD, BW), ("v", 0, KD, BW), ("small", 0, KD, N_SMALL),
          ("qk", 2, KD, BW), ("qk", 3, KD, BW), ("v", 1, KD, BW),
          ("uq", 0, 2, 4 * QH), ("uq", 1, 2, 4 * QH), ("gate", 0, KD, 512), ("branch", 0, 4, 512),
          ("ukv", 0, 1, 512), ("ukv", 1, 1, 512), ("gate", 1, KD, 512), ("branch", 1, 4, 512)]
for _b in (1, 2):
    for _c in (0, 1):
        GROUPS += [("gate", 2 * _b + _c, KD, 512), ("branch", 2 * _b + _c, 4, 512)]
GROUPS += [("out", 0, KD, 512), ("out", 1, KD, 512)]
PIECES = [(g, k) for g, grp in enumerate(GROUPS) for k in range(grp[2])]
NP_ = len(PIECES)
START = {g: min(s for s, pc in enumerate(PIECES) if pc[0] == g) for g in range(len(GROUPS))}
END = {g: START[g] + GROUPS[g][2] - 1 for g in START}
GID = {(n, i): g for g, (n, i, _, _) in enumerate(GROUPS)}
OUT0 = START[GID["out", 0]]
MERGED_TURN = {OUT0 - 2: range(0, KD // 2), OUT0 + 2: range(KD // 2, KD)}
UNITS = [(b, qt, h) for b in range(3) for qt in range(NT) for h in range(H)]
UNIT_SLOT = {}
_s = END[GID["v", 0]] + 1
for _i, (_b, _qt, _h) in enumerate(UNITS):
    UNIT_SLOT.setdefault(_s, []).append(_i)
    if not (_b > 0 and _qt == 0 and _h % 2 == 0):
        _s += 1
LAST_UNIT_SLOT = _s - 1
POSTS = [("qk", 0), ("qk", 1), ("qk", 2), ("qk", 3), ("uq", 0), ("uq", 1), ("ukv", 0), ("ukv", 1)]
POST_AT = {GID[p]: j for j, p in enumerate(POSTS)}
POST_PE = {}
POST_LAG = {"qk": 7, "uq": 9, "ukv": 7}
for _j, _p in enumerate(POSTS):
    _e = END[GID[_p]] + POST_LAG[_p[0]] + (3 if _p == ("uq", 1) else 1 if _p == ("ukv", 1) else 0)
    POST_PE.setdefault(_e, []).append((_j, (0, 1)))
    POST_PE.setdefault(_e + 1, []).append((_j, (2, 3)))


def posts_done(j, n):
    return j + 1 if j < 4 else 4 + NT * (j - 4) + n + 1


SMALL_END = END[GID["small", 0]]
C_TR = {SMALL_END + 9: [("cum",)], SMALL_END + 12: [("C", 0)], SMALL_END + 13: [("C", 1)],
        SMALL_END + 14: [("C", 2)]}
O_TR = {}
for _s0, _us in UNIT_SLOT.items():
    for _i in _us:
        if UNITS[_i][2] == H - 1:
            O_TR.setdefault(_s0 + 3, []).append((UNITS[_i][0], UNITS[_i][1]))


def steps_of(slot):
    us = UNIT_SLOT.get(slot, [])
    if len(us) == 2:
        return [(us[0], us[0] - 1, (0, 1)), (us[1], us[1] - 1, (2, 3))]
    if len(us) == 1:
        return [(us[0], us[0] - 1 if us[0] else None, (0, 1, 2, 3))]
    if slot == LAST_UNIT_SLOT + 1:
        return [(None, len(UNITS) - 1, (0, 1, 2, 3))]
    return [(None, None, (0, 1, 2, 3))]


def turn_order():
    order = {}
    for s in range(OUT0):
        for key in turns_of(s):
            order[key] = len(order)
    return order


def turns_of(s):
    keys = [("O", b, qt) for b, qt in O_TR.get(s, [])]
    keys += C_TR.get(s, [])
    for j, toks in POST_PE.get(s, []):
        keys += [("Q", j, t) for t in toks]
    return keys


TURN = turn_order()
SOFT = {0: 1.0 / math.sqrt(HD), 1: 1.0 / math.sqrt(HD), 2: 1.0 / math.sqrt(QH)}


def build(nc, t):
    ctx = ExitStack()
    with ctx:
        def sb(name, shape, dt=F32):
            return ctx.enter_context(nc.sbuf_tensor(name, shape, dt))

        def sem(name):
            return ctx.enter_context(nc.semaphore(name))

        bank = [ctx.enter_context(nc.psum_tensor(f"bank{i}", [P, 512], F32)) for i in range(8)]
        acc, sc_bank, turn, o_bank = bank[0:4], bank[4:6], bank[6], bank[7]

        with nc.sbuf_tensor("x_rows", [P, NT, D], F32) as x_rows:
            pass
        oT1 = sb("oT1", [P, 2, 4, SEQ], F32R)
        oT0 = sb("oT0", [P, 2, 4, SEQ], F32R)
        rows = sb("rows", [P, NT, D])
        xT = sb("xT", [P, 2, KD, SEQ], F32R)
        raw = sb("raw", [P, RAW, 512])
        wh = sb("wh", [P, HL, 512], F32R)
        wl = sb("wl", [P, HL, 512], F32R)
        q_c = sb("q_c", [P, H, SEQ])
        bias_a = q_c
        ac = sb("ac", [P, 6144])
        qT_a = ac[:, 0:2048].rearrange("p (c s) -> p c s", c=4)
        kT_a = ac[:, 2048:4096].rearrange("p (c s) -> p c s", c=4)
        v_a = ac[:, 4096:6144].rearrange("p (n c) -> p n c", n=NT)
        kT_c = ac[:, 0:4096].rearrange("p (h s) -> p h s", h=H)
        v_c = v_a
        bqkv = sb("bqkv", [P, 6144])
        qT_b = bqkv[:, 0:2048].rearrange("p (c s) -> p c s", c=4)
        kT_b = bqkv[:, 2048:4096].rearrange("p (c s) -> p c s", c=4)
        v_b = bqkv[:, 4096:6144].rearrange("p (n c) -> p n c", n=NT)
        head_odd = sb("head_odd", [P, NT, 512])
        head_rows = [rows[:, :, 512:D], head_odd]
        small = rows[:, :, 0:N_SMALL]
        squares = sb("squares", [P, 2, 512])
        gate_t = sb("gate_t", [P, NT, 512])
        prob = sb("prob", [P, 2, 512])
        probT = sb("probT", [P, 512])
        o_rows = sb("o_rows", [P, 512])
        cT_kv = sb("cT_kv", [P, 2, 1, SEQ], F32R)
        cT = [oT1[:, :, 0, :], oT1[:, :, 1, :], cT_kv[:, :, 0, :]]
        ident = sb("ident", [P, P])
        tri = gate_t[:, 0, :]
        mask = sb("mask", [P, SEQ])
        sel = sb("sel", [96, H, P], BF16)
        cum = squares[0:96, 0, :]
        cum_b = squares[0:96, 1, 0:SEQ // 2].bitcast(BF16)
        cum_p = sb("cum_p", [96, SEQ], BF16)
        lf96 = gate_t[:, 1, 0:NT * 96].rearrange("p (n c) -> p n c", n=NT)
        cosT = sb("cosT", [P, NT, HALF])
        sinT = sb("sinT", [P, NT, HALF])
        freq = sb("freq", [P, HALF])
        first = sb("first", [P, 4])
        pos_i = sb("pos_i", [P, NT], I32)
        pos_f = sb("pos_f", [P, NT])
        ssx = sb("ssx", [P, NT])
        ssh = sb("ssh", [P, NT])
        rsx = sb("rsx", [P, NT])
        pw = sb("pw", [P, 32])
        ssq2 = sb("ssq", [P, 2, NT, 8])
        rsq2 = sb("rsq", [P, 2, NT, 8])
        ssc = sb("ssc", [P, 3, NT])
        rsc = sb("rsc", [P, 3, NT])
        nmax = sb("nmax", [P, 2])
        den = sb("den", [P, 2, H])
        rden = sb("rden", [P, H])
        rope_t = sb("rope_t", [P, 4, 4 * HALF])
        kr = sb("kr", [P, NT, ROPE])
        fz = sb("fz", [P, 4, NT * H])
        gcol = sb("gcol", [P, KD])
        ghead = sb("ghead", [P, 6])
        gc = sb("gc", [P, 3])
        grope = sb("grope", [P, 2, ROPE])
        bfg = sb("bfg", [P, H])
        bro = sb("bro", [P, NG + NE])
        wr = sb("wr", [P, KD, NG + NE])
        wrh = sb("wrh", [P, KD, NG + NE], F32R)
        wrl = sb("wrl", [P, KD, NG + NE], F32R)
        relb = sb("relb", [N_BUCKETS + 1, H])
        r4 = prob[:, 0, 0:128].rearrange("p (q n c) -> p q n c", q=8, n=NT)
        r1 = prob[:, 0, 128:176].rearrange("p (q n) -> p q n", q=12)
        lgT = squares[0:NG + NE, 0, :]
        lg = prob[:, 0, 192:192 + NT * (NG + NE)].rearrange("p (n c) -> p n c", n=NT)
        grow = ac[:, 0:D]
        tri2 = ac[:, 1024:1280]
        work = ac[:, 1280:1536].rearrange("p (q n e) -> p q n e", q=4, n=NT)
        mk = ac[:, 1536:1728].rearrange("p (q n e) -> p q n e", q=3, n=NT)
        few = ac[:, 1728:1848].rearrange("p (q e) -> p q e", q=5)
        iota = ac[:, 1848:1848 + P]
        at_row = squares.rearrange("p a c -> p (a c)").rearrange("p (m q) -> p m q", q=P)
        at_chunk = gate_t[:, 0, 0:2 * NT * NCH].rearrange("p (m c) -> p m c", c=NCH)
        xg = ac[:, 2048:4096].rearrange("p (b d) -> p b d", b=2)
        ysb = ac[:, 4096:6144].rearrange("p (b d) -> p b d", b=2)
        raw_slots = [bqkv.rearrange("p (j k c) -> p j k c", j=6, k=2),
                     q_c.rearrange("p h s -> p (h s)").rearrange("p (j k c) -> p j k c", j=4, k=2),
                     head_odd.rearrange("p (j k) c -> p j k c", j=2)]
        pair_raw = [[raw_slots[0][:, j] for j in range(6)],
                    [raw_slots[1][:, j] for j in range(4)] + [raw_slots[2][:, j] for j in range(2)]]
        pair_w = xT.rearrange("p a k s -> p (a k s)").rearrange("p (r h k c) -> p r h k c", r=4, h=2, k=2)
        xgT_all = oT0.rearrange("p a k s -> p (a k s)").rearrange("p (b h k s) -> p b h k s", b=2, h=2, k=KD)
        xgT = [xgT_all[:, 0], xgT_all[:, 1]]
        hidT = cT_kv.rearrange("p a o s -> p (a o s)")[:, 0:512].rearrange("p (h k s) -> p h k s", h=2, k=2)
        th, hid = squares[:, 0, 0:FF], squares[:, 1, 0:FF]
        erow = sb("erow", [P, NE])
        tok_id = sb("tok_id", [P, 2 * NT])
        addr_i = sb("addr_i", [P, 2 * NT], I32)
        tab_i = sb("tab_i", [P, NCH], I32)
        idx_ov = sb("idx_ov", [P, 1], I32)
        ctl = sb("ctl", [1, 8], I32)
        h_bank, y_bank, hid_bank, xg_bank, count_bank = bank[0:2], bank[2:4], bank[4], bank[5:7], bank[7]
        xn_dram = nc.dram_tensor("xn_dram", [SEQ, D], F32, kind="Internal").ap()
        yslots = nc.dram_tensor("yslots", [P, NCH, D], F32, kind="Internal").ap()
        hot = head_odd[0:N_BUCKETS + 1, :, :].rearrange("p b c -> p (b c)")[:, 0:BIAS_LEN]
        biasT = squares[0:H, :, :].rearrange("p a b -> p (a b)")[:, 0:BIAS_LEN]
        bias_dram = nc.dram_tensor("bias_dram", [H, P, BIAS_LEN], F32, kind="Internal")

        OV = ["w", "x", "idx", "hi", "lo", "used", "turned", "xhi", "xT", "th", "silu", "hid", "hturned", "hhi",
              "hT", "y0", "y1", "out"]
        NAMES = ["gcol_in", "gains_in", "bias_in", "x_again", "hi_ready", "lo_ready", "piece_used", "acc_done",
                 "acc_read", "gate_read", "sum_ready", "scale_ready", "rows_ready", "wide_done", "wide_hi", "wide_lo",
                 "turn_done", "turn_hi", "turn_read", "scores_done", "shifted", "probs_ready", "pv_done",
                 "o_ready", "v_copied", "rows_copied", "sq_ready", "sq_summed", "post_done", "post_aux",
                 "branch_ready", "merged", "cum_split", "small_copied", "fz_dve", "fz_act",
                 "csq_ready", "csum_ready", "c_ready", "pool_own", "dve_own",
                 "router_done", "r_dve", "r_act", "r_mask", "r_counted", "r_addr", "r_ctl", "wr_split", "r_pair",
                 "experts_const", "xn_out", 
                 "pair_hi_ready", "pair_lo_ready", "pair_used", "h_done", "y_done", "xg_turned", "xgT_hi", "xgT_lo",
                 "th_ready", "silu_half", "hid_ready", "hid_turned", "hidT_hi", "hidT_lo", "waits_passed",
                 "x_first", "x_done", "logits_copied", "logits_turned", "r_ranked", "r_table", "probs_turned", "probT_ready"]
        RAW_SEMS = [sem(f"raw_in{i}") for i in range(RAW)]
        pair_in = [[sem(f"pair_in{b}_{j}") for j in range(6)] for b in range(2)]
        xg_in = [sem(f"xg_in{b}") for b in range(2)]
        y_out = [sem(f"y_out{b}") for b in range(2)]
        y_read = [sem(f"y_read{b}") for b in range(2)]
        back_in = [sem(f"back_in{n}") for n in range(NT)]
        ov = {n: sem(f"over_{n}") for n in OV}
        S = {n: sem(n) for n in NAMES}
        (gcol_in, gains_in, bias_in, x_again, hi_ready, lo_ready, piece_used, acc_done, acc_read, gate_read, sum_ready,
         scale_ready, rows_ready, wide_done, wide_hi, wide_lo, turn_done, turn_hi, turn_read, scores_done,
         shifted, probs_ready, pv_done, o_ready, v_copied, rows_copied, sq_ready, sq_summed, post_done,
         post_aux, branch_ready, merged, cum_split, small_copied, fz_dve, fz_act, csq_ready,
         csum_ready, c_ready, pool_own, dve_own, router_done, r_dve, r_act, r_mask, r_counted, r_addr,
         r_ctl, wr_split, r_pair, experts_const, xn_out, pair_hi_ready,
         pair_lo_ready, pair_used, h_done, y_done, xg_turned, xgT_hi, xgT_lo, th_ready, silu_half, hid_ready,
         hid_turned, hidT_hi, hidT_lo, waits_passed, x_first, x_done, logits_copied,
         logits_turned, r_ranked, r_table, probs_turned, probT_ready) = (S[n] for n in NAMES)
        arrived, released, resumed, x_moved = sem("arrived"), sem("released"), sem("resumed"), sem("x_moved")
        const_in, bias_mm, bias_sb, bias_out, rope_ready, set_ready, rope_steps = (
            sem(n) for n in ("const_in", "bias_mm", "bias_sb", "bias_out", "rope_ready", "set_ready", "rope_steps"))
        cleared = range(RAW_SEMS[0].num, probT_ready.num + 1)
        assert len(cleared) == RAW + 22 + len(OV) + len(NAMES)
        N_CONST = 9
        sel_in, slots_set, out_set = sem("sel_in"), sem("slots_set"), sem("out_set")
        first_sums, first_scale = sem("first_sums"), sem("first_scale")
        dve_c, pool_c = sem("dve_c"), sem("pool_c")
        LO_TURN = {}
        for key in sorted(TURN, key=TURN.get):
            if key[0] in ("C", "O"):
                LO_TURN[key] = len(LO_TURN)

        block = ctx.enter_context(nc.Block())

        def raw_landed(eng, i):
            eng.wait_ge(RAW_SEMS[i % RAW], 16 * (i // RAW + 1))

        def layer_end(eng, layer):
            eng.sem_inc(arrived, 1)
            eng.wait_ge(released, layer + 1)
            eng.sem_inc(resumed, 1)

        def at(ap, layer):
            v = ap[bass.ds(layer, 1)]
            names = "abcd"[:len(ap.shape) - 1]
            return v.rearrange(f"o {' '.join(names)} -> (o {names[0]}) {' '.join(names[1:])}")

        N_GAINS = 8 + 4 + 2 + 3 + 2 + 1

        def skew(dram, h):
            ap = dram[h:h + 1, 0, P - 1:P - 1 + SEQ]
            return bass.AP(tensor=ap.tensor, offset=ap.offset, ap=[[BIAS_LEN - 1, P], [1, SEQ]])

        def sums_read(eng, g, n):
            gate = GROUPS[g][0] == "gate"
            before = sum((GROUPS[q][0] == "gate") == gate for q in range(g))
            eng.wait_ge(gate_read if gate else acc_read, 4 * before + n + 1)

        def multiplied(eng, i):
            g = PIECES[i][0]
            if i == END[g]:
                return eng.wait_ge(acc_done, 4 * (g + 1))
            return eng.wait_ge(piece_used, sum(q != END[PIECES[q][0]] for q in range(i + 1)))

        def split_hi(i, width):
            raw_landed(nc.scalar, i)
            if i >= HL:
                multiplied(nc.scalar, i - HL)
            nc.scalar.activation(wh[:, i % HL, 0:width], raw[:, i % RAW, 0:width], ACT.Copy).then_inc(hi_ready, 1)

        def split_lo(i, width):
            nc.vector.wait_ge(hi_ready, i + 1)
            raw_landed(nc.vector, i)
            nc.vector.tensor_tensor(wl[:, i % HL, 0:width], raw[:, i % RAW, 0:width],
                                    wh[:, i % HL, 0:width].bitcast(F32), ALU.subtract).then_inc(lo_ready, 1)

        def width_of(i):
            return GROUPS[PIECES[i][0]][3]

        def wide_bank(w, kt):
            return bank[4 + kt % 4] if w == 1 else acc[kt % 4]

        def passes(out, lhs, rhs, start, stop):
            nc.tensor.matmul(out, lhs[0], rhs[0], start=start, stop=False)
            nc.tensor.matmul(out, lhs[0], rhs[1], start=False, stop=False)
            return nc.tensor.matmul(out, lhs[1], rhs[0], start=False, stop=stop)

        def is_const(e, value):
            return isinstance(e, int) and e == value

        def pos_wait(eng, s_, value):
            if not isinstance(value, int) or value > 0:
                eng.wait_ge(s_, value)

        def expert_steps(eng, step):
            step(0, 0, 0)
            step(1, 1, 0)
            with eng.Fori(0, (NE - 4) // 2) as i:
                step(2 * i + 2, 0, i + 1)
                step(2 * i + 3, 1, i + 1)
            step(NE - 2, 0, NE // 2 - 1)
            step(NE - 1, 1, NE // 2 - 1)

        def pair_no(e, j):
            return j if is_const(e, -1) else 4 + 6 * e + j

        def pair_role(e, j):
            return 4 + j if is_const(e, NE - 1) else j

        def pair_ring(e, j, par):
            return j if is_const(e, -1) else (2 * par + j) % 4

        def pair_place(e, j, par, half):
            role = pair_role(e, j)
            if role < 4:
                return pair_raw[1 - par][role], pair_in[1 - par][role], 32 * (half + par + 1)
            return pair_raw[par][role], pair_in[par][role], 16 * (half + 1)

        def pair_multiplied(eng, e, j):
            if j == 3:
                eng.wait_ge(h_done, e + 2)
            elif j > 3:
                eng.wait_ge(y_done, 2 * e + j - 3)
            else:
                eng.wait_ge(pair_used, 3 * (e + 1) + j + 1)

        def pair_hi(e, j, par, half):
            pair, landed, count = pair_place(e, j, par, half)
            nc.scalar.wait_ge(landed, count)
            if j >= 4:
                pair_multiplied(nc.scalar, e, j - 4)
            elif is_const(e, 0):
                pair_multiplied(nc.scalar, -1, j)
            elif not is_const(e, -1):
                pair_multiplied(nc.scalar, e - 1, j + 2)
            nc.scalar.activation(pair_w[:, pair_ring(e, j, par), 0], pair, ACT.Copy).then_inc(pair_hi_ready, 1)

        def pair_lo(e, j, par, half):
            pair, landed, count = pair_place(e, j, par, half)
            nc.vector.wait_ge(pair_hi_ready, pair_no(e, j) + 1)
            nc.vector.wait_ge(landed, count)
            nc.vector.tensor_tensor(pair_w[:, pair_ring(e, j, par), 1], pair,
                                    pair_w[:, pair_ring(e, j, par), 0].bitcast(F32),
                                    ALU.subtract).then_inc(pair_lo_ready, 1)

        def load_gate_up(sp, expert, j, par, s_):
            for half, w in ((0, "w_expert_gate"), (1, "w_expert_up")):
                src = at(t[w].rearrange("l e (k p) f -> (l e) p k f", p=P), expert)
                sp.dma_start(pair_raw[par][j][:, :, half * FF:(half + 1) * FF], src[:, 2 * j:2 * j + 2, :]).then_inc(s_, 16)

        def load_down(sp, expert, c, par, s_):
            src = at(t["w_expert_down"].rearrange("l e (k p) d -> (l e) p k d", p=P), expert)
            sp.dma_start(pair_raw[par][4 + c], src[:, :, 512 * c:512 * (c + 1)]).then_inc(s_, 16)

        def gate_up(out, x_, r_, j):
            for k in range(2):
                kt = 2 * j + k
                mm = passes(out, (x_[:, 0, kt], x_[:, 1, kt]), (pair_w[:, r_, 0, k], pair_w[:, r_, 1, k]),
                            kt == 0, kt == KD - 1)
            return mm

        def down(out, r_):
            for k in range(2):
                mm = passes(out, (hidT[:, 0, k], hidT[:, 1, k]), (pair_w[:, r_, 0, k], pair_w[:, r_, 1, k]),
                            k == 0, k == 1)
            return mm

        def turn_chunk_rows(src, inc):
            for b in range(2):
                for k in range(4):
                    mm = nc.tensor.transpose(xg_bank[b][:, k * P:(k + 1) * P],
                                             src[:, (4 * b + k) * P:(4 * b + k + 1) * P], ident[:])
                mm.then_inc(inc, 1)

        def turn_hidden(inc):
            for k in range(2):
                mm = nc.tensor.transpose(hid_bank[:, k * P:(k + 1) * P], hid[:, k * P:(k + 1) * P], ident[:])
            mm.then_inc(inc, 1)

        def chunk_T(x_, half, b):
            return x_[:, half, 4 * b:4 * b + 4].rearrange("p k s -> p (k s)")

        def hidden_T(half):
            return hidT[:, half].rearrange("p k s -> p (k s)")

        def overflow(eng, body):
            eng.wait_ge(r_ctl, 1)
            n_over = eng.value_load(ctl[0:1, 7:8], min_val=0, max_val=NCH - NE)
            with eng.If(n_over > 0):
                for par in range(2):
                    eng.wait_ge(y_out[par], 16 * NE // 2)
                with eng.Fori(0, n_over) as c:
                    body(c)
                    eng.wait_ge(ov["out"], 16 * (c + 1))
                    eng.sem_inc(waits_passed, 1)

        def overflow_sp(sp, layer):
            def body(c):
                expert = sp.value_load(ctl[0:1, bass.ds(c, 1)], min_val=0, max_val=NE - 1)
                for j in range(4):
                    load_gate_up(sp, layer * NE + expert, j, 0, ov["w"])
                for q in range(2):
                    load_down(sp, layer * NE + expert, q, 0, ov["w"])
            overflow(sp, body)

        def overflow_pe(pe):
            def body(c):
                pe.wait_ge(ov["x"], 16 * (c + 1))
                turn_chunk_rows(xg[:, 0, :], ov["turned"])
                pe.wait_ge(ov["xT"], 2 * c + 2)
                for j in range(4):
                    pe.wait_ge(ov["lo"], 6 * c + j + 1)
                    gate_up(h_bank[0][:], xgT[0], j % 3, j).then_inc(ov["used"], 1)
                pe.wait_ge(ov["hid"], c + 1)
                turn_hidden(ov["hturned"])
                pe.wait_ge(ov["hT"], c + 1)
                for q in range(2):
                    pe.wait_ge(ov["lo"], 6 * c + 5 + q)
                    down(y_bank[q][:], (4 + q) % 3).then_inc(ov["used"], 1)
            overflow(pe, body)

        def overflow_act(act):
            def body(c):
                def hi(j):
                    act.wait_ge(ov["w"], 160 * (c + 1))
                    if j >= 3:
                        act.wait_ge(ov["used"], 6 * c + j - 2)
                    nc.scalar.activation(pair_w[:, j % 3, 0], pair_raw[0][j], ACT.Copy).then_inc(ov["hi"], 1)
                for j in range(3):
                    hi(j)
                for b in range(2):
                    act.wait_ge(ov["turned"], 2 * c + b + 1)
                    nc.scalar.activation(chunk_T(xgT[0], 0, b), xg_bank[b][:], ACT.Copy).then_inc(ov["xhi"], 1)
                for j in range(3, 6):
                    hi(j)
                act.wait_ge(ov["used"], 6 * c + 4)
                nc.scalar.activation(th, h_bank[0][:, 0:FF], ACT.Tanh, scale=0.5).then_inc(ov["th"], 1)
                act.wait_ge(ov["hturned"], c + 1)
                nc.scalar.activation(hidden_T(0), hid_bank[:, 0:2 * P], ACT.Copy).then_inc(ov["hhi"], 1)
                act.wait_ge(ov["used"], 6 * c + 5)
                nc.scalar.activation(ysb[:, 0, 0:512], y_bank[0][:], ACT.Copy).then_inc(ov["y0"], 1)
                act.wait_ge(ov["y0"], c + 1)
                act.wait_ge(ov["y1"], c + 1)
                act.wait_ge(slots_set, 32)
                act.dma_start(yslots[:, bass.ds(NE + c, 1), :].rearrange("p o d -> p (o d)"), ysb[:, 0, :])\
                    .then_inc(ov["out"], 16)
            overflow(act, body)

        def overflow_dve(dve):
            def body(c):
                nc.vector.tensor_copy(idx_ov[:], tab_i[:, bass.ds(NE + c, 1)]).then_inc(ov["idx"], 1)

                def lo(j):
                    dve.wait_ge(ov["hi"], 6 * c + j + 1)
                    nc.vector.tensor_tensor(pair_w[:, j % 3, 1], pair_raw[0][j], pair_w[:, j % 3, 0].bitcast(F32),
                                            ALU.subtract).then_inc(ov["lo"], 1)
                for j in range(3):
                    lo(j)
                for b in range(2):
                    dve.wait_ge(ov["xhi"], 2 * c + b + 1)
                    nc.vector.tensor_tensor(chunk_T(xgT[0], 1, b), xg_bank[b][:], chunk_T(xgT[0], 0, b).bitcast(F32),
                                            ALU.subtract).then_inc(ov["xT"], 1)
                for j in range(3, 6):
                    lo(j)
                dve.wait_ge(ov["th"], c + 1)
                nc.vector.scalar_tensor_tensor(out=th, in0=th, scalar=1.0, in1=h_bank[0][:, 0:FF], op0=ALU.add,
                                               op1=ALU.mult).then_inc(ov["silu"], 1)
                dve.wait_ge(ov["silu"], c + 1)
                nc.vector.tensor_tensor(hid, th, h_bank[0][:, FF:], ALU.mult).then_inc(ov["hid"], 1)
                dve.wait_ge(ov["hhi"], c + 1)
                nc.vector.tensor_tensor(hidden_T(1), hid_bank[:, 0:2 * P], hidden_T(0).bitcast(F32), ALU.subtract)\
                    .then_inc(ov["hT"], 1)
                dve.wait_ge(ov["used"], 6 * c + 6)
                nc.vector.tensor_copy(ysb[:, 0, 512:], y_bank[1][:]).then_inc(ov["y1"], 1)
            overflow(dve, body)

        def overflow_pool(pool):
            def body(c):
                pool.wait_ge(ov["idx"], c + 1)
                pool.sem_inc(waits_passed, 1)
                gather(xg[:, 0, :], xn_dram, idx_ov[:, 0:1], ov["x"])
            overflow(pool, body)

        def gather(dst, dram, index, inc):
            nc.gpsimd.indirect_dma_start(out=dst, out_offset=None, in_=dram,
                                         in_offset=bass.IndirectOffsetOnAxis(ap=index, axis=0)).then_inc(inc, 16)

        def experts_sp(sp, layer):
            def passed(value):
                sp.wait_ge(pair_lo_ready, value)
                sp.sem_inc(waits_passed, 1)

            def step(e, par, half):
                if not is_const(e, 0) and not is_const(e, NE - 1):
                    for j in range(4):
                        passed(j + 1 if is_const(e, 1) else pair_no(e - 2, j) + 1)
                        load_gate_up(sp, layer * NE + (e + 1), j, 1 - par, pair_in[1 - par][j])
                if not is_const(e, 0) and not is_const(e, 1):
                    for c in range(2):
                        passed(pair_no(e - 2, 4 + c) + 1)
                        load_down(sp, layer * NE + e, c, par, pair_in[par][4 + c])

            expert_steps(sp, step)
            overflow_sp(sp, layer)

        def experts_pe(pe):
            pe.wait_ge(r_mask, 1)
            chosen = mk[:, 2].rearrange("p n e -> p (n e)")
            nc.tensor.matmul(count_bank[:, 0:NT * NE], tri2[:, 0:P], chosen, start=True, stop=True)
            nc.tensor.matmul(count_bank[:, NT * NE:2 * NT * NE], tri2[:, P:], chosen, start=True, stop=True)\
                .then_inc(r_counted, 1)
            pe.wait_ge(r_ranked, 1)
            for m in range(2 * NT):
                mm = nc.tensor.matmul(count_bank[:, 128:128 + NCH], at_row[:, m, :], at_chunk[:, m, :],
                                      start=(m == 0), stop=(m == 2 * NT - 1))
            mm.then_inc(r_table, 1)

            def turn_chunk(e, par, half):
                pe.wait_ge(xg_in[par], 16 * (half + 1))
                pos_wait(pe, xgT_lo, 2 * e)
                turn_chunk_rows(xg[:, par, :], xg_turned)

            turn_chunk(0, 0, 0)
            turn_chunk(1, 1, 0)
            for j in range(4):
                pe.wait_ge(pair_lo_ready, j + 1)
                gate_up(h_bank[0][:], xgT[0], pair_ring(-1, j, 1), j).then_inc(h_done if j == 3 else pair_used, 1)

            def step(e, par, half):
                for j in range(4):
                    if not is_const(e, NE - 1):
                        if j == 0:
                            pos_wait(pe, hid_ready, e)
                            pe.wait_ge(xgT_lo, 2 * (e + 2))
                        pe.wait_ge(pair_lo_ready, pair_no(e, j) + 1)
                        gate_up(h_bank[1 - par][:], xgT[1 - par], pair_ring(e, j, par), j)\
                            .then_inc(h_done if j == 3 else pair_used, 1)
                    if j == 1:
                        pe.wait_ge(hid_ready, e + 1)
                        pos_wait(pe, hidT_lo, e)
                        turn_hidden(hid_turned)
                if not (isinstance(e, int) and e >= NE - 2):
                    turn_chunk(e + 2, par, half + 1)
                pe.wait_ge(hidT_lo, e + 1)
                for c in range(2):
                    j = c if is_const(e, NE - 1) else 4 + c
                    pos_wait(pe, y_read[c], e)
                    pe.wait_ge(pair_lo_ready, pair_no(e, j) + 1)
                    down(y_bank[c][:], pair_ring(e, j, par)).then_inc(y_done, 1)

            expert_steps(pe, step)
            overflow_pe(pe)

        def experts_act(act):
            def rows_hi(e, par):
                for b in range(2):
                    act.wait_ge(xg_turned, 2 * e + b + 1)
                    nc.scalar.activation(chunk_T(xgT[par], 0, b), xg_bank[b][:], ACT.Copy).then_inc(xgT_hi, 1)

            def gate_tanh(e, par):
                act.wait_ge(h_done, e + 1)
                pos_wait(act, hid_ready, e)
                nc.scalar.activation(th, h_bank[par][:, 0:FF], ACT.Tanh, scale=0.5).then_inc(th_ready, 1)

            pair_hi(-1, 2, 1, -1)
            rows_hi(0, 0)
            rows_hi(1, 1)
            pair_hi(-1, 3, 1, -1)
            pair_hi(0, 0, 0, 0)
            pair_hi(0, 1, 0, 0)
            gate_tanh(0, 0)
            pair_hi(0, 2, 0, 0)

            def step(e, par, half):
                end = is_const(e, NE - 1)
                if not end:
                    pair_hi(e, 3, par, half)
                act.wait_ge(hid_turned, e + 1)
                nc.scalar.activation(hidden_T(0), hid_bank[:, 0:2 * P], ACT.Copy).then_inc(hidT_hi, 1)
                if not end:
                    pair_hi(e, 4, par, half)
                    pair_hi(e, 5, par, half)
                    gate_tanh(e + 1, 1 - par)
                    if not is_const(e, NE - 2):
                        rows_hi(e + 2, par)
                    pair_hi(e + 1, 0, 1 - par, half + par)
                act.wait_ge(y_done, 2 * e + 1)
                pos_wait(act, y_out[par], 16 * half)
                nc.scalar.activation(ysb[:, par, 0:512], y_bank[0][:], ACT.Copy).then_inc(y_read[0], 1)
                if not end:
                    pair_hi(e + 1, 1, 1 - par, half + par)
                act.wait_ge(y_done, 2 * e + 2)
                nc.scalar.activation(ysb[:, par, 512:], y_bank[1][:], ACT.Copy).then_inc(y_read[1], 1)
                if not end and not is_const(e, NE - 2):
                    pair_hi(e + 1, 2, 1 - par, half + par)
                act.wait_ge(y_read[0], e + 1)
                act.wait_ge(y_read[1], e + 1)
                dst = yslots[:, e:e + 1, :] if isinstance(e, int) else yslots[:, bass.ds(e, 1), :]
                act.dma_start(dst.rearrange("p o d -> p (o d)"), ysb[:, par, :]).then_inc(y_out[par], 16)

            expert_steps(act, step)
            overflow_act(act)

        def experts_dve(dve):
            def rows_lo(e, par):
                for b in range(2):
                    dve.wait_ge(xgT_hi, 2 * e + b + 1)
                    nc.vector.tensor_tensor(chunk_T(xgT[par], 1, b), xg_bank[b][:],
                                            chunk_T(xgT[par], 0, b).bitcast(F32), ALU.subtract).then_inc(xgT_lo, 1)

            def silu(e, par):
                dve.wait_ge(th_ready, e + 1)
                nc.vector.scalar_tensor_tensor(out=th, in0=th, scalar=1.0, in1=h_bank[par][:, 0:FF], op0=ALU.add,
                                               op1=ALU.mult).then_inc(silu_half, 1)
                dve.wait_ge(silu_half, e + 1)
                pos_wait(dve, hid_turned, e)
                nc.vector.tensor_tensor(hid, th, h_bank[par][:, FF:], ALU.mult).then_inc(hid_ready, 1)

            for j in range(3):
                pair_lo(-1, j, 1, -1)
            rows_lo(0, 0)
            rows_lo(1, 1)
            pair_lo(-1, 3, 1, -1)
            pair_lo(0, 0, 0, 0)
            pair_lo(0, 1, 0, 0)
            silu(0, 0)
            pair_lo(0, 2, 0, 0)

            def step(e, par, half):
                end = is_const(e, NE - 1)
                if not end:
                    pair_lo(e, 3, par, half)
                dve.wait_ge(hidT_hi, e + 1)
                nc.vector.tensor_tensor(hidden_T(1), hid_bank[:, 0:2 * P], hidden_T(0).bitcast(F32), ALU.subtract)\
                    .then_inc(hidT_lo, 1)
                if not end:
                    pair_lo(e, 4, par, half)
                    pair_lo(e, 5, par, half)
                    silu(e + 1, 1 - par)
                    if not is_const(e, NE - 2):
                        rows_lo(e + 2, par)
                    pair_lo(e + 1, 0, 1 - par, half + par)
                    pair_lo(e + 1, 1, 1 - par, half + par)
                if not end and not is_const(e, NE - 2):
                    pair_lo(e + 1, 2, 1 - par, half + par)

            expert_steps(dve, step)
            overflow_dve(dve)
            for n in range(NT):
                dve.wait_ge(back_in[n], 32)
                for k in range(2):
                    if k:
                        dve.wait_ge(x_first, n + 1)
                    nc.vector.scalar_tensor_tensor(out=x_rows[:, n, :], in0=back(n, k), scalar=r1[:, 9 + k, n:n + 1],
                                                   in1=x_rows[:, n, :], op0=ALU.mult, op1=ALU.add)\
                        .then_inc((x_first, x_done)[k], 1)

        def back(n, k):
            return rows[:, n, :] if k else q_c.rearrange("p h s -> p (h s)")[:, n * D:(n + 1) * D]

        def experts_pool(pool):
            pool.wait_ge(r_addr, 1)
            pool.wait_ge(xn_out, 16 * NT)
            for e in range(NE):
                if e >= 2:
                    pool.wait_ge(xg_turned, 2 * (e - 1))
                gather(xg[:, e % 2, :], xn_dram, tab_i[:, e:e + 1], xg_in[e % 2])
            overflow_pool(pool)
            for par in range(2):
                pool.wait_ge(y_out[par], 16 * NE // 2)
            pool.wait_ge(slots_set, 32)
            for n in range(NT):
                for k in range(2):
                    gather(back(n, k), yslots.rearrange("p c d -> (p c) d"),
                           addr_i[:, k * NT + n:k * NT + n + 1], back_in[n])

        def route(dve):
            count = [0]

            def step(ins):
                ins.then_inc(r_dve, 1)
                count[0] += 1
                dve.wait_ge(r_dve, count[0])

            def b4(a):
                return a.unsqueeze(2).broadcast_to([P, NT, 4])

            def be(a):
                return a.unsqueeze(1).broadcast_to([P, NT, NE])

            fst = first[:].unsqueeze(1).broadcast_to([P, NT, 4])
            tt, tr, ts = nc.vector.tensor_tensor, nc.vector.tensor_reduce, nc.vector.tensor_scalar
            stt = nc.vector.scalar_tensor_tensor
            dve.wait_ge(logits_turned, 1)
            step(tt(lg, sc_bank[1][:, 0:NT * 32].rearrange("p (n c) -> p n c", n=NT)[:, :, 0:NG + NE],
                    bro[:].unsqueeze(1).broadcast_to([P, NT, NG + NE]), ALU.add))
            gl = lg[:, :, 0:NG]
            step(tr(r1[:, 0, :], gl, AX_X, ALU.max))
            step(tt(r4[:, 0], gl, b4(r1[:, 0, :]), ALU.subtract))

            def first_best(dst, values, best, tmp, tmp1):
                step(tt(tmp, values, b4(best), ALU.is_ge))
                step(tt(tmp, tmp, fst, ALU.mult))
                step(tr(tmp1, tmp, AX_X, ALU.max))
                step(tt(dst, tmp, b4(tmp1), ALU.is_equal))

            g1, e1, e2, esel = r4[:, 2], r4[:, 3], r4[:, 4], r4[:, 5]
            first_best(g1, gl, r1[:, 0, :], r4[:, 6], r1[:, 1, :])
            el = lg[:, :, NG:].rearrange("p n (g e) -> p n g e", g=NG)
            gsel = work[:, 0].rearrange("p n (g e) -> p n g e", g=NG)
            for n in range(NT):
                ins = tt(gsel[:, n], el[:, n], g1[:, n].unsqueeze(2).broadcast_to([P, NG, EG]), ALU.mult)
            step(ins)
            for n in range(NT):
                ins = tr(esel[:, n], gsel[:, n].rearrange("p g e -> p e g"), AX_X, ALU.add)
            step(ins)
            step(tr(r1[:, 2, :], esel, AX_X, ALU.max))
            first_best(e1, esel, r1[:, 2, :], r4[:, 6], r1[:, 1, :])
            step(stt(out=r4[:, 7], in0=e1, scalar=MASKED, in1=esel, op0=ALU.mult, op1=ALU.add))
            step(tr(r1[:, 3, :], r4[:, 7], AX_X, ALU.max))
            first_best(e2, r4[:, 7], r1[:, 3, :], r4[:, 6], r1[:, 1, :])
            for k, ek in ((0, e1), (1, e2)):
                for n in range(NT):
                    ins = tt(mk[:, k, n].rearrange("p (g e) -> p g e", g=NG),
                             ek[:, n].unsqueeze(1).broadcast_to([P, NG, EG]),
                             g1[:, n].unsqueeze(2).broadcast_to([P, NG, EG]), ALU.mult)
            step(ins)
            step(tt(mk[:, 2], mk[:, 0], mk[:, 1], ALU.add))
            dve.sem_inc(r_mask, 1)
            step(tt(r1[:, 4, :], r1[:, 3, :], r1[:, 2, :], ALU.subtract))
            dve.sem_inc(r_pair, 1)
            dve.wait_ge(r_counted, 1)
            rank, over, q_, place = work[:, 1], work[:, 2], work[:, 3], work[:, 0]
            cnt, ovc, extra = few[:, 0, 8:], few[:, 1, 8:], few[:, 2, 8:]
            within, total = (count_bank[:, c:c + NT * NE].rearrange("p (n e) -> p n e", n=NT) for c in (0, NT * NE))
            step(ts(rank, within, -1.0, None, ALU.add))
            for m in range(NT - 1):
                later = rank[:, m + 1:, :]
                step(tt(later, later, total[:, m:m + 1, :].broadcast_to([P, NT - 1 - m, NE]), ALU.add))
            step(tr(cnt, total.rearrange("p n e -> p e n"), AX_X, ALU.add))
            step(nc.vector.memset(few[:, 3:5, :], 0.0))
            step(ts(ovc, cnt, float(P), None, ALU.is_gt))
            step(stt(out=ovc, in0=cnt, scalar=2.0 * P, in1=ovc, op0=ALU.is_gt, op1=ALU.add))
            step(stt(out=ovc, in0=cnt, scalar=3.0 * P, in1=ovc, op0=ALU.is_gt, op1=ALU.add))
            step(nc.vector.tensor_copy(few[:, 3, 8:], ovc))
            for b, sh in enumerate((1, 2, 4, 8)):
                s_, d_ = few[:, 3 + b % 2], few[:, 4 - b % 2]
                step(tt(d_[:, 8:], s_[:, 8:], s_[:, 8 - sh:8 + NE - sh], ALU.add))
            incl = few[:, 3, 8:]
            step(tt(extra, incl, ovc, ALU.subtract))
            step(stt(out=extra, in0=extra, scalar=float(NE - 1), in1=erow[:], op0=ALU.add, op1=ALU.subtract))
            step(ts(over, rank, float(P), None, ALU.is_ge))
            step(stt(out=q_, in0=rank, scalar=2.0 * P, in1=over, op0=ALU.is_ge, op1=ALU.add))
            step(stt(out=q_, in0=rank, scalar=3.0 * P, in1=q_, op0=ALU.is_ge, op1=ALU.add))
            step(tt(place, over, be(extra), ALU.mult))
            step(tt(place, place, be(erow[:]), ALU.add))
            step(tt(place, place, q_, ALU.add))
            step(stt(out=rank, in0=q_, scalar=-float(P), in1=rank, op0=ALU.mult, op1=ALU.add))
            both = [P, 2, NT, NE]
            for d, src in ((6, rank), (8, place)):
                step(tt(work[:, 2:4], mk[:, 0:2], src.unsqueeze(1).broadcast_to(both), ALU.mult))
                step(tr(r1[:, d:d + 2, :], work[:, 2:4], AX_X, ALU.add))
            row, chunk = (r1[:, d:d + 2, :].rearrange("p k n -> p (k n)") for d in (6, 8))
            m8 = 2 * NT
            nc.vector.tensor_tensor(at_row, iota.unsqueeze(1).broadcast_to([P, m8, P]),
                                    row.unsqueeze(2).broadcast_to([P, m8, P]), ALU.is_equal)
            step(tt(at_chunk, iota[:, 0:NCH].unsqueeze(1).broadcast_to([P, m8, NCH]),
                    chunk.unsqueeze(2).broadcast_to([P, m8, NCH]), ALU.is_equal))
            step(tt(at_chunk, at_chunk, tok_id[:].unsqueeze(2).broadcast_to([P, m8, NCH]), ALU.mult))
            dve.sem_inc(r_ranked, 1)
            step(stt(out=r1[:, 10:12, :], in0=r1[:, 6:8, :], scalar=float(NCH), in1=r1[:, 8:10, :], op0=ALU.mult,
                     op1=ALU.add))
            step(nc.vector.tensor_copy(addr_i[:], r1[:, 10:12, :].rearrange("p k n -> p (k n)")))
            dve.wait_ge(r_table, 1)
            nc.vector.tensor_copy(tab_i[:], count_bank[:, 128:128 + NCH]).then_inc(r_addr, 1)
            dve.wait_ge(r_addr, 1)
            n_ov = NCH - NE
            cmp = work[0:1, 1:3].rearrange("p a n e -> p (a n e)")[:, 0:n_ov * NE].rearrange("p (c e) -> p c e", c=n_ov)
            step(tt(cmp, incl[0:1].unsqueeze(1).broadcast_to([1, n_ov, NE]),
                    erow[0:1, 0:n_ov].unsqueeze(2).broadcast_to([1, n_ov, NE]), ALU.is_le))
            step(tr(few[0:1, 2, 0:n_ov], cmp, AX_X, ALU.add))
            step(nc.vector.tensor_copy(ctl[0:1, 0:n_ov], few[0:1, 2, 0:n_ov]))
            step(nc.vector.tensor_copy(ctl[0:1, 7:8], few[0:1, 3, 8 + NE - 1:8 + NE]))
            dve.sem_inc(r_ctl, 1)
            dve.wait_ge(r_act, 2)
            step(tr(r1[:, 6, :], r4[:, 1], AX_X, ALU.add))
            step(ts(r1[:, 7, :], r1[:, 5, :], 1.0, None, ALU.add))
            step(tt(r1[:, 8, :], r1[:, 7, :], r1[:, 6, :], ALU.mult))
            step(nc.vector.reciprocal(r1[:, 9, :], r1[:, 8, :]))
            step(ts(r1[:, 9, :], r1[:, 9, :], 0.5, None, ALU.mult))
            step(tt(r1[:, 10, :], r1[:, 9, :], r1[:, 5, :], ALU.mult))

        @block.sync
        def _(sp):
            sp.dma_start(ident[:], t["ident"]).then_inc(const_in, 16)
            sp.dma_start(hot, t["hot"]).then_inc(const_in, 16)
            sp.dma_start(mask[:], t["mask"]).then_inc(const_in, 16)
            sp.dma_start(freq[:], t["freq"]).then_inc(const_in, 16)
            sp.dma_start(first[:], t["first"]).then_inc(const_in, 16)
            sp.dma_start(erow[:], t["erow"]).then_inc(const_in, 16)
            sp.dma_start(tok_id[:], t["tok_id"]).then_inc(const_in, 16)
            with nc.allow_non_contiguous_dma(reason="512 positions, once"):
                sp.dma_start(pos_i[:], t["positions"].rearrange("b (n p) -> p (b n)", p=P)).then_inc(const_in, 16)
            sp.wait_ge(set_ready, 2)
            sp.dma_start(relb[0:N_BUCKETS, :], t["rel_bias"]).then_inc(const_in, 16)
            sp.wait_ge(bias_sb, 2)
            sp.dma_start(bias_dram[:], biasT.unsqueeze(1).broadcast_to([H, P, BIAS_LEN]))\
                .then_inc(bias_out, 16)
            with sp.Fori(0, DEPTH) as layer:
                w_in = at(t["w_in"], layer)
                sp.dma_start(tri, t["tri"]).then_inc(gains_in, 16)

                def load_piece(i):
                    if i >= RAW:
                        sp.wait_ge(lo_ready, i - RAW + 1)
                    g, k = PIECES[i]
                    name, idx, _, width = GROUPS[g]
                    dst = raw[:, i % RAW, 0:width]
                    if name in ("qk", "v", "small", "gate"):
                        col = {"qk": [0, BW, 3 * BW, 4 * BW], "v": [2 * BW, 5 * BW], "small": [COL_SMALL],
                               "gate": [COL_GATE + 512 * c for c in range(6)]}[name][idx]
                        src = w_in[k * P:(k + 1) * P, col:col + width]
                    elif name == "uq":
                        src = at(t["w_uq"], layer)[k * P:(k + 1) * P, idx * width:(idx + 1) * width]
                    elif name == "ukv":
                        src = at(t["w_ukv"], layer)[:, idx * 512:(idx + 1) * 512]
                    elif name == "branch":
                        b, c = idx // 2, idx % 2
                        src = at(t["w_branch"].rearrange("l g c d -> l (g c) d"), layer)[
                            b * BW + k * P:b * BW + (k + 1) * P, c * 512:(c + 1) * 512]
                    else:
                        src = at(t["w_out"], layer)[k * P:(k + 1) * P, idx * 512:(idx + 1) * 512]
                    sp.dma_start(dst, src).then_inc(RAW_SEMS[i % RAW], 16)

                with nc.allow_non_contiguous_dma(reason="gains as columns"):
                    sp.dma_start(gcol[:, 0:KD], at(t["norm_mix"].rearrange("l (k p) -> l p k", p=P), layer))\
                        .then_inc(gcol_in, 16)
                for i in range(RAW):
                    load_piece(i)
                with nc.allow_non_contiguous_dma(reason="gains as columns"):
                    def gain(dst, src):
                        sp.dma_start(dst, src).then_inc(gains_in, 16)

                    for c, name in enumerate(("gq_a", "gk_a", "gq_b", "gk_b")):
                        for half in range(2):
                            gain(ghead[half * HD:(half + 1) * HD, c:c + 1],
                                 at(t[name].rearrange("l (p o) -> l p o", o=1), layer))
                    for c, name in enumerate(("gq_c", "gk_c")):
                        full = t[name].rearrange("l (p o) -> l p o", o=1)
                        gain(ghead[0:NOPE, 4 + c:5 + c], at(full, layer)[0:NOPE])
                        gain(grope[:, c, :], t[name][bass.ds(layer, 1), NOPE:QH].broadcast_to([P, ROPE]))
                    gain(gc[:, 0:2], at(t["norm_cq"].rearrange("l (k p) -> l p k", p=P), layer))
                    gain(gc[:, 2:3], at(t["norm_ckv"].rearrange("l (k p) -> l p k", p=P), layer))
                    gain(bfg[:], t["b_forget"][bass.ds(layer, 1), :].broadcast_to([P, H]))
                    gain(bro[:, 0:NG], t["b_router_group"][bass.ds(layer, 1), :].broadcast_to([P, NG]))
                    gain(bro[:, NG:], t["b_router_expert"][bass.ds(layer, 1), :].broadcast_to([P, NE]))
                    gain(wr[:, :, 0:NG], at(t["w_router_group"].rearrange("l (k p) g -> l p k g", p=P), layer))
                    gain(wr[:, :, NG:], at(t["w_router_expert"].rearrange("l (k p) g -> l p k g", p=P), layer))
                sp.wait_ge(bias_out, 16)
                for h in range(H):
                    sp.dma_start(bias_a[:, h, :], skew(bias_dram, h)).then_inc(bias_in, 16)
                sp.wait_ge(x_moved, (layer + 1) * (16 * NT))
                sp.sem_inc(waits_passed, 1)
                for i in range(RAW, NP_):
                    if i == END[GID["branch", 3]] + RAW:
                        multiplied(sp, END[GID["branch", 3]])
                        sp.wait_ge(out_set, 16)
                        for n in range(NT):
                            sp.dma_start(x_rows[:, n, :],
                                         t["out"].rearrange("b (n p) d -> (b n) p d", p=P)[n]).then_inc(x_again, 16)
                    load_piece(i)
                    if i == OUT0:
                        sp.wait_ge(pv_done, len(UNITS))
                        sp.dma_start(grow, t["norm_ffn"][bass.ds(layer, 1), :].broadcast_to([P, D]))\
                            .then_inc(experts_const, 16)
                        sp.dma_start(tri2, t["tri"][:, 0:2 * P]).then_inc(experts_const, 16)
                        sp.dma_start(iota, t["iota"]).then_inc(experts_const, 16)
                for e in range(2):
                    for j in range(4):
                        load_gate_up(sp, layer * NE + e, j, e, pair_in[e][j])
                    for c in range(2):
                        load_down(sp, layer * NE + e, c, e, pair_in[e][4 + c])
                for n in range(NT):
                    sp.wait_ge(rows_ready, NT * 2 + n + 1)
                    sp.dma_start(xn_dram.rearrange("(n p) d -> n p d", p=P)[n], rows[:, n, :]).then_inc(xn_out, 16)
                experts_sp(sp, layer)
                for n in range(NT):
                    sp.wait_ge(x_done, n + 1)
                    sp.dma_start(t["out"].rearrange("b (n p) d -> (b n) p d", p=P)[n], x_rows[:, n, :])\
                        .then_inc(x_moved, 16)
                layer_end(sp, layer)
            sp.wait_ge(x_moved, 16 * NT * (DEPTH + 1))

        @block.tensor
        def _(pe):
            pe.wait_ge(const_in, 16 * N_CONST)
            pe.wait_ge(sel_in, 16)
            pe.wait_ge(set_ready, 2)
            for c in range(2):
                half = BIAS_LEN // 2
                pe.matmul(acc[c][0:H, 0:half], relb[:], hot[:, c * half:(c + 1) * half],
                          start=True, stop=True).then_inc(bias_mm, 1)

            def router(k):
                pe.wait_ge(wide_lo, 2 * KD + k + 1)
                if k == 0:
                    pe.wait_ge(wr_split, 2)
                mm = passes(sc_bank[0][0:NG + NE, :], (wrh[:, k, :], wrl[:, k, :]), (xT[:, 0, k, :], xT[:, 1, k, :]),
                            k == 0, k == KD - 1)
                if k == KD - 1:
                    mm.then_inc(router_done, 1)

            def wide_turn(w, kts=range(KD)):
                for kt in kts:
                    n = KD * w + kt
                    if kt == 0 and w == 1:
                        pe.wait_ge(merged, 12)
                        pe.wait_ge(o_ready, 3 * NT)
                        pe.wait_ge(turn_read, len(TURN))
                    elif kt == 0 or (kt == kts[0] and w == 1):
                        pe.wait_ge(rows_ready, NT * (w + 1))
                        if w == 2:
                            sums_read(pe, GID["out", 1], NT - 1)
                    if kt >= 4:
                        pe.wait_ge(wide_lo, n - 3)
                    for n_t in range(NT):
                        mm = pe.transpose(wide_bank(w, kt)[:, n_t * P:(n_t + 1) * P],
                                          rows[:, n_t, kt * P:(kt + 1) * P], ident[:])
                    mm.then_inc(wide_done, 1)
                    if w == 2 and kt >= 4:
                        router(kt - 4)

            def piece(s, toks):
                g, k = PIECES[s]
                name, idx, nk, width = GROUPS[g]
                if toks[0] == 0:
                    pe.wait_ge(lo_ready, s + 1)
                if s == OUT0 + KD // 2:
                    pe.wait_ge(wide_lo, 2 * KD)
                if k == 0 and toks[0] == 0:
                    if name == "uq":
                        pe.wait_ge(turn_read, TURN["C", 1] + 1)
                    if name == "ukv":
                        pe.wait_ge(turn_read, TURN["C", 2] + 1)
                    if name == "branch":
                        pe.wait_ge(turn_read, TURN["O", idx // 2, NT - 1] + 1)
                    if g == 0:
                        pe.wait_ge(wide_lo, KD)
                    if name == "out" and idx == 0:
                        pe.wait_ge(wide_lo, KD + KD // 2)
                for n in toks:
                    if k == 0 and g > 0:
                        sums_read(pe, g - 1, n)
                    ts = slice(n * P, (n + 1) * P)
                    if name == "uq":
                        lhs = cT[k][:, 0, ts], cT[k][:, 1, ts]
                    elif name == "ukv":
                        lhs = cT[2][:, 0, ts], cT[2][:, 1, ts]
                    elif name == "branch":
                        o = (oT0, oT1, oT0)[idx // 2]
                        lhs = o[:, 0, k, ts], o[:, 1, k, ts]
                    else:
                        lhs = xT[:, 0, k, ts], xT[:, 1, k, ts]
                    mm = passes(acc[n][:, 0:width], lhs, (wh[:, s % HL, 0:width], wl[:, s % HL, 0:width]),
                                k == 0, k == nk - 1)
                    if k == nk - 1:
                        mm.then_inc(acc_done, 1)
                if toks[-1] == NT - 1 and k < nk - 1:
                    mm.then_inc(piece_used, 1)

            def scores(i):
                b, qt, h = UNITS[i]
                w = P * (qt + 1)
                out = sc_bank[i % 2][:, 0:w]
                if i >= 2:
                    pe.wait_ge(shifted, i - 1)
                qs = slice(qt * P, (qt + 1) * P)
                if b < 2:
                    q, k = (qT_a, kT_a) if b == 0 else (qT_b, kT_b)
                    r = slice((h % 2) * HD, (h % 2 + 1) * HD)
                    if (qt, h) == (0, 0):
                        pe.wait_ge(turn_read, TURN["Q", 2 * b + 1, NT - 1] + 1)
                        if b == 1:
                            pe.wait_ge(cum_split, 1)
                    if b == 1:
                        pe.matmul(out, sel[:, h, :], cum_p[:, 0:w], start=True, stop=False)
                    pe.matmul(out, q[r, h // 2, qs], k[r, h // 2, 0:w], start=(b == 0), stop=True)\
                        .then_inc(scores_done, 1)
                else:
                    if (qt, h) == (0, 0):
                        pe.wait_ge(turn_read, TURN["Q", 7, NT - 1] + 1)
                    pe.matmul(out, q_c[0:QH, h, qs], kT_c[0:QH, h, 0:w], start=True, stop=True)\
                        .then_inc(scores_done, 1)

            def turn_probs(i):
                b, qt, h = UNITS[i]
                pe.wait_ge(probs_ready, i + 1)
                for kt in range(qt + 1):
                    mm = pe.transpose(sc_bank[i % 2][:, kt * P:(kt + 1) * P],
                                      prob[:, i % 2, kt * P:(kt + 1) * P], ident[:])
                mm.then_inc(probs_turned, 1)

            def weighted(i):
                b, qt, h = UNITS[i]
                v = (v_a, v_b, v_c)[b]
                if (qt, h) == (0, 0):
                    pe.wait_ge(v_copied, (4, 8, 16)[b])
                if h == 0 and i:
                    pe.wait_ge(o_ready, i // H)
                pe.wait_ge(probT_ready, i + 1)
                for kt in range(qt + 1):
                    mm = pe.matmul(o_bank[:, h * HD:(h + 1) * HD], probT[:, kt * P:(kt + 1) * P],
                                   v[:, kt, h * HD:(h + 1) * HD], start=(kt == 0), stop=(kt == qt))
                mm.then_inc(pv_done, 1)

            def other_turn(key):
                n = TURN[key]
                if n:
                    pe.wait_ge(turn_read, n)
                if key[0] == "cum":
                    pe.wait_ge(fz_dve, 6)
                    for n_t in range(NT):
                        mm = pe.matmul(turn[0:96, n_t * P:SEQ], lf96[:, n_t, :], tri[:, 0:SEQ - n_t * P],
                                       start=(n_t == 0), stop=(n_t == NT - 1))
                elif key[0] == "C":
                    c0 = H + key[1] * P
                    pe.wait_ge(c_ready, 1)
                    for n_t in range(NT):
                        mm = pe.transpose(turn[:, n_t * P:(n_t + 1) * P], small[:, n_t, c0:c0 + P], ident[:])
                elif key[0] == "O":
                    pe.wait_ge(o_ready, NT * key[1] + key[2] + 1)
                    for c in range(4):
                        mm = pe.transpose(turn[:, c * P:(c + 1) * P], o_rows[:, c * P:(c + 1) * P], ident[:])
                else:
                    _, j, n_t = key
                    pe.wait_ge(post_done, posts_done(j, n_t))
                    for c in range(4):
                        if j < 4:
                            mm = pe.transpose(turn[:, c * P:(c + 1) * P],
                                              head_rows[j % 2][:, n_t, c * P:(c + 1) * P], ident[:])
                        else:
                            mm = pe.transpose(turn[0:QH, c * P:(c + 1) * P],
                                              head_rows[j % 2][:, n_t, c * QH:(c + 1) * QH], ident[:])
                mm.then_inc(turn_done, 1)

            with pe.Fori(0, DEPTH) as layer:
                wide_turn(0)
                for s in range(NP_):
                    if s in MERGED_TURN:
                        wide_turn(1, MERGED_TURN[s])
                    for n_s, (new, old, toks) in enumerate(steps_of(s)):
                        if new is not None:
                            scores(new)
                        if old is not None:
                            turn_probs(old)
                        if toks[-1] != NT - 1:
                            piece(s, toks)
                        else:
                            keys = turns_of(s)
                            half = toks[:(len(toks) + 1) // 2]
                            rest = toks[len(half):]
                            for q, part in enumerate((half[:1], half[1:], rest)):
                                if q < len(keys):
                                    other_turn(keys[q])
                                if part:
                                    piece(s, part)
                            for key in keys[3:]:
                                other_turn(key)
                        if old is not None:
                            weighted(old)
                wide_turn(2)
                for k in range(4, KD):
                    router(k)
                pe.wait_ge(logits_copied, 1)
                for n in range(NT):
                    mm = pe.transpose(sc_bank[1][:, n * 32:n * 32 + NG + NE], lgT[:, n * P:(n + 1) * P],
                                      ident[0:NG + NE, 0:NG + NE])
                mm.then_inc(logits_turned, 1)
                experts_pe(pe)
                layer_end(pe, layer)

        @block.scalar
        def _(act):
            def square_rows(w, inc):
                for n in range(NT):
                    if w == 1:
                        sums_read(act, GID["out", 1], n)
                    if w == 2:
                        act.wait_ge(x_done, n + 1)
                    cols = slice(512 if w == 1 else 0, D)
                    act.activation(rows[:, n, cols], x_rows[:, n, cols], ACT.Square, accum_out=ssx[:, n:n + 1])\
                        .then_inc(inc, 1)

            def square_left():
                for n in range(NT):
                    sums_read(act, GID["out", 0], n)
                    act.wait_ge(wide_done, 2 * KD)
                    act.activation(rows[:, n, 0:512], x_rows[:, n, 0:512], ACT.Square, accum_out=ssh[:, n:n + 1])\
                        .then_inc(sum_ready, 1)

            for n in range(NT):
                act.dma_start(x_rows[:, n, :], t["x"].rearrange("b (n p) d -> (b n) p d", p=P)[n]).then_inc(x_moved, 16)
            act.wait_ge(bias_mm, 2)
            half = BIAS_LEN // 2
            for c in range(2):
                act.activation(biasT[:, c * half:(c + 1) * half], acc[c][0:H, 0:half], ACT.Copy).then_inc(bias_sb, 1)
            act.wait_ge(x_moved, 16 * NT)
            square_rows(0, first_sums)
            act.wait_ge(rope_ready, 1)
            act.activation(sinT[:], rope_t[:, 0, 0:NT * HALF].rearrange("p (n f) -> p n f", n=NT), ACT.Sin)\
                .then_inc(rope_steps, 1)
            act.activation(cosT[:], rope_t[:, 1, 0:NT * HALF].rearrange("p (n f) -> p n f", n=NT), ACT.Sin)\
                .then_inc(rope_steps, 1)

            def wide_hi_of(w, kts=range(KD)):
                for kt in kts:
                    act.wait_ge(wide_done, KD * w + kt + 1)
                    if w == 0 and kt == 0:
                        act.wait_ge(gcol_in, 16)
                    if kt == 0 and w:
                        multiplied(act, END[GID["gate", 5]] if w == 1 else NP_ - 1)
                    scale = (gcol[:, kt:kt + 1], 0.5, 1.0)[w]
                    act.activation(xT[:, 0, kt, :], wide_bank(w, kt)[:], ACT.Copy, scale=scale).then_inc(wide_hi, 1)

            def expo(i):
                b, qt, h = UNITS[i]
                w = P * (qt + 1)
                act.wait_ge(shifted, i + 1)
                if h == 0 and i >= 2 * H:
                    act.wait_ge(o_ready, i // H - 1)
                act.activation(prob[:, i % 2, 0:w], prob[:, i % 2, 0:w], ACT.Exp, scale=-1.0,
                               bias=nmax[:, i % 2:i % 2 + 1],
                               accum_out=den[:, (i // H) % 2, h:h + 1]).then_inc(probs_ready, 1)

            def probs_turn(i):
                w = P * (UNITS[i][1] + 1)
                act.wait_ge(probs_turned, i + 1)
                if i:
                    act.wait_ge(pv_done, i)
                act.activation(probT[:, 0:w], sc_bank[i % 2][:, 0:w], ACT.Copy).then_inc(probT_ready, 1)

            def turned(key):
                act.wait_ge(turn_done, TURN[key] + 1)
                if key[0] == "cum":
                    act.activation(cum[:], turn[0:96, :], ACT.Copy).then_inc(turn_read, 1)
                elif key[0] == "C":
                    act.wait_ge(rows_ready, NT)
                    act.activation(cT[key[1]][:, 0, :], turn[:], ACT.Copy, scale=gc[:, key[1]:key[1] + 1])\
                        .then_inc(turn_hi, 1)
                elif key[0] == "O":
                    _, b, qt = key
                    o = (oT0, oT1, oT0)[b]
                    if b == 2 and qt == 0:
                        multiplied(act, END[GID["branch", 1]])
                    if b == 1 and qt == 0:
                        multiplied(act, END[GID["uq", 1]])
                    act.activation(o[:, 0, :, qt * P:(qt + 1) * P],
                                   turn[:].rearrange("p (c s) -> p c s", c=4), ACT.Copy).then_inc(turn_hi, 1)
                else:
                    _, j, n_t = key
                    ts = slice(n_t * P, (n_t + 1) * P)
                    if j < 4:
                        dst = (qT_a, kT_a, qT_b, kT_b)[j][:, :, ts]
                        act.activation(dst, turn[:].rearrange("p (c s) -> p c s", c=4), ACT.Copy,
                                       scale=ghead[:, j:j + 1]).then_inc(turn_read, 1)
                    else:
                        a_done = 4 * H * 1
                        if n_t == 0:
                            act.wait_ge(pv_done, a_done)
                        full = q_c if j < 6 else kT_c
                        dst = full[0:QH, 4 * (j % 2):4 * (j % 2) + 4, ts]
                        act.activation(dst, turn[0:QH, :].rearrange("p (c s) -> p c s", c=4), ACT.Copy,
                                       scale=ghead[0:QH, 4 + (j - 4) // 2:5 + (j - 4) // 2]).then_inc(turn_read, 1)

            def squares_of(j):
                width = (512, 4 * QH, 512)[(j - 2) // 2 if j >= 4 else 0]
                for n in range(NT):
                    m = 4 * j + n
                    act.wait_ge(rows_copied, m + 1)
                    if m >= 2:
                        act.wait_ge(sq_summed, m - 1)
                    if m == 8:
                        act.wait_ge(cum_split, 1)
                    act.activation(squares[:, m % 2, 0:width], head_rows[j % 2][:, n, 0:width], ACT.Square)\
                        .then_inc(sq_ready, 1)
                if j >= 6:
                    if j == 6:
                        act.wait_ge(pv_done, 4 * H)
                    for n in range(NT):
                        act.activation(v_c[:, n, 256 * (j - 6):256 * (j - 5)].rearrange("p (h c) -> p h c", h=4),
                                       head_rows[j % 2][:, n, :].rearrange("p (h c) -> p h c", h=4)[:, :, NOPE:],
                                       ACT.Copy).then_inc(v_copied, 1)

            with act.Fori(0, DEPTH) as layer:
                wide_hi_of(0)
                for i in range(LEAD):
                    split_hi(i, width_of(i))
                for s in range(NP_):
                    if s == END[GID["qk", 0]]:
                        act.wait_ge(gains_in, 16 * N_GAINS)
                    if s in MERGED_TURN:
                        wide_hi_of(1, MERGED_TURN[s])
                    if s == END[GID["out", 0]] + 3:
                        square_left()
                    for new, old, toks in steps_of(s):
                        if old is not None:
                            probs_turn(old)
                        if new is not None:
                            expo(new)
                    if s:
                        g = PIECES[s - 1][0]
                        if END[g] == s - 1 and GROUPS[g][0] == "gate":
                            for n in range(NT):
                                act.wait_ge(acc_done, 4 * g + n + 1)
                                if GROUPS[g][1]:
                                    act.wait_ge(branch_ready, 4 * (GROUPS[g][1] - 1) + n + 1)
                                act.activation(gate_t[:, n, :], acc[n][:], ACT.Tanh, scale=0.5).then_inc(gate_read, 1)
                    for key in turns_of(s):
                        turned(key)
                    if s + LEAD < NP_:
                        split_hi(s + LEAD, width_of(s + LEAD))
                    for g, j in POST_AT.items():
                        if s == END[g] + 2:
                            squares_of(j)
                    if s == SMALL_END + 2:
                        act.wait_ge(small_copied, NT)
                        act.wait_ge(sq_summed, 8)
                        for c, (c0, c1) in enumerate(((H, H + Q_LORA), (H + Q_LORA, H + Q_LORA + KV_LORA),
                                                      (H + Q_LORA + KV_LORA, N_SMALL))):
                            for n in range(NT):
                                m = NT * c + n
                                if m >= 4:
                                    act.wait_ge(csq_ready, m - 3)
                                act.activation(squares[:, (m % 4) // 2, 256 * (m % 2):256 * (m % 2) + c1 - c0], small[:, n, c0:c1], ACT.Square,
                                               accum_out=ssc[:, c, n:n + 1]).then_inc(csq_ready, 1)
                        act.wait_ge(fz_dve, 2)
                        act.activation(fz[:, 2, :], fz[:, 1, :], ACT.Exp, scale=-1.0).then_inc(fz_act, 1)
                        act.wait_ge(fz_act, 1)
                        act.activation(fz[:, 3, :], fz[:, 2, :], ACT.Ln, bias=1.0).then_inc(fz_act, 1)
                act.activation(wrh[:], wr[:], ACT.Copy).then_inc(wr_split, 1)
                square_rows(1, sum_ready)
                wide_hi_of(2)
                act.wait_ge(router_done, 1)
                act.activation(lgT, sc_bank[0][0:NG + NE, :], ACT.Copy).then_inc(logits_copied, 1)
                act.wait_ge(r_dve, 3)
                act.activation(r4[:, 1], r4[:, 0], ACT.Exp).then_inc(r_act, 1)
                act.wait_ge(router_done, 1)
                pair_hi(-1, 0, 1, -1)
                act.wait_ge(r_pair, 1)
                act.activation(r1[:, 5, :], r1[:, 4, :], ACT.Exp).then_inc(r_act, 1)
                pair_hi(-1, 1, 1, -1)
                experts_act(act)
                square_rows(2, sum_ready)
                layer_end(act, layer)


        @block.vector
        def _(dve):
            nc.vector.memset(relb[:], 1.0).then_inc(set_ready, 1)
            nc.vector.memset(ghead[:], 1.0).then_inc(set_ready, 1)
            dve.wait_ge(const_in, 16 * N_CONST)
            nc.vector.tensor_copy(pos_f[:], pos_i[:]).then_inc(dve_c, 1)
            ang, turns, r = (rope_t[:, c, 0:NT * HALF] for c in (0, 1, 2))
            v3 = lambda a: a.rearrange("p (n f) -> p n f", n=NT)
            dve.wait_ge(dve_c, 1)
            nc.vector.tensor_tensor(v3(ang), pos_f[:].unsqueeze(2).broadcast_to([P, NT, HALF]),
                                    freq[:].unsqueeze(1).broadcast_to([P, NT, HALF]), ALU.mult).then_inc(dve_c, 1)
            dve.wait_ge(dve_c, 2)
            ROUND = 1.5 * 2.0 ** 23
            nc.vector.tensor_scalar(turns, ang, 1.0 / (2 * math.pi), ROUND, ALU.mult, ALU.add).then_inc(dve_c, 1)
            dve.wait_ge(dve_c, 3)
            nc.vector.tensor_scalar(turns, turns, ROUND, None, ALU.subtract).then_inc(dve_c, 1)
            dve.wait_ge(dve_c, 4)
            parts = (6.28125, 0.0019350051879882812, 2 * math.pi - 6.28125 - 0.0019350051879882812)
            c = 4
            src = ang
            for part in parts:
                nc.vector.scalar_tensor_tensor(out=r, in0=turns, scalar=-part, in1=src, op0=ALU.mult,
                                               op1=ALU.add).then_inc(dve_c, 1)
                c += 1
                dve.wait_ge(dve_c, c)
                src = r
            LIM = 3.1415925
            nc.vector.tensor_scalar(ang, r, LIM, -LIM, ALU.min, ALU.max).then_inc(dve_c, 1)
            dve.wait_ge(dve_c, c + 1)
            nc.vector.scalar_tensor_tensor(out=r, in0=ang, scalar=-1.0, in1=ang, op0=ALU.mult, op1=ALU.min)\
                .then_inc(dve_c, 1)
            dve.wait_ge(dve_c, c + 2)
            nc.vector.tensor_scalar(turns, r, math.pi / 2, None, ALU.add).then_inc(rope_ready, 1)

            def scaled_rows(w):
                for n in range(NT):
                    if n == 0:
                        dve.wait_ge(scale_ready if w else first_scale, 1)
                        if w:
                            dve.wait_ge(experts_const, 48)
                    if w == 0:
                        nc.vector.tensor_scalar(rows[:, n, :], x_rows[:, n, :], rsx[:, n:n + 1], None, ALU.mult)\
                            .then_inc(rows_ready, 1)
                    else:
                        nc.vector.scalar_tensor_tensor(out=rows[:, n, :], in0=x_rows[:, n, :], scalar=rsx[:, n:n + 1],
                                                       in1=grow, op0=ALU.mult, op1=ALU.mult).then_inc(rows_ready, 1)

            def wide_lo_of(w, kts=range(KD)):
                for kt in kts:
                    dve.wait_ge(wide_hi, KD * w + kt + 1)
                    hi = xT[:, 0, kt, :].bitcast(F32)
                    scale = (gcol[:, kt:kt + 1], 0.5, 1.0)[w]
                    nc.vector.scalar_tensor_tensor(out=xT[:, 1, kt, :], in0=wide_bank(w, kt)[:], scalar=scale, in1=hi,
                                                   op0=ALU.mult, op1=ALU.subtract).then_inc(wide_lo, 1)

            def shift(i):
                b, qt, h = UNITS[i]
                w = P * (qt + 1)
                dve.wait_ge(scores_done, i + 1)
                if i == 0:
                    dve.wait_ge(bias_in, 16 * H)
                if i >= 2:
                    dve.wait_ge(probs_turned, i - 1)
                add = bias_a[:, h, SEQ - w:] if b == 0 else mask[:, SEQ - w:]
                nc.vector.tensor_tensor_reduce(prob[:, i % 2, 0:w], sc_bank[i % 2][:, 0:w], add, -SOFT[b], 3.0e38,
                                               ALU.add, ALU.min, nmax[:, i % 2:i % 2 + 1]).then_inc(shifted, 1)

            def normalise(i):
                q = i // H
                dve.wait_ge(probs_ready, i + 1)
                if q:
                    b, qt, _ = UNITS[i - H]
                    dve.wait_ge(turn_done, TURN["O", b, qt] + 1)
                nc.vector.reciprocal(rden[:], den[:, q % 2, :]).then_inc(dve_own, 1)
                dve.wait_ge(pv_done, i + 1)
                dve.wait_ge(dve_own, q + 1)
                nc.vector.tensor_tensor(o_rows[:].rearrange("p (h c) -> p h c", h=H),
                                        o_bank[:].rearrange("p (h c) -> p h c", h=H),
                                        rden[:].unsqueeze(2).broadcast_to([P, H, HD]), ALU.mult).then_inc(o_ready, 1)

            def turned_lo(key):
                dve.wait_ge(turn_hi, LO_TURN[key] + 1)
                if key[0] == "C":
                    k = key[1]
                    nc.vector.scalar_tensor_tensor(out=cT[k][:, 1, :], in0=turn[:], scalar=gc[:, k:k + 1],
                                                   in1=cT[k][:, 0, :].bitcast(F32), op0=ALU.mult,
                                                   op1=ALU.subtract).then_inc(turn_read, 1)
                else:
                    _, b, qt = key
                    o = (oT0, oT1, oT0)[b]
                    qs = slice(qt * P, (qt + 1) * P)
                    nc.vector.tensor_tensor(o[:, 1, :, qs], turn[:].rearrange("p (c s) -> p c s", c=4),
                                            o[:, 0, :, qs].bitcast(F32), ALU.subtract).then_inc(turn_read, 1)

            def read_group(g, n):
                name, idx, _, width = GROUPS[g]
                dve.wait_ge(acc_done, 4 * g + n + 1)
                src = acc[n][:, 0:width]
                if g in POST_AT:
                    j = POST_AT[g]
                    if j >= 2 and n == 0:
                        dve.wait_ge(turn_done, TURN["Q", j - 2, NT - 1] + 1)
                    if j >= 2 and n == 0 and j - 2 >= 6:
                        dve.wait_ge(v_copied, 16)
                    if j == 0 and n == 0:
                        dve.wait_ge(wide_done, KD)
                    nc.vector.tensor_copy(head_rows[j % 2][:, n, 0:width], src).then_inc(acc_read, 1)
                elif name == "v":
                    v = (v_a, v_b)[idx]
                    nc.vector.tensor_copy(v[:, n, :], src).then_inc(acc_read, 1)
                elif name == "small":
                    nc.vector.tensor_copy(small[:, n, :], src).then_inc(acc_read, 1)
                elif name == "branch":
                    b, c = idx // 2, idx % 2
                    cs = slice(512 * c, 512 * (c + 1))
                    if n == 0 and b == 0 and c == 0:
                        dve.wait_ge(turn_done, TURN["C", 2] + 1)
                        dve.wait_ge(post_done, posts_done(2, 0))
                    if n == 0 and b == 0 and c == 1:
                        dve.wait_ge(turn_done, TURN["Q", 6, NT - 1] + 1)
                    if b == 0:
                        nc.vector.scalar_tensor_tensor(out=rows[:, n, cs], in0=gate_t[:, n, :], scalar=1.0, in1=src,
                                                       op0=ALU.add, op1=ALU.mult).then_inc(acc_read, 1)
                    else:
                        m = 4 * (idx - 2) + n
                        nc.vector.scalar_tensor_tensor(out=gate_t[:, n, :], in0=gate_t[:, n, :], scalar=1.0,
                                                       in1=src, op0=ALU.add, op1=ALU.mult).then_inc(acc_read, 1)
                        sums_read(dve, g, n)
                        nc.vector.tensor_tensor(rows[:, n, cs], rows[:, n, cs], gate_t[:, n, :], ALU.add)\
                            .then_inc(merged, 1)
                else:
                    cs = slice(512 * idx, 512 * (idx + 1))
                    if n == 0 and idx == 0:
                        dve.wait_ge(x_again, 16 * NT)
                    nc.vector.tensor_tensor(x_rows[:, n, cs], x_rows[:, n, cs], src, ALU.add).then_inc(acc_read, 1)

            def after_read(g, n):
                name, idx, _, _ = GROUPS[g]
                if name not in ("qk", "uq", "ukv", "v", "small", "branch"):
                    return
                if name == "branch" and idx >= 2:
                    dve.wait_ge(merged, 4 * (idx - 2) + n + 1)
                sums_read(dve, g, n)
                s_ = {"v": v_copied, "small": small_copied, "branch": branch_ready}.get(name, rows_copied)
                dve.sem_inc(s_, 1)

            def sums_of(j):
                name = POSTS[j][0]
                ssq = ssq2[:, j % 2]
                for n in range(NT):
                    m = 4 * j + n
                    dve.wait_ge(sq_ready, m + 1)
                    if n == 0 and j >= 2:
                        dve.wait_ge(post_done, posts_done(j - 2, NT - 1))
                    sq = squares[:, m % 2, :]
                    if name == "qk":
                        nc.vector.tensor_reduce(ssq[:, n, :], sq.rearrange("p (h c) -> p h c", h=H), AX_X, ALU.add)\
                            .then_inc(sq_summed, 1)
                    elif name == "uq":
                        v = sq[:, 0:4 * QH].rearrange("p (h c) -> p h c", h=4)
                        nc.vector.tensor_reduce(ssq[:, n, 0:4], v[:, :, 0:NOPE], AX_X, ALU.add)
                        nc.vector.tensor_reduce(ssq[:, n, 4:8], v[:, :, NOPE:], AX_X, ALU.add).then_inc(sq_summed, 1)
                    else:
                        v = sq.rearrange("p (h c) -> p h c", h=4)
                        nc.vector.tensor_reduce(ssq[:, n, 0:4], v[:, :, 0:NOPE], AX_X, ALU.add).then_inc(sq_summed, 1)

            with dve.Fori(0, DEPTH) as layer:
                scaled_rows(0)
                wide_lo_of(0)
                for i in range(LEAD):
                    split_lo(i, width_of(i))
                for s in range(NP_):
                    if s == OUT0:
                        for n in range(NT):
                            read_group(PIECES[s - 1][0], n)
                        dve.wait_ge(merged, 16)
                        for n in range(NT):
                            dve.sem_inc(rows_ready, 1)
                    if s in MERGED_TURN:
                        wide_lo_of(1, MERGED_TURN[s])
                    g = PIECES[s - 1][0] if s else None
                    ended = s and s != OUT0 and END[g] == s - 1 and GROUPS[g][0] != "gate"
                    steps = steps_of(s)
                    for n_s, (new, old, toks) in enumerate(steps):
                        half = toks[:len(toks) // 2] if len(toks) == 4 else toks[:1]
                        rest = toks[len(half):]
                        if ended:
                            for n in half:
                                read_group(g, n)
                        if new is not None:
                            shift(new)
                        if ended:
                            for n in rest:
                                read_group(g, n)
                            for n in toks:
                                after_read(g, n)
                        if len(steps) == 2 and old is not None and UNITS[old][2] == H - 1:
                            normalise(old)
                    for _, old, _ in (steps_of(s - 1) if s else []):
                        if len(steps_of(s - 1)) == 1 and old is not None and UNITS[old][2] == H - 1:
                            normalise(old)
                    for key in turns_of(s):
                        if key in LO_TURN:
                            turned_lo(key)
                    if s + LEAD < NP_:
                        split_lo(s + LEAD, width_of(s + LEAD))
                    for gg, j in POST_AT.items():
                        if s == END[gg] + 2:
                            sums_of(j)
                    if s == SMALL_END + 2:
                        z, a, ln = fz[:, 0, :], fz[:, 1, :], fz[:, 3, :]
                        hf = lambda q: q.rearrange("p (n h) -> p n h", n=NT)
                        nc.vector.tensor_tensor(hf(z), small[:, :, 0:H],
                                                bfg[:].unsqueeze(1).broadcast_to([P, NT, H]), ALU.add)\
                            .then_inc(fz_dve, 1)
                        dve.wait_ge(fz_dve, 1)
                        nc.vector.scalar_tensor_tensor(out=a, in0=z, scalar=-1.0, in1=z, op0=ALU.mult,
                                                       op1=ALU.max).then_inc(fz_dve, 1)
                        dve.wait_ge(fz_act, 2)
                        nc.vector.scalar_tensor_tensor(out=a, in0=z, scalar=0.0, in1=ln, op0=ALU.min,
                                                       op1=ALU.subtract).then_inc(fz_dve, 1)
                        dve.wait_ge(fz_dve, 3)
                        nc.vector.memset(lf96, 0.0).then_inc(csum_ready, 1)
                        dve.wait_ge(csum_ready, 1)
                        for c in range(3):
                            nc.vector.tensor_copy(lf96[:, :, 32 * c:32 * c + H], hf(a)).then_inc(fz_dve, 1)
                    if s == SMALL_END + 9:
                        dve.wait_ge(turn_read, TURN["cum",] + 1)
                        done = [0]

                        def chain(ins):
                            done[0] += 1
                            ins.then_inc(post_aux, 1)
                            dve.wait_ge(post_aux, done[0])

                        chain(nc.vector.tensor_copy(cum_b[:], cum[:]))
                        nc.vector.tensor_copy(cum_p[0:32, :], cum_b[0:32, :])
                        chain(nc.vector.tensor_tensor(cum[:], cum[:], cum_b[:], ALU.subtract))
                        chain(nc.vector.tensor_copy(cum_b[:], cum[:]))
                        nc.vector.tensor_copy(cum_p[32:64, :], cum_b[32:64, :])
                        chain(nc.vector.tensor_tensor(cum[:], cum[:], cum_b[:], ALU.subtract))
                        nc.vector.tensor_copy(cum_p[64:96, :], cum[64:96, :]).then_inc(cum_split, 1)
                g = len(GROUPS) - 1
                for n in range(NT):
                    read_group(g, n)
                dve.wait_ge(wr_split, 1)
                nc.vector.tensor_tensor(wrl[:], wr[:], wrh[:].bitcast(F32), ALU.subtract).then_inc(wr_split, 1)
                scaled_rows(1)
                wide_lo_of(2)
                route(dve)
                experts_dve(dve)
                layer_end(dve, layer)

        @block.gpsimd
        def _(pool):
            nc.gpsimd.memset(pw[:], -0.5).then_inc(pool_c, 1)
            pool.dma_start(sel[:].rearrange("p h q -> p (h q)"), t["sel"]).then_inc(sel_in, 16)
            pool.wait_ge(pool_c, 1)
            pool.wait_ge(first_sums, NT)
            nc.gpsimd.tensor_scalar(ssx[:], ssx[:], 1.0 / D, EPS, ALU.mult, ALU.add).then_inc(pool_c, 1)
            pool.wait_ge(pool_c, 2)
            nc.gpsimd.tensor_tensor(rsx[:], ssx[:], pw[:, 0:NT], ALU.pow).then_inc(first_scale, 1)
            pool.wait_ge(RAW_SEMS[RAW - 1], 16)
            pool.dma_start(t["out"], t["x"]).then_inc(out_set, 16)
            slots = yslots.rearrange("p c d -> p (c d)")
            x_flat = x_rows[:].rearrange("p n d -> p (n d)")
            pool.dma_start(slots[:, NE * D:(NE + NT) * D], x_flat).then_inc(slots_set, 16)
            pool.dma_start(slots[:, (NE + NT) * D:], x_flat[:, 0:(NCH - NE - NT) * D]).then_inc(slots_set, 16)
            pool.wait_ge(rope_steps, 2)
            with pool.Fori(0, DEPTH) as layer:
                own = [0]

                def step(ins):
                    ins.then_inc(pool_own, 1)
                    own[0] += 1
                    pool.wait_ge(pool_own, own[0])

                def rsqrt(dst, src, n, divisor):
                    step(nc.gpsimd.tensor_scalar(src, src, 1.0 / divisor, EPS, ALU.mult, ALU.add))
                    return nc.gpsimd.tensor_tensor(dst, src, pw[:, 0:n], ALU.pow)

                def heads_normed(j):
                    name, idx = POSTS[j]
                    pool.wait_ge(sq_summed, 4 * j + 4)
                    buf = head_rows[j % 2]
                    ssq, rsq = ssq2[:, j % 2], rsq2[:, j % 2]
                    if name == "qk":
                        step(rsqrt(rsq.rearrange("p n h -> p (n h)"), ssq.rearrange("p n h -> p (n h)"), 32, HD))
                        for n in range(NT):
                            v = buf[:, n, :].rearrange("p (h c) -> p h c", h=H)
                            ins = nc.gpsimd.tensor_tensor(v, v, rsq[:, n, :].unsqueeze(2).broadcast_to([P, H, HD]),
                                                          ALU.mult)
                        ins.then_inc(post_done, 1)
                        return
                    pw4 = pw[:, 0:16].rearrange("p (n h) -> p n h", n=NT)
                    step(nc.gpsimd.tensor_scalar(ssq[:, :, 0:4], ssq[:, :, 0:4], 1.0 / NOPE, EPS, ALU.mult, ALU.add))
                    step(nc.gpsimd.tensor_tensor(rsq[:, :, 0:4], ssq[:, :, 0:4], pw4, ALU.pow))
                    if name == "uq":
                        step(nc.gpsimd.tensor_scalar(ssq[:, :, 4:8], ssq[:, :, 4:8], 1.0 / ROPE, EPS, ALU.mult, ALU.add))
                        step(nc.gpsimd.tensor_tensor(rsq[:, :, 4:8], ssq[:, :, 4:8], pw4, ALU.pow))
                        for n in range(NT):
                            v = buf[:, n, 0:4 * QH].rearrange("p (h c) -> p h c", h=4)
                            nc.gpsimd.tensor_tensor(v[:, :, 0:NOPE], v[:, :, 0:NOPE],
                                                    rsq[:, n, 0:4].unsqueeze(2).broadcast_to([P, 4, NOPE]), ALU.mult)
                            step(nc.gpsimd.tensor_tensor(v[:, :, NOPE:], v[:, :, NOPE:],
                                                         rsq[:, n, 4:8].unsqueeze(2).broadcast_to([P, 4, ROPE]),
                                                         ALU.mult))
                            step(nc.gpsimd.tensor_tensor(v[:, :, NOPE:], v[:, :, NOPE:],
                                                         grope[:, 0, :].unsqueeze(1).broadcast_to([P, 4, ROPE]),
                                                         ALU.mult))
                            rotate(v[:, :, NOPE:NOPE + HALF], v[:, :, NOPE + HALF:], n, 4)
                            pool.sem_inc(post_done, 1)
                        return
                    if j == 6:
                        pool.wait_ge(v_copied, 12)
                    else:
                        pool.wait_ge(v_copied, 16)
                    for n in range(NT):
                        src = buf[:, n, :].rearrange("p (h c) -> p h c", h=4)
                        tmp = rope_t[:, 0:4, :].rearrange("p a b -> p (a b)")[:, 0:4 * NOPE]\
                            .rearrange("p (h c) -> p h c", h=4)
                        step(nc.gpsimd.tensor_tensor(tmp, src[:, :, 0:NOPE],
                                                     rsq[:, n, 0:4].unsqueeze(2).broadcast_to([P, 4, NOPE]), ALU.mult))
                        dst = buf[:, n, 0:4 * QH].rearrange("p (h c) -> p h c", h=4)
                        nc.gpsimd.tensor_copy(dst[:, :, 0:NOPE], tmp)
                        step(nc.gpsimd.tensor_copy(dst[:, :, NOPE:], kr[:, n, :].unsqueeze(1).broadcast_to([P, 4, ROPE])))
                        pool.sem_inc(post_done, 1)

                def rotate(x1, x2, n, heads):
                    shape = [P, heads, HALF]
                    c = cosT[:, n, :].unsqueeze(1).broadcast_to(shape)
                    s_ = sinT[:, n, :].unsqueeze(1).broadcast_to(shape)
                    m = [rope_t[:, q, 0:heads * HALF].rearrange("p (h f) -> p h f", h=heads) for q in range(4)]
                    tt = nc.gpsimd.tensor_tensor
                    tt(m[0], x1, c, ALU.mult)
                    tt(m[1], x2, s_, ALU.mult)
                    tt(m[2], x1, s_, ALU.mult)
                    step(tt(m[3], x2, c, ALU.mult))
                    tt(x1, m[0], m[1], ALU.subtract)
                    step(tt(x2, m[2], m[3], ALU.add))

                def row_scale(w):
                    pool.wait_ge(sum_ready, NT * (w + 1))
                    if w == 1:
                        step(nc.gpsimd.tensor_tensor(ssx[:], ssx[:], ssh[:], ALU.add))
                    step(nc.gpsimd.tensor_scalar(ssx[:], ssx[:], 1.0 / D, EPS, ALU.mult, ALU.add))
                    nc.gpsimd.tensor_tensor(rsx[:], ssx[:], pw[:, 0:NT], ALU.pow).then_inc(scale_ready, 1)

                heads_normed(0)
                heads_normed(1)
                pool.wait_ge(csq_ready, 3 * NT)
                pool.wait_ge(slots_set, 32)
                for c, width in enumerate((Q_LORA, KV_LORA, ROPE)):
                    step(rsqrt(rsc[:, c, :], ssc[:, c, :], NT, width))
                for n in range(NT):
                    nc.gpsimd.tensor_scalar(small[:, n, H:H + Q_LORA], small[:, n, H:H + Q_LORA],
                                            rsc[:, 0, n:n + 1], None, ALU.mult)
                    ins = nc.gpsimd.tensor_scalar(small[:, n, H + Q_LORA:H + Q_LORA + KV_LORA],
                                                  small[:, n, H + Q_LORA:H + Q_LORA + KV_LORA],
                                                  rsc[:, 1, n:n + 1], None, ALU.mult)
                ins.then_inc(c_ready, 1)
                for n in range(NT):
                    step(nc.gpsimd.tensor_scalar(kr[:, n, :], small[:, n, N_SMALL - ROPE:], rsc[:, 2, n:n + 1],
                                                 None, ALU.mult))
                    step(nc.gpsimd.tensor_tensor(kr[:, n, :], kr[:, n, :], grope[:, 1, :], ALU.mult))
                    rotate(kr[:, n, 0:HALF].unsqueeze(1), kr[:, n, HALF:].unsqueeze(1), n, 1)
                for j in range(2, 8):
                    heads_normed(j)
                row_scale(1)
                experts_pool(pool)
                row_scale(2)
                pool.wait_ge(arrived, 4 * layer + 4)
                pool.sem_inc(resumed, 1)
                pool.dma_reset(cleared)
                pool.sem_clear(cleared)
                pool.sem_inc(released, 1)



_INS = ["x", "positions", "rel_bias", "norm_mix", "w_in", "b_forget", "gq_a", "gk_a", "gq_b", "gk_b", "gq_c", "gk_c",
        "norm_cq", "norm_ckv", "w_uq", "w_ukv", "w_branch", "w_out", "norm_ffn", "w_router_group", "b_router_group",
        "w_router_expert", "b_router_expert", "w_expert_gate", "w_expert_up", "w_expert_down"]


def kernel(**inputs):
    import numpy as _np
    import concourse.bacc as _bacc
    from concourse import mybir as _mybir
    from concourse.bass_utils import run_bass_kernel_spmd as _run

    nc = _bacc.Bacc("TRN2", target_bir_lowering=False, num_devices=1)
    arrays, t = {}, {}
    given = {name: _np.ascontiguousarray(inputs[name]) for name in _INS}
    given.update(shape_constants())
    for name, a in given.items():
        arrays[f"in_{name}_dram"] = a
        t[name] = nc.dram_tensor(f"in_{name}_dram", a.shape, _mybir.dt.from_np(a.dtype), kind="ExternalInput").ap()
    t["out"] = nc.dram_tensor("out_0_dram", (1, SEQ, D), _mybir.dt.float32, kind="ExternalOutput").ap()
    build(nc, t)
    r = _run(nc, [arrays], core_ids=[0])
    return r.results[0]["out_0_dram"]
```
